# Optimizing a Trainium2 kernel written in Bass

```python
import functools
import jax, jax.numpy as jnp
from jax import lax
import numpy as np

D_MODEL = 1024
BATCH = 1
SEQ = 512
DEPTH = 1
DEC_BATCH = 8
DEC_SEQ = 1
PAST_LEN = 4096
PAGE_SIZE = 128

N_HEADS = 8
HEAD_DIM = 64
ATTN_WIDTH = N_HEADS * HEAD_DIM
CONV_WIDTH = D_MODEL - ATTN_WIDTH
CONV_GROUPS = 8
CONV_GROUP_DIM = CONV_WIDTH // CONV_GROUPS
CONV_K = 3
MIX_WIDTH = ATTN_WIDTH + CONV_WIDTH
IN_WIDTH = 3 * ATTN_WIDTH + N_HEADS + 3 * CONV_WIDTH
N_GROUPS = 4
EXPERTS_PER_GROUP = 8
N_EXPERTS = N_GROUPS * EXPERTS_PER_GROUP
TOP_K = 2
D_EXPERT = 256
Q_BLOCK = 128
EPS = 1e-6
FORGET_BIAS_INIT = 2.0

kernel_name = "hymba_fox_shortconv_hmoe_adaln_step"

def _rms_norm(x, g):
    x32 = x.astype(jnp.float32)
    y = x32 * lax.rsqrt(jnp.mean(x32 * x32, axis=-1, keepdims=True) + EPS)
    return y.astype(x.dtype) * g

def _adaln(c, w, b, n):
    mod = jax.nn.silu(c) @ w + b
    return jnp.split(mod[:, None, :], n, axis=-1)

def _mixer_inputs(h, w_in, b_forget):
    bsz, t, _ = h.shape
    proj = h @ w_in
    a, c = ATTN_WIDTH, CONV_WIDTH
    cuts = [a, 2 * a, 3 * a, 3 * a + N_HEADS, 3 * a + N_HEADS + c, 3 * a + N_HEADS + 2 * c]
    q, k, v, f, u, gate_b, gate_c = jnp.split(proj, cuts, axis=-1)
    heads = lambda z: z.reshape(bsz, t, N_HEADS, HEAD_DIM)
    logf = jax.nn.log_sigmoid((f + b_forget).astype(jnp.float32))
    return heads(q), heads(k), heads(v), logf, gate_c * u, gate_b

def _short_conv(conv_in, buf, conv_w):
    t = conv_in.shape[1]
    full = jnp.concatenate([buf.astype(conv_in.dtype), conv_in], axis=1)
    y = sum(conv_w[j] * full[:, j:j + t] for j in range(CONV_K))
    return y, full[:, t:]

def _fox_prompt(q, k, v, logf):
    bsz, t, h, hd = q.shape
    nb = t // Q_BLOCK
    cum = jnp.cumsum(logf, axis=1)
    cum_k = cum.transpose(0, 2, 1)[:, :, None, :]
    qb = q.reshape(bsz, nb, Q_BLOCK, h, hd).transpose(1, 0, 2, 3, 4)
    cqb = cum.reshape(bsz, nb, Q_BLOCK, h).transpose(1, 0, 2, 3)
    key_pos = jnp.arange(t)
    scale = HEAD_DIM ** -0.5

    def block(args):
        i, qi, ci = args
        s = jnp.einsum('bqhd,bkhd->bhqk', qi, k).astype(jnp.float32) * scale
        s = s + ci.transpose(0, 2, 1)[..., None] - cum_k
        qpos = i * Q_BLOCK + jnp.arange(Q_BLOCK)
        s = jnp.where(key_pos[None, :] <= qpos[:, None], s, -jnp.inf)
        p = jax.nn.softmax(s, axis=-1).astype(v.dtype)
        return jnp.einsum('bhqk,bkhd->bqhd', p, v)

    out = lax.map(block, (jnp.arange(nb), qb, cqb))
    return out.transpose(1, 0, 2, 3, 4).reshape(bsz, t, h, hd)

def _fox_sample(q, k_new, v_new, logf_new, cache_k, cache_v, cache_logf, page_table):
    bsz, n_pages = page_table.shape
    past = n_pages * PAGE_SIZE
    s_new = q.shape[1]
    k_past = cache_k[page_table].reshape(bsz, past, N_HEADS, HEAD_DIM)
    v_past = cache_v[page_table].reshape(bsz, past, N_HEADS, HEAD_DIM)
    f_past = cache_logf[page_table].reshape(bsz, past, N_HEADS).astype(jnp.float32)
    k_all = jnp.concatenate([k_past.astype(k_new.dtype), k_new], axis=1)
    v_all = jnp.concatenate([v_past.astype(v_new.dtype), v_new], axis=1)
    cum = jnp.cumsum(jnp.concatenate([f_past, logf_new], axis=1), axis=1)
    cq = cum[:, past:].transpose(0, 2, 1)[..., None]
    ck = cum.transpose(0, 2, 1)[:, :, None, :]
    s = jnp.einsum('bqhd,bkhd->bhqk', q, k_all).astype(jnp.float32) * (HEAD_DIM ** -0.5)
    s = s + cq - ck
    key_pos = jnp.arange(past + s_new)
    qpos = past + jnp.arange(s_new)
    s = jnp.where(key_pos[None, :] <= qpos[:, None], s, -jnp.inf)
    p = jax.nn.softmax(s, axis=-1).astype(v_all.dtype)
    return jnp.einsum('bhqk,bkhd->bqhd', p, v_all)

def _merge_heads(attn, conv_y, gate_b, g_attn, g_conv, w_out):
    bsz, t = attn.shape[:2]
    a = _rms_norm(attn, g_attn).reshape(bsz, t, ATTN_WIDTH)
    cv = (gate_b * conv_y).reshape(bsz, t, CONV_GROUPS, CONV_GROUP_DIM)
    cv = _rms_norm(cv, g_conv).reshape(bsz, t, CONV_WIDTH)
    return jnp.concatenate([a, cv], axis=-1) @ w_out

def _hier_moe(h, w_rg, b_rg, w_re, b_re, w_eg, w_eu, w_ed):
    shape = h.shape
    x = h.reshape(-1, D_MODEL)
    n = x.shape[0]
    glog = (x @ w_rg + b_rg).astype(jnp.float32)
    gprob = jax.nn.softmax(glog, axis=-1)
    g_oh = jax.nn.one_hot(jnp.argmax(glog, axis=-1), N_GROUPS, dtype=jnp.float32)
    gp = jnp.sum(gprob * g_oh, axis=-1, keepdims=True)
    elog = (x @ w_re + b_re).astype(jnp.float32).reshape(n, N_GROUPS, EXPERTS_PER_GROUP)
    elog_sel = jnp.einsum('ng,nge->ne', g_oh, elog)
    topv, topi = lax.top_k(jax.nn.softmax(elog_sel, axis=-1), TOP_K)
    topv = topv / jnp.sum(topv, axis=-1, keepdims=True) * gp
    ew = jnp.sum(jax.nn.one_hot(topi, EXPERTS_PER_GROUP, dtype=jnp.float32) * topv[..., None], axis=1)
    weights = (g_oh[:, :, None] * ew[:, None, :]).astype(x.dtype)
    wg = w_eg.reshape(N_GROUPS, EXPERTS_PER_GROUP, D_MODEL, D_EXPERT)
    wu = w_eu.reshape(N_GROUPS, EXPERTS_PER_GROUP, D_MODEL, D_EXPERT)
    wd = w_ed.reshape(N_GROUPS, EXPERTS_PER_GROUP, D_EXPERT, D_MODEL)
    y = jnp.zeros_like(x)
    for g in range(N_GROUPS):
        hg = jax.nn.silu(jnp.einsum('nd,edf->nef', x, wg[g])) * jnp.einsum('nd,edf->nef', x, wu[g])
        y = y + jnp.einsum('nef,efd->nd', hg * weights[:, g, :, None], wd[g])
    return y.reshape(shape)

def _layer(x, c, conv_buf, attend, w_ada, b_ada, g_norm1, w_in, b_forget, conv_w, g_attn_out,
           g_conv_out, w_out, g_norm2, w_rg, b_rg, w_re, b_re, w_eg, w_eu, w_ed):
    sh1, sc1, ga1, sh2, sc2, ga2 = _adaln(c, w_ada, b_ada, 6)
    h = _rms_norm(x, g_norm1) * (1.0 + sc1) + sh1
    q, k, v, logf, conv_in, gate_b = _mixer_inputs(h, w_in, b_forget)
    attn = attend(q, k, v, logf)
    conv_y, new_buf = _short_conv(conv_in, conv_buf, conv_w)
    x = x + ga1 * _merge_heads(attn, conv_y, gate_b, g_attn_out, g_conv_out, w_out)
    h = _rms_norm(x, g_norm2) * (1.0 + sc2) + sh2
    x = x + ga2 * _hier_moe(h, w_rg, b_rg, w_re, b_re, w_eg, w_eu, w_ed)
    return x, k, v, logf, new_buf

def setup_inputs(seed: int = 0) -> dict:
    key = jax.random.key(seed)
    ks = jax.random.split(key, 32)
    D = D_MODEL
    n_pages = PAST_LEN // PAGE_SIZE
    n_used = DEC_BATCH * n_pages
    n_pool = n_used + max(1, n_used // 4)
    nrm = lambda k, shape, s: s * jax.random.normal(k, shape, jnp.float32)
    page_table = jax.random.permutation(ks[8], n_pool)[:n_used].reshape(DEC_BATCH, n_pages).astype(jnp.int32)
    return {
        "x_prompt": nrm(ks[0], (BATCH, SEQ, D), 1.0),
        "x_sample": nrm(ks[1], (DEC_BATCH, DEC_SEQ, D), 1.0),
        "c_prompt": nrm(ks[2], (BATCH, D), 1.0),
        "c_sample": nrm(ks[3], (DEC_BATCH, D), 1.0),
        "cache_k": nrm(ks[4], (DEPTH, n_pool, PAGE_SIZE, N_HEADS, HEAD_DIM), 1.0),
        "cache_v": nrm(ks[5], (DEPTH, n_pool, PAGE_SIZE, N_HEADS, HEAD_DIM), 1.0),
        "cache_logf": jax.nn.log_sigmoid(FORGET_BIAS_INIT + nrm(ks[6], (DEPTH, n_pool, PAGE_SIZE, N_HEADS), 1.0)),
        "state_conv": nrm(ks[7], (DEPTH, DEC_BATCH, CONV_K - 1, CONV_WIDTH), 1.0),
        "page_table": page_table,
        "w_ada": nrm(ks[9], (DEPTH, D, 6 * D), 0.5 * D ** -0.5),
        "b_ada": nrm(ks[10], (DEPTH, 6 * D), 0.02),
        "g_norm1": 1.0 + nrm(ks[11], (DEPTH, D), 0.01),
        "w_in": nrm(ks[12], (DEPTH, D, IN_WIDTH), D ** -0.5),
        "b_forget": FORGET_BIAS_INIT + nrm(ks[13], (DEPTH, N_HEADS), 0.5),
        "conv_w": nrm(ks[14], (DEPTH, CONV_K, CONV_WIDTH), CONV_K ** -0.5),
        "g_attn_out": 1.0 + nrm(ks[15], (DEPTH, N_HEADS, HEAD_DIM), 0.01),
        "g_conv_out": 1.0 + nrm(ks[16], (DEPTH, CONV_GROUPS, CONV_GROUP_DIM), 0.01),
        "w_out": nrm(ks[17], (DEPTH, MIX_WIDTH, D), MIX_WIDTH ** -0.5),
        "g_norm2": 1.0 + nrm(ks[18], (DEPTH, D), 0.01),
        "w_router_group": nrm(ks[19], (DEPTH, D, N_GROUPS), D ** -0.5),
        "b_router_group": nrm(ks[20], (DEPTH, N_GROUPS), 0.01),
        "w_router_expert": nrm(ks[21], (DEPTH, D, N_EXPERTS), D ** -0.5),
        "b_router_expert": nrm(ks[22], (DEPTH, N_EXPERTS), 0.01),
        "w_expert_gate": nrm(ks[23], (DEPTH, N_EXPERTS, D, D_EXPERT), D ** -0.5),
        "w_expert_up": nrm(ks[24], (DEPTH, N_EXPERTS, D, D_EXPERT), D ** -0.5),
        "w_expert_down": nrm(ks[25], (DEPTH, N_EXPERTS, D_EXPERT, D), D_EXPERT ** -0.5),
        "w_ada_final": nrm(ks[26], (D, 2 * D), 0.5 * D ** -0.5),
        "b_ada_final": nrm(ks[27], (2 * D,), 0.02),
        "g_final": 1.0 + nrm(ks[28], (D,), 0.01),
    }

def reference(x_prompt, x_sample, c_prompt, c_sample, cache_k, cache_v, cache_logf, state_conv,
              page_table, w_ada, b_ada, g_norm1, w_in, b_forget, conv_w, g_attn_out, g_conv_out,
              w_out, g_norm2, w_router_group, b_router_group, w_router_expert, b_router_expert,
              w_expert_gate, w_expert_up, w_expert_down, w_ada_final, b_ada_final, g_final):
    xp, xs = x_prompt, x_sample
    kp_l, vp_l, fp_l, cp_l, ks_l, vs_l, fs_l, cs_l = [], [], [], [], [], [], [], []
    for l in range(DEPTH):
        lw = (w_ada[l], b_ada[l], g_norm1[l], w_in[l], b_forget[l], conv_w[l], g_attn_out[l],
              g_conv_out[l], w_out[l], g_norm2[l], w_router_group[l], b_router_group[l],
              w_router_expert[l], b_router_expert[l], w_expert_gate[l], w_expert_up[l],
              w_expert_down[l])
        zero_buf = jnp.zeros((xp.shape[0], CONV_K - 1, CONV_WIDTH), xp.dtype)
        xp, kp, vp, fp, cp = _layer(xp, c_prompt, zero_buf, _fox_prompt, *lw)
        attend_s = functools.partial(_fox_sample, cache_k=cache_k[l], cache_v=cache_v[l],
                                     cache_logf=cache_logf[l], page_table=page_table)
        xs, ksn, vsn, fsn, csn = _layer(xs, c_sample, state_conv[l], attend_s, *lw)
        kp_l.append(kp); vp_l.append(vp); fp_l.append(fp); cp_l.append(cp)
        ks_l.append(ksn); vs_l.append(vsn); fs_l.append(fsn); cs_l.append(csn)
    shp, scp = _adaln(c_prompt, w_ada_final, b_ada_final, 2)
    shs, scs = _adaln(c_sample, w_ada_final, b_ada_final, 2)
    y_prompt = _rms_norm(xp, g_final) * (1.0 + scp) + shp
    y_sample = _rms_norm(xs, g_final) * (1.0 + scs) + shs
    k_prompt = jnp.stack(kp_l); v_prompt = jnp.stack(vp_l)
    logf_prompt = jnp.stack(fp_l); conv_prompt = jnp.stack(cp_l)
    k_sample = jnp.stack(ks_l); v_sample = jnp.stack(vs_l)
    logf_sample = jnp.stack(fs_l); conv_sample = jnp.stack(cs_l)
    return (y_prompt, y_sample, k_prompt, v_prompt, logf_prompt, conv_prompt,
            k_sample, v_sample, logf_sample, conv_sample)


_drawn_inputs = setup_inputs


def setup_inputs(seed=0):
    import zlib

    import numpy as np

    out = dict(_drawn_inputs(seed))
    spreads = {}
    factors = {'g_norm1': 4.534,
     'g_attn_out': 8.0,
     'g_conv_out': 8.0,
     'g_norm2': 6.707,
     'b_router_group': 8.0,
     'b_router_expert': 7.263,
     'g_final': 31.578,
     'b_ada_final': 2.942}
    for name, (base, spread) in spreads.items():
        noise = np.random.default_rng([zlib.crc32(name.encode()), seed]).standard_normal(out[name].shape)
        drawn = base * np.exp(spread * noise) if base else spread * noise
        out[name] = __import__('jax').numpy.asarray(drawn.astype(out[name].dtype))
    for name, factor in factors.items():
        out[name] = (out[name] * factor).astype(out[name].dtype)
    return out
```

```python
from contextlib import ExitStack

import concourse.bass as bass
from concourse import mybir

F32 = mybir.dt.float32
I32 = mybir.dt.int32
ALU = mybir.AluOpType
ACT = mybir.ActivationFunctionType
AX = mybir.AxisListType
RED = bass.bass_isa.ReduceOp

P = 128
D = 1024
KD = D // P
T = 512
NT = T // P
B = 8
H, HD = 8, 64
HW = H * HD
C4 = HW // P
NPG, PG = 32, 128
PPP = PG * NPG // P
CH = 4
NCH = PPP // CH
NKV = B * NCH
RING = 4
SCALE = HD ** -0.5
EPS = 1e-6
NEG = -1.0e30
NG, EPG = 4, 8
NE = NG * EPG
DE = 256
SLOTS = 64
PASSES = -(-(T + B) // SLOTS)
FAR = 4096.0
HP = T + B + 24
SECS = 512


def build(nc, x_prompt, x_sample, c_prompt, c_sample, cache_k, cache_v, cache_logf, state_conv,
          page_table, w_ada, b_ada, g_norm1, w_in, b_forget, conv_w, g_attn_out, g_conv_out,
          w_out, g_norm2, w_router_group, b_router_group, w_router_expert, b_router_expert,
          w_expert_gate, w_expert_up, w_expert_down, w_ada_final, b_ada_final, g_final,
          y_prompt, y_sample, k_prompt, v_prompt, logf_prompt, conv_prompt, k_sample, v_sample,
          logf_sample, conv_sample, cap=SLOTS):
    ctx = ExitStack()
    with ctx:
        def sb(name, shape, dt=F32):
            return ctx.enter_context(nc.sbuf_tensor(name, shape, dt))

        def sem(name):
            return ctx.enter_context(nc.semaphore(name))

        q_rows_dram = nc.dram_tensor("q_rows_scratch", [B, HW], F32, kind="Internal").ap()
        h2_dram = nc.dram_tensor("h2_scratch", [2 * (T + B), D // 2], F32, kind="Internal").ap()
        y_dram = nc.dram_tensor("expert_rows_scratch", [4 * (T + B), D // 2], F32, kind="Internal").ap()

        n_pool = cache_k.shape[1]
        k_rows = cache_k.rearrange("l n (g r) h d -> (l n g) (r h d)", r=CH)
        v_rows = cache_v.rearrange("l n (g r) h d -> (l n g) (r h d)", r=CH)
        f_rows = cache_logf.rearrange("l n (g r) h -> (l n g) (r h)", r=PPP)
        w_ada_v = w_ada.rearrange("l (k p) n -> (l p) k n", p=P)
        w_fin_v = w_ada_final.rearrange("(k p) n -> p k n", p=P)
        w_in_v = w_in.rearrange("l (k p) n -> (l p) k n", p=P)
        w_out_v = w_out.rearrange("l (k p) n -> (l p) k n", p=P)
        f_col = 3 * HW
        sec_col = [0, HW, 2 * HW, f_col + H, f_col + H + 2 * HW, f_col + H + HW]

        R_x = sb("R_x", [P, 5120])
        R_part = sb("R_part", [P, 6144])
        R_h = sb("R_h", [P, KD * HP])
        R_cm = sb("R_cm", [P, 8264])
        R_kv = sb("R_kv", [P, RING * CH * HW])
        R_w = sb("R_w", [P, 6144])
        R_q = sb("R_q", [P, 8192])
        R_t = sb("R_t", [P, 3584])

        def view(region, lo, dims, parts=P):
            n = 1
            for d in dims:
                n *= d
            v = region[0:parts, lo:lo + n]
            if len(dims) == 1:
                return v
            names = "abcd"[:len(dims)]
            return v.rearrange(f"p ({' '.join(names)}) -> p {' '.join(names)}",
                               **{c: d for c, d in zip(names[1:], dims[1:])})

        ident = sb("ident", [P, P])
        block64 = sb("block64", [P, P])
        later = sb("later", [P, P])
        earlier = sb("earlier", [P, P])
        ones = sb("ones", [P, P])
        causal = sb("causal", [P, P])
        sel = sb("sel", [P, B + 1, P])
        head_mask = sb("head_mask", [P, HW])
        vecs = sb("vecs", [P, 20])
        kv_index = sb("kv_index", [P, NKV], I32)
        f_index = sb("f_index", [P, B], I32)
        v_new = sb("v_new", [B, HW])
        eps = sb("eps", [P, 1])
        ssq = sb("ssq", [P, 5])
        rstd = sb("rstd", [P, 5])
        b_f = sb("b_f", [H, 1])
        neg_max = sb("neg_max", [P, 2])
        row_sum = sb("row_sum", [P, 2 * H])
        head_ssq = sb("head_ssq", [P, H])
        quarter = sb("quarter", [P, 10])
        max_count = sb("max_count", [1, 1], I32)
        small_one = sb("small_one", [P, 1])
        e_cols = sb("e_cols", [P, 2], I32)

        sh1_p, sc1_p, sh1_s, sc1_s, g1_b = (view(R_q, i * 1024, [1024]) for i in range(5))
        part_a = view(R_q, 5120, [4, 512])
        x_a = view(R_x, 0, [5, D])
        c_row = view(R_part, 0, [D], B + 1)
        c_t = view(R_q, 7680, [KD, 32])
        b_row_a = view(R_part, 1280, [2048], 1)
        vec_rows = view(R_part, 3328, [P], 20)
        pt_int = view(R_part, 3456, [NPG], B).bitcast(I32)
        pt_exp = view(R_part, 3488, [NPG, 4], B)
        lane = view(R_part, 3616, [1]).bitcast(I32)
        h_row = [view(R_t, i * 1024, [D]) for i in range(2)]
        junk = view(R_t, 2048, [D])
        h_t = view(R_h, 0, [KD, HP])
        q_t, k_t, v_r = (view(R_q, i * 2048, [C4, T]) for i in range(3))
        s_part = view(R_q, 6144, [3, HW])
        qk_new = view(R_part, 4096, [2, HW], B)
        u_part = view(R_part, 5120, [HW])
        qk_prod = view(R_part, 5632, [HW], B)
        conv_in = view(R_cm, 0, [C4, T + B + 2])
        mix_c = view(R_cm, 2088, [C4, T + B])
        scores = view(R_cm, 4168, [B, PPP, H])
        decay = view(R_cm, 6216, [B, PPP, H])
        prod = view(R_x, 0, [CH * H, HD])
        q_b = view(R_x, 2048, [2, HW])
        f_t = view(R_x, 3072, [T + B], H)
        f_a = view(R_x, 3592, [T + B], H)
        cum = view(R_x, 4112, [T], H)
        neg_cum = f_a
        w_f = view(R_x, 4624, [KD, H])
        k_row = [view(R_t, i * 512, [HW]) for i in range(2)]
        c_rows = view(R_t, 1024, [HW], 2 + B)
        sq_c = view(R_t, 1536, [T + B])
        rt_c = view(R_t, 2056, [T + B])
        probs = [view(R_t, i * 512, [T]) for i in range(2)]
        probs_t = [view(R_t, 1024 + i * 512, [NT, P]) for i in range(2)]
        o_row = view(R_t, 2048, [H, HD])
        o_sq = view(R_t, 2560, [H, HD])
        news = view(R_t, 3072, [B, H])
        top = view(R_t, 3136, [B, H])
        top_all = view(R_t, 3200, [B, H])
        p_new = view(R_t, 3264, [B, H])
        p_sum = view(R_t, 3328, [B, H])
        lf_rows = view(R_t, 3392, [5, H])
        lf_diag = view(R_t, 3432, [B, H], B)
        tail = view(R_t, 3496, [B, H])
        state_t = view(R_part, 3620, [C4, B, 2])
        state_rows = view(R_part, 1280, [HW], 2 * B)
        y_tmp = view(R_part, 3684, [C4, B])
        kv = view(R_kv, 0, [RING, CH * H, HD])
        v_ring = view(R_kv, 0, [RING, CH, HW])
        kv_flat = view(R_kv, 0, [RING, CH * HW])
        w_unit = view(R_w, 0, [3, 4, SECS])
        part = view(R_part, 0, [12, SECS])
        mix_a = view(R_h, 0, [C4, T + B])
        o_m = [view(R_h, 2080 + i * 512, [HW]) for i in range(2)]
        o_t = view(R_h, 3104, [C4, B])
        o_q = view(R_h, 3136, [C4, B])
        o_r = view(R_h, 3168, [C4, B])
        b_row = view(R_h, 3200, [1024], 1)
        x_r = view(R_x, 0, [5, D])
        wo = view(R_q, 0, [KD, D])
        ga1_p, sh2_p, sc2_p, ga1_s, sh2_s, sc2_s = (view(R_w, i * 1024, [D]) for i in range(6))
        g_b = view(R_t, 2048, [D])
        prod_o = view(R_cm, 0, [D])
        junk2 = view(R_part, 0, [D])
        h2_t = view(R_cm, 1024, [KD, P])
        w_r = view(R_h, 3200, [KD, NG + NE])
        b_r = view(R_h, 3488, [NG + NE])
        lg = view(R_h, 3524, [5, NG + NE])
        slot_is = view(R_t, 0, [2, 5, P])
        vals = view(R_t, 1280, [2, 5, 3 * NE])
        oh = view(R_t, 2240, [2, 5, NE])
        both = view(R_t, 2560, [5, NE])
        rank_e = view(R_t, 2720, [5, NE])
        els = view(R_t, 2880, [5, NG, EPG])
        el = view(R_t, 3040, [5, EPG])
        e_c = view(R_t, 3080, [2, 5, EPG])
        e_t = view(R_t, 3160, [5, EPG])
        ge = view(R_t, 3200, [5, NG])
        g_oh = view(R_t, 3220, [5, NG])
        st = view(R_t, 3240, [12, 5])
        rank = view(R_t, 3300, [2, 5])
        slot_no = view(R_t, 3310, [P])
        tok2 = view(R_t, 3438, [5])
        desc = view(R_t, 3443, [EPG])
        half_no = view(R_t, 3451, [1])
        far_half = view(R_t, 3452, [1])
        tmp5 = view(R_t, 3453, [5])
        cnt = view(R_t, 3458, [NE])
        cnt_max = view(R_t, 3490, [1])
        tabs = view(R_part, 2048, [NE])
        g_idx = view(R_part, 2080, [NE]).bitcast(I32)
        mark = view(R_part, 2144, [1])
        s_idx = view(R_part, 2112, [NE]).bitcast(I32)
        exp_w = [view(r, 0, [6144]) for r in (R_w, R_kv, R_q, R_cm)]
        x_e = [view(R_h, i * 512, [512]) for i in range(2)]
        xe_t = [view(R_h, 1024 + i * 512, [4, 2, SLOTS]) for i in range(2)]
        sig = [view(R_h, 2048 + i * 256, [DE], SLOTS) for i in range(2)]
        hid = [view(R_h, 2560 + i * 256, [DE], SLOTS) for i in range(2)]
        hid_t = [view(R_h, 3072 + i * 128, [2, SLOTS]) for i in range(2)]
        y_e = [view(R_h, 3328 + i * 512, [512]) for i in range(2)]
        y_g = [view(R_w, i * 2048, [2, D]) for i in range(3)] + [view(R_kv, i * 2048, [2, D]) for i in range(2)]
        ga2_p, ga2_s = (view(R_kv, 6144 + i * 1024, [D]) for i in range(2))
        shf_p, shf_s = (view(R_q, 6144 + i * 1024, [D]) for i in range(2))
        scf_p, scf_s = (view(R_cm, 6216 + i * 1024, [D]) for i in range(2))
        gf_b = view(R_part, 1024, [D])

        bank = [ctx.enter_context(nc.psum_tensor(f"bank{i}", [P, 512], F32)) for i in range(8)]

        names = """ov_held unit_used ada_done consts_ready setup_ready setup_psum c_silu vec_loaded ba_loaded
            part_ready sh_ready expand_done h_row_ready ht_ready h_psum samp_evac samp_done row_evac
            row_done samp_u samp_g samp_t acc_act acc_dve acc_done krow_evac krow_done wf_loaded
            f_done lf_ready lf_done st_loaded st_done lf_evac crow_done crow_evac st_evac sq_ready
            cn_done cn_sqrt decay_sum select_done tail_done p_ready s_done pt_ready pt_done o_taken
            pv_done o_ready mix_ready ot_done tail_evac mod2_act wo_loaded mix_ready_c wo_taken
            samp_norm_dve wo_done h2_ready h2t_ready h2_psum mod2_dve wr_loaded lg_done exp_ready
            zeroed pnew_ready om_ready v_used pvs_done ot2_done softmax_in samp_norm_psum
            samp_norm_act route_in rank_done vals_ready tabs_done xe_done xet_ready gu_done hid_ready
            hidt_done hidt_ready y_ready y_done tabs_ready mod3_ready act_step c_loaded x_loaded
            rstd_sq q_stored outs f_taken ln_ready max_ready o_sq_ready o_ssq o_sqrt x1_ready
            norm_sqrt route_exp sig_ready dve_step pt_loaded g_loaded k_used select_in top_ready
            lg_taken route_consts count_ready ov_slots fin_ready pool_step f_loaded ov_cols y_all
            state_out""".split()
        S = {n: sem(n) for n in names}
        unit_loaded = [sem(f"unit_loaded{i}") for i in range(3)]
        b_loaded = [sem(f"bias_loaded{i}") for i in range(2)]
        kv_loaded = [sem(f"kv_loaded{i}") for i in range(RING)]
        qb_loaded = [sem(f"qb_loaded{i}") for i in range(2)]
        krow_out = [sem(f"krow_out{i}") for i in range(2)]
        h2_out = [sem(f"h2_out{i}") for i in range(2)]
        gate_loaded = [sem(f"gate_loaded{i}") for i in range(4)]
        down_loaded = [sem(f"down_loaded{i}") for i in range(4)]
        xe_loaded = [sem(f"xe_loaded{i}") for i in range(2)]
        y_stored = [sem(f"y_stored{i}") for i in range(2)]
        yg_loaded = [sem(f"yg_loaded{i}") for i in range(5)]
        y_out = [sem(f"y_out{i}") for i in range(2)]

        block = ctx.enter_context(nc.Block())
        sel8 = sel[:, 0:B, 0]
        chunk_sec = [(w_ada_v, n * SECS) for n in range(12)] + [(w_fin_v, n * SECS) for n in range(4)]
        STORED = 16 * (NE // 2)
        NEW_AT, DIAG_AT = 16, 25

        def after_sections(w):
            return {1: 0, 4: 1, 6: 2}.get(w % 8, -1) + 3 * (w // 8) if w % 8 in (1, 4, 6) else None

        @block.tensor
        def _(pe):
            def use_unit(u):
                pe.wait_ge(unit_loaded[u % 3], 16 * (u // 3 + 1))
                return w_unit[:, u % 3]

            def ada_chunk(n, psum, brow):
                for half in range(2):
                    u = (2 * n if n < 4 else 12 + 2 * n) + half
                    w = use_unit(u)
                    for j in range(4):
                        last = nc.tensor.matmul(psum[32 * j:32 * j + 32, :], c_t[:, 4 * half + j, :], w[:, j, :],
                                                start=(half == 0), stop=(half == 1 and j > 0))
                    last.then_inc(S["unit_used"], 1)
                nc.tensor.matmul(psum[0:32, :], ones[0:1, 0:32], brow, start=False, stop=True)\
                    .then_inc(S["ada_done"], 1)

            pe.wait_ge(S["consts_ready"], 4)
            pe.wait_ge(S["setup_ready"], 1)
            nc.tensor.matmul(bank[6][:, 32:32 + B], pt_exp[:, :, :].rearrange("p a b -> p (a b)"), ident[0:B, 0:B], start=True, stop=True)\
                .then_inc(S["setup_psum"], 1)
            pe.wait_ge(S["c_silu"], 1)
            for k in range(KD):
                last = nc.tensor.transpose(bank[7][:, 9 * k:9 * k + 9], c_row[:, k * P:(k + 1) * P],
                                           ident[0:B + 1, 0:B + 1])
            last.then_inc(S["setup_psum"], 1)
            pe.wait_ge(S["vec_loaded"], 64)
            pe.wait_ge(S["setup_ready"], 3)
            nc.tensor.transpose(bank[6][:, 0:20], vec_rows[:, :], ident[0:20, 0:20]).then_inc(S["setup_psum"], 1)
            pe.wait_ge(S["setup_ready"], 4)
            pe.wait_ge(S["ba_loaded"], 16)

            def expand_first(n):
                pe.wait_ge(S["part_ready"], n + 1)
                if n >= 2:
                    pe.wait_ge(S["sh_ready"], n - 1)
                nc.tensor.matmul(bank[2 + n % 2][0:B, :], sel8, part_a[:, n, :], start=True, stop=True)
                nc.tensor.matmul(bank[4 + n % 2][:, :], sel[:, B, :], part_a[:, n, :], start=True, stop=True)\
                    .then_inc(S["expand_done"], 1)

            for n in range(4):
                if n >= 2:
                    pe.wait_ge(S["part_ready"], n - 1)
                ada_chunk(n, bank[n % 2], b_row_a[:, n * SECS:(n + 1) * SECS])
                if n:
                    expand_first(n - 1)
            expand_first(3)

            def transpose_h(i):
                pe.wait_ge(S["h_row_ready"], i + 1)
                if i == 0:
                    for k in range(KD):
                        last = nc.tensor.transpose(bank[6][:, 64 + 8 * k:72 + 8 * k],
                                                   h_row[0][0:B, k * P:(k + 1) * P], ident[0:B, 0:B])
                else:
                    if i >= 3:
                        pe.wait_ge(S["ht_ready"], i - 1)
                    for k in range(KD):
                        last = nc.tensor.transpose(bank[(2 if i % 2 else 4) + k // 4][:, (k % 4) * P:(k % 4 + 1) * P],
                                                   h_row[i % 2][:, k * P:(k + 1) * P], ident[:])
                last.then_inc(S["h_psum"], 1)

            def sample_section(s):
                pe.wait_ge(S["ht_ready"], 1)
                pe.wait_ge(S["consts_ready"], 2)
                if s:
                    pe.wait_ge(S["samp_evac"], s)
                for half in range(2):
                    w = use_unit(8 + 2 * s + half)
                    for j in range(4):
                        last = nc.tensor.matmul(bank[7][32 * j:32 * j + 32, :],
                                                h_t[:, 4 * half + j, T:T + 32], w[:, j, :],
                                                start=(half == 0), stop=(half == 1))
                last.then_inc(S["samp_done"], 1)

            def sample_rows(s):
                pe.wait_ge(S["samp_evac"], s + 1)
                if s:
                    pe.wait_ge(S["row_evac"], s)
                nc.tensor.matmul(bank[6][0:B, :], sel8, s_part[:, s, :], start=True, stop=True)\
                    .then_inc(S["row_done"], 1)

            def sample_columns(s):
                pe.wait_ge(S["samp_evac"], s + 1)
                pe.wait_ge(*{3: (S["row_evac"], 3), 4: (S["samp_u"], 1), 5: (S["samp_g"], 1)}[s])
                for c in range(C4):
                    last = nc.tensor.matmul(bank[6][:, c * B:(c + 1) * B], u_part[:, c * P:(c + 1) * P], sel8,
                                            start=True, stop=True)
                last.then_inc(S["samp_t"], 1)

            def prompt_section(s):
                for half in range(2):
                    w = use_unit(8 + 2 * s + half)
                    for m in range(4):
                        if half == 0:
                            if 1 <= s <= 4:
                                pe.wait_ge(S["acc_act"], 4 * (s - 1) + m + 1)
                            if s == 5:
                                pe.wait_ge(S["acc_dve"], m + 1)
                        for j in range(4):
                            k = 4 * half + j
                            if s == 2:
                                l, r = h_t[:, k, m * P:(m + 1) * P], w[:, j, :]
                            else:
                                l, r = w[:, j, m * P:(m + 1) * P], h_t[:, k, 0:T]
                            last = nc.tensor.matmul(bank[m][:, :], l, r, start=(k == 0), stop=(k == KD - 1))
                        if half:
                            last.then_inc(S["acc_done"], 1)
                    if half == 0:
                        last.then_inc(S["unit_used"], 1)

            transpose_h(0)
            sample_section(0)
            transpose_h(1)
            sample_rows(0)
            for i in range(2, 5):
                transpose_h(i)
            pe.wait_ge(S["ht_ready"], 5)
            prompt_section(0)
            for s in (1, 2):
                sample_section(s)
                prompt_section(s)
                sample_rows(s)
            pe.wait_ge(S["acc_act"], 8)
            for t in range(NT):
                if t >= 2:
                    pe.wait_ge(S["krow_evac"], t - 1)
                for c in range(C4):
                    last = nc.tensor.transpose(bank[4 + t % 2][:, c * P:(c + 1) * P],
                                               k_t[:, c, t * P:(t + 1) * P], ident[:])
                last.then_inc(S["krow_done"], 1)
            pe.wait_ge(S["krow_evac"], 4)
            pe.wait_ge(S["wf_loaded"], 16)
            for k in range(KD):
                nc.tensor.matmul(bank[4][0:H, :], w_f[:, k, :], h_t[:, k, 0:T], start=(k == 0), stop=(k == KD - 1))
            for k in range(KD):
                last = nc.tensor.matmul(bank[5][0:H, 0:B], w_f[:, k, :], h_t[:, k, T:T + B],
                                        start=(k == 0), stop=(k == KD - 1))
            last.then_inc(S["f_done"], 1)
            sample_section(3)
            prompt_section(3)
            sample_columns(3)
            pe.wait_ge(S["lf_ready"], 1)
            for t in range(NT):
                nc.tensor.transpose(bank[4][:, t * H:(t + 1) * H], f_t[:, t * P:(t + 1) * P], ident[0:H, 0:H])
            nc.tensor.transpose(bank[4][0:B, 32:32 + H], f_t[:, T:T + B], ident[0:H, 0:H]).then_inc(S["lf_done"], 1)
            pe.wait_ge(S["st_loaded"], 16)
            for c in range(C4):
                last = nc.tensor.transpose(bank[5][:, c * 16:(c + 1) * 16], state_rows[:, c * P:(c + 1) * P],
                                           ident[0:16, 0:16])
            last.then_inc(S["st_done"], 1)
            sample_section(4)
            prompt_section(4)
            sample_columns(4)
            sample_section(5)
            prompt_section(5)
            sample_columns(5)
            pe.wait_ge(S["acc_dve"], 4)
            pe.wait_ge(S["samp_g"], 1)
            pe.wait_ge(S["lf_evac"], 2)
            for c in range(C4):
                last = nc.tensor.transpose(bank[4][0:2 + B, c * P:(c + 1) * P], conv_in[:, c, T:T + 2 + B], ident[:])
            last.then_inc(S["crow_done"], 1)
            pe.wait_ge(S["crow_evac"], 1)
            pe.wait_ge(S["st_evac"], 1)
            for c in range(C4):
                pe.wait_ge(S["sq_ready"], c + 1)
                nc.tensor.matmul(bank[4][:, :], block64[:], sq_c[:, 0:T], start=True, stop=True)
                nc.tensor.matmul(bank[5][:, 0:B], block64[:], sq_c[:, T:T + B], start=True, stop=True)\
                    .then_inc(S["cn_done"], 1)
            pe.wait_ge(S["cn_sqrt"], 4)
            pe.wait_ge(S["decay_sum"], 5)
            pe.wait_ge(S["select_done"], 2)
            nc.tensor.matmul(bank[4][:, 0:B * H], later[:], decay[:, :, 0, :], start=True, stop=False)
            nc.tensor.matmul(bank[4][:, 0:B * H], ones[0:B, :], lf_diag[:, :, :].rearrange("p a b -> p (a b)"),
                             start=False, stop=True).then_inc(S["tail_done"], 1)

            def score(w):
                t, h = divmod(w, H)
                n, c, o = (t + 1) * P, h // 2, (h % 2) * HD
                if w >= 2:
                    pe.wait_ge(S["p_ready"], w - 1)
                out = bank[w % 2][:, 0:n]
                nc.tensor.matmul(out, q_t[o:o + HD, c, t * P:(t + 1) * P], k_t[o:o + HD, c, 0:n], start=True, stop=False)
                nc.tensor.matmul(out, sel[0:H, h, :], neg_cum[:, 0:n], start=False, stop=False)
                nc.tensor.matmul(out, cum[:, t * P:(t + 1) * P], sel[0:H, h, 0:1].to_broadcast([H, n]),
                                 start=False, stop=True).then_inc(S["s_done"], 1)

            def turn(w):
                t = w // H
                pe.wait_ge(S["p_ready"], w + 1)
                if w >= 2:
                    pe.wait_ge(S["pt_ready"], w - 1)
                for b in range(t + 1):
                    last = nc.tensor.transpose(bank[2 + w % 2][:, b * P:(b + 1) * P],
                                               probs[w % 2][:, b * P:(b + 1) * P], ident[:])
                last.then_inc(S["pt_done"], 1)

            def weigh(w):
                t, h = divmod(w, H)
                pe.wait_ge(S["pt_ready"], w + 1)
                if h == 0 and t >= 2:
                    pe.wait_ge(S["o_taken"], t - 1)
                for b in range(t + 1):
                    last = nc.tensor.matmul(bank[4 + t % 2][:, h * HD:(h + 1) * HD], probs_t[w % 2][:, b, :],
                                            v_r[:, b, h * HD:(h + 1) * HD], start=(b == 0), stop=(b == t))
                last.then_inc(S["pv_done"], 1)

            def turn_output(t):
                pe.wait_ge(S["o_ready"], t + 1)
                if t:
                    pe.wait_ge(S["mix_ready"], t)
                for c in range(C4):
                    last = nc.tensor.transpose(bank[6][:, c * P:(c + 1) * P],
                                               o_row[:, :, :].rearrange("p a b -> p (a b)")[:, c * P:(c + 1) * P],
                                               ident[:])
                last.then_inc(S["ot_done"], 1)

            pe.wait_ge(S["acc_dve"], 8)
            pe.wait_ge(S["tail_evac"], 1)
            pe.wait_ge(S["samp_evac"], 6)
            pe.wait_ge(S["samp_g"], 2)
            score(0)
            for w in range(NT * H):
                if w + 1 < NT * H:
                    score(w + 1)
                n = after_sections(w)
                if n is not None:
                    if n:
                        pe.wait_ge(S["part_ready"], 4 + n)
                    pe.wait_ge(b_loaded[n % 2], 16 * (n // 2 + 1))
                    ada_chunk(4 + n, bank[7], b_row[:, (n % 2) * SECS:(n % 2 + 1) * SECS])
                turn(w)
                weigh(w)
                if w % H == 2 and w > H:
                    turn_output(w // H - 1)
            turn_output(NT - 1)

            for j in range(6):
                pe.wait_ge(S["part_ready"], 4 + j + 1)
                if j == 0:
                    pe.wait_ge(S["mix_ready"], NT)
                if j >= 2:
                    pe.wait_ge(S["mod2_act"], j - 1)
                nc.tensor.matmul(bank[j % 2][0:B, :], sel8, part[:, j, :], start=True, stop=True)
                nc.tensor.matmul(bank[2 + j % 2][:, :], sel[:, B, :], part[:, j, :], start=True, stop=True)\
                    .then_inc(S["expand_done"], 1)

            def out_project(t):
                lo, n = t * P, (P if t < NT else B)
                if t == 0:
                    pe.wait_ge(S["wo_loaded"], 16)
                    pe.wait_ge(S["mix_ready_c"], 4)
                if t:
                    pe.wait_ge(S["wo_taken"], 2 * t)
                if t == NT:
                    pe.wait_ge(S["samp_norm_dve"], 2)
                for half in range(2):
                    for k in range(KD):
                        m = mix_a[:, k, lo:lo + n] if k < C4 else mix_c[:, k - C4, lo:lo + n]
                        last = nc.tensor.matmul(bank[4 + half][0:n, :], m, wo[:, k, half * 512:(half + 1) * 512],
                                                start=(k == 0), stop=(k == KD - 1))
                    last.then_inc(S["wo_done"], 1)

            def route(t):
                n = P if t < NT else B
                pe.wait_ge(S["h2_ready"], t + 1)
                if t:
                    pe.wait_ge(S["h2t_ready"], t)
                h = h_row[t % 2][0:n, :].rearrange("p (a k) -> p k a", k=KD)
                for k in range(KD):
                    last = nc.tensor.transpose(bank[6 + k // 4][:, (k % 4) * P:(k % 4) * P + n], h[:, k, :], ident[0:n, 0:n])
                last.then_inc(S["h2_psum"], 1)
                pe.wait_ge(S["h2t_ready"], t + 1)
                if t == 0:
                    pe.wait_ge(S["mod2_dve"], 2)
                    pe.wait_ge(S["wr_loaded"], 64)
                for k in range(KD):
                    last = nc.tensor.matmul(bank[3][0:n, t * 36:(t + 1) * 36], h2_t[:, k, 0:n], w_r[:, k, :],
                                            start=(k == 0), stop=(k == KD - 1))
                last.then_inc(S["lg_done"], 1)

            def sample_values(b):
                pe.wait_ge(S["exp_ready"], b + 1)
                if b == 0:
                    pe.wait_ge(S["zeroed"], 1)
                    pe.wait_ge(S["pnew_ready"], 1)
                if b >= 2:
                    pe.wait_ge(S["om_ready"], b - 1)
                for s in range(NCH):
                    g = NKV + b * NCH + s
                    pe.wait_ge(kv_loaded[g % RING], 16 * (g // RING + 1))
                    for j in range(CH):
                        last = nc.tensor.matmul(bank[b % 2][32 * j:32 * j + H, :], scores[:, b, s * CH + j, :],
                                                v_ring[:, g % RING, j, :], start=(s == 0),
                                                stop=(s == NCH - 1 and j > 0))
                    last.then_inc(S["v_used"], 1)
                nc.tensor.matmul(bank[b % 2][0:H, :], p_new[0:B, b, :], v_new[:], start=False, stop=True)\
                    .then_inc(S["pvs_done"], 1)

            def gather_values(b):
                pe.wait_ge(S["om_ready"], b + 1)
                for c in range(C4):
                    last = nc.tensor.matmul(bank[2][:, c * B + b:c * B + b + 1], o_m[b % 2][:, c * P:(c + 1) * P],
                                            ones[:, 0:1], start=True, stop=True)
                last.then_inc(S["ot2_done"], 1)

            pe.wait_ge(S["mod2_act"], 4)
            for t in range(NT):
                out_project(t)
                sample_values(2 * t)
                if t:
                    gather_values(2 * t - 1)
                route(t)
                sample_values(2 * t + 1)
                gather_values(2 * t)
            gather_values(B - 1)
            pe.wait_ge(S["softmax_in"], 4)
            for c in range(C4):
                for hh in range(2):
                    last = nc.tensor.matmul(bank[2][hh * HD:(hh + 1) * HD, 64 + c * B:64 + (c + 1) * B],
                                            ones[:, 0:HD], p_sum[:, :, 2 * c + hh], start=True, stop=True)
            last.then_inc(S["samp_norm_psum"], 1)
            pe.wait_ge(S["samp_norm_act"], 1)
            nc.tensor.matmul(bank[2][:, 128:128 + C4 * B], block64[:], o_q[:, :, :].rearrange("p a b -> p (a b)"),
                             start=True, stop=True).then_inc(S["samp_norm_psum"], 1)
            out_project(NT)
            route(NT)

            pe.wait_ge(S["route_in"], 3)
            for t in range(5):
                n = P if t < NT else B
                for u in range(t + 1):
                    l = ones[:, 0:n] if u < t else earlier[0:n, 0:n]
                    m = P if u < NT else B
                    nc.tensor.matmul(bank[0][0:n, t * NE:(t + 1) * NE], l, both[0:m, u, :],
                                     start=(u == 0), stop=(u == t))
            for u in range(5):
                m = P if u < NT else B
                last = nc.tensor.matmul(bank[1][:, 0:NE], ones[0:m, :], both[0:m, u, :], start=(u == 0), stop=(u == 4))
            last.then_inc(S["rank_done"], 1)

            def tables(wait_on, count, done):
                pe.wait_ge(wait_on, count)
                for c in range(2):
                    for t in range(5):
                        m = P if t < NT else B
                        last = nc.tensor.matmul(bank[2][:, 0:3 * NE], slot_is[0:m, c, t, :], vals[0:m, c, t, :],
                                                start=(c == 0 and t == 0), stop=(c == 1 and t == 4))
                last.then_inc(done, 1)

            tables(S["vals_ready"], 1, S["tabs_done"])

            def gate_up(s, xs):
                gw = exp_w[s][:, 0:2048].rearrange("p (a c f) -> p a c f", a=2, c=4)
                uw = exp_w[s][:, 2048:4096].rearrange("p (a c f) -> p a c f", a=2, c=4)
                for a in range(2):
                    for c in range(4):
                        k = 4 * a + c
                        nc.tensor.matmul(bank[2 + xs][0:SLOTS, 0:DE], xe_t[xs][:, c, a, :], gw[:, a, c, :],
                                         start=(k == 0), stop=(k == 7))
                        last = nc.tensor.matmul(bank[2 + xs][SLOTS:2 * SLOTS, 0:DE], xe_t[xs][:, c, a, :],
                                                uw[:, a, c, :], start=(k == 0), stop=(k == 7))
                return last

            def transpose_x(xs):
                x4 = x_e[xs][:, :].rearrange("p (a c) -> p c a", c=4)
                for c in range(4):
                    last = nc.tensor.transpose(bank[xs][:, c * P:(c + 1) * P], x4[:, c, :], ident[:])
                return last

            def transpose_hidden(xs):
                h2 = hid[xs][:, :].rearrange("p (a k) -> p k a", k=2)
                for k in range(2):
                    last = nc.tensor.matmul(bank[2 + xs][:, 256 + k * SLOTS:256 + (k + 1) * SLOTS], h2[:, k, :],
                                            ident[0:SLOTS, 0:SLOTS], start=True, stop=True)
                return last

            def down(s, xs):
                dw = exp_w[s][:, 4096:6144].rearrange("p (k n) -> p k n", k=2)
                for k in range(2):
                    for half in range(2):
                        last = nc.tensor.matmul(bank[4 + xs][half * SLOTS:(half + 1) * SLOTS, :], hid_t[xs][:, k, :],
                                                dw[:, k, half * 512:(half + 1) * 512], start=(k == 0), stop=(k == 1))
                return last

            def front_of(g, s):
                xs, e1 = s % 2, 4 * g + s + 1
                pe.wait_ge(xe_loaded[xs], (2 * g + s // 2 + 1) * 16)
                transpose_x(xs).then_inc(S["xe_done"], 1)
                pe.wait_ge(S["xet_ready"], e1)
                pe.wait_ge(gate_loaded[s], (g + 1) * 32)
                gate_up(s, xs).then_inc(S["gu_done"], 1)

            def back_of(g, s):
                xs, e1 = s % 2, 4 * g + s + 1
                pe.wait_ge(S["hid_ready"], e1)
                transpose_hidden(xs).then_inc(S["hidt_done"], 1)
                pe.wait_ge(S["hidt_ready"], e1)
                pe.wait_ge(down_loaded[s], (g + 1) * 16)
                pe.wait_ge(S["y_ready"], e1)
                down(s, xs).then_inc(S["y_done"], 1)

            pe.wait_ge(S["tabs_ready"], 1)
            front_of(0, 0)
            front_of(0, 1)
            back_of(0, 0)
            front_of(0, 2)
            back_of(0, 1)
            front_of(0, 3)
            back_of(0, 2)
            with pe.Fori(1, NE // 4) as g:
                for s in range(4):
                    front_of(g, s)
                    if s == 0:
                        back_of(g - 1, 3)
                    else:
                        back_of(g, s - 1)
            back_of(NE // 4 - 1, 3)

            count = pe.value_load(max_count[0:1, 0:1], min_val=0, max_val=2 * (T + B))
            with pe.If(count > cap):
                with pe.Fori(1, PASSES) as p:
                    tables(S["vals_ready"], p + 1, S["tabs_done"])
                    with pe.Fori(0, NE) as e:
                        n = p * NE + e
                        pe.wait_ge(xe_loaded[0], (n - NE) * 16 + NE * 8 + 16)
                        transpose_x(0).then_inc(S["xe_done"], 1)
                        pe.wait_ge(S["xet_ready"], n + 1)
                        pe.wait_ge(gate_loaded[0], (n - NE) * 32 + NE * 8 + 32)
                        gate_up(0, 0).then_inc(S["gu_done"], 1)
                        pe.wait_ge(S["hid_ready"], n + 1)
                        transpose_hidden(0).then_inc(S["hidt_done"], 1)
                        pe.wait_ge(S["hidt_ready"], n + 1)
                        pe.wait_ge(down_loaded[0], (n - NE) * 16 + NE * 4 + 16)
                        pe.wait_ge(S["y_ready"], n + 1)
                        down(0, 0).then_inc(S["y_done"], 1)

            for j in range(6):
                if j >= 2:
                    pe.wait_ge(S["mod3_ready"], j - 1)
                nc.tensor.matmul(bank[j % 2][0:B, :], sel8, part[:, 6 + j, :], start=True, stop=True)
                nc.tensor.matmul(bank[2 + j % 2][:, :], sel[:, B, :], part[:, 6 + j, :], start=True, stop=True)\
                    .then_inc(S["expand_done"], 1)

        @block.scalar
        def _(act):
            steps = [0]

            def step(ins):
                steps[0] += 1
                ins.then_inc(S["act_step"], 1)
                act.wait_ge(S["act_step"], steps[0])

            def copy(out, in_, scale=1.0):
                return nc.scalar.activation(out, in_, ACT.Copy, scale=scale)

            act.wait_ge(S["c_loaded"], 32)
            nc.scalar.activation(c_row[:, :], c_row[:, :], ACT.Silu).then_inc(S["c_silu"], 1)
            act.wait_ge(S["x_loaded"], 32)
            act.wait_ge(S["consts_ready"], 2)
            for t in (NT, 0, 1, 2, 3):
                n = P if t < NT else B
                step(nc.scalar.activation(junk[0:n, :], x_a[0:n, t, :], ACT.Square, accum_out=ssq[0:n, t:t + 1]))
            nc.scalar.activation(ssq[:, :], ssq[:, :], ACT.Sqrt, bias=eps[:, 0:1], scale=1.0 / D)\
                .then_inc(S["rstd_sq"], 1)
            for n in range(4):
                act.wait_ge(S["ada_done"], n + 1)
                copy(part_a[:, n, :], bank[n % 2][:, :]).then_inc(S["part_ready"], 1)
                if n in (1, 2):
                    m = n - 1
                    act.wait_ge(S["expand_done"], m + 1)
                    copy(sh1_s[0:B, m * SECS:(m + 1) * SECS], bank[2 + m][0:B, :])
                    copy(sh1_p[:, m * SECS:(m + 1) * SECS], bank[4 + m][:, :]).then_inc(S["sh_ready"], 1)
            for i in range(5):
                act.wait_ge(S["h_psum"], i + 1)
                if i == 0:
                    copy(h_t[:, :, T:T + B], bank[6][:, 64:128].rearrange("p (k n) -> p k n", k=KD))\
                        .then_inc(S["ht_ready"], 1)
                    continue
                lo = (i - 1) * P
                for q in range(2):
                    last = copy(h_t[:, 4 * q:4 * q + 4, lo:lo + P],
                                bank[(2 if i % 2 else 4) + q][:, :].rearrange("p (k n) -> p k n", k=4))
                last.then_inc(S["ht_ready"], 1)
                if i == 1:
                    act.wait_ge(S["samp_done"], 1)
                    copy(s_part[:, 0, :], bank[7][:, :]).then_inc(S["samp_evac"], 1)
                    act.wait_ge(S["row_done"], 1)
                    copy(qk_new[:, 0, :], bank[6][0:B, :]).then_inc(S["row_evac"], 1)
                    act.wait_ge(S["row_evac"], 1)
                    act.dma_start(q_rows_dram[:, :], qk_new[:, 0, :]).then_inc(S["q_stored"], 16)

            def acc(s, m):
                act.wait_ge(S["acc_done"], 4 * s + m + 1)

            for m in range(4):
                acc(0, m)
                copy(q_t[:, m, :], bank[m][:, :], SCALE).then_inc(S["acc_act"], 1)
            for s in (1, 2):
                act.wait_ge(S["samp_done"], s + 1)
                copy(s_part[:, s, :], bank[7][:, :]).then_inc(S["samp_evac"], 1)
                for m in range(4):
                    acc(s, m)
                    copy((k_t if s == 1 else v_r)[:, m, :], bank[m][:, :]).then_inc(S["acc_act"], 1)
                act.wait_ge(S["row_done"], s + 1)
                new = qk_new[:, 1, :] if s == 1 else v_new[:, :]
                copy(new, bank[6][0:B, :]).then_inc(S["row_evac"], 1)
                act.wait_ge(S["row_evac"], s + 1)
                dst = (k_sample if s == 1 else v_sample).rearrange("l b t h d -> (l b t) (h d)")
                act.dma_start(dst, new).then_inc(S["outs"], 16)
            act.wait_ge(S["acc_act"], 12)
            act.dma_start(v_prompt.rearrange("l b (t p) h d -> (l b p) t (h d)", p=P), v_r[:, :, :])\
                .then_inc(S["outs"], 16)
            kp = k_prompt.rearrange("l b (t p) h d -> (l b t) p (h d)", p=P)
            for t in range(NT):
                act.wait_ge(S["krow_done"], t + 1)
                if t >= 2:
                    act.wait_ge(krow_out[t % 2], 16)
                copy(k_row[t % 2][:, :], bank[4 + t % 2][:, :]).then_inc(S["krow_evac"], 1)
                act.wait_ge(S["krow_evac"], t + 1)
                act.dma_start(kp[t, :, :], k_row[t % 2][:, :]).then_inc(krow_out[t % 2], 16)
            act.wait_ge(S["f_taken"], 1)
            step(nc.scalar.activation(f_a[:, :], f_a[:, :], ACT.Exp, scale=-1.0))
            nc.scalar.activation(f_a[:, :], f_a[:, :], ACT.Ln, bias=ones[0:H, 0:1]).then_inc(S["ln_ready"], 1)
            act.wait_ge(S["samp_done"], 4)
            act.wait_ge(S["consts_ready"], 3)
            copy(u_part[:, :], bank[7][:, :]).then_inc(S["samp_evac"], 1)
            for m in range(4):
                acc(3, m)
                copy(conv_in[:, m, 2:2 + T], bank[m][:, :]).then_inc(S["acc_act"], 1)
            act.wait_ge(S["samp_t"], 1)
            copy(conv_in[:, :, T + 2:T + 2 + B], bank[6][:, 0:C4 * B].rearrange("p (c b) -> p c b", c=C4))\
                .then_inc(S["samp_u"], 1)
            act.wait_ge(S["lf_done"], 1)
            copy(lf_rows[:, 0:NT, :], bank[4][:, 0:NT * H].rearrange("p (t h) -> p t h", t=NT))\
                .then_inc(S["lf_evac"], 1)
            copy(lf_rows[0:B, NT, :], bank[4][0:B, 32:32 + H]).then_inc(S["lf_evac"], 1)
            act.wait_ge(S["lf_evac"], 2)
            act.dma_start(logf_prompt.rearrange("l b (t p) h -> (l b p) t h", p=P), lf_rows[:, 0:NT, :])\
                .then_inc(S["outs"], 16)
            act.dma_start(logf_sample.rearrange("l b t h -> (l b t) h"), lf_rows[0:B, NT, :])\
                .then_inc(S["outs"], 16)
            act.wait_ge(S["st_done"], 1)
            copy(state_t[:, :, :, :], bank[5][:, 0:C4 * 16].rearrange("p (c b j) -> p c b j", c=C4, b=B))\
                .then_inc(S["st_evac"], 1)
            for s in (4, 5):
                act.wait_ge(S["samp_done"], s + 1)
                act.wait_ge(S["samp_t"], s - 3)
                copy(u_part[:, :], bank[7][:, :]).then_inc(S["samp_evac"], 1)
            act.wait_ge(S["crow_done"], 1)
            act.wait_ge(krow_out[0], 32)
            act.wait_ge(krow_out[1], 32)
            copy(c_rows[:, :], bank[4][0:2 + B, :]).then_inc(S["crow_evac"], 1)
            act.wait_ge(S["crow_evac"], 1)
            act.dma_start(conv_prompt.rearrange("l b j c -> (l b j) c"), c_rows[0:2, :]).then_inc(S["outs"], 16)
            act.dma_start(conv_sample[0, :, 1, :], c_rows[2:2 + B, :]).then_inc(S["outs"], 16)
            for c in range(C4):
                act.wait_ge(S["acc_dve"], 4 + C4)
                act.wait_ge(S["samp_g"], 2)
                if c:
                    act.wait_ge(S["cn_done"], c)
                nc.scalar.activation(sq_c[:, :], mix_c[:, c, :], ACT.Square).then_inc(S["sq_ready"], 1)
                act.wait_ge(S["cn_done"], c + 1)
                if c:
                    act.wait_ge(S["mix_ready_c"], c)
                nc.scalar.activation(rt_c[:, 0:T], bank[4][:, :], ACT.Sqrt, bias=eps[:, 0:1], scale=1.0 / HD)
                nc.scalar.activation(rt_c[:, T:T + B], bank[5][:, 0:B], ACT.Sqrt, bias=eps[:, 0:1], scale=1.0 / HD)\
                    .then_inc(S["cn_sqrt"], 1)
            act.wait_ge(S["tail_done"], 1)
            copy(tail[:, :, :], bank[4][:, 0:B * H].rearrange("p (b h) -> p b h", b=B)).then_inc(S["tail_evac"], 1)
            act.wait_ge(S["outs"], 16 * 7)
            act.wait_ge(S["mix_ready_c"], 4)

            def ada_evac(n):
                act.wait_ge(S["ada_done"], 4 + n + 1)
                copy(part[:, n, :], bank[7][:, :]).then_inc(S["part_ready"], 1)

            def soft(w):
                t = w // H
                n = (t + 1) * P
                act.wait_ge(S["max_ready"], w + 1)
                if w >= 2:
                    act.wait_ge(S["pt_done"], w - 1)
                i = (t % 2) * H + w % H
                nc.scalar.activation(probs[w % 2][:, 0:n], bank[w % 2][:, 0:n], ACT.Exp,
                                     bias=neg_max[:, w % 2:w % 2 + 1], accum_out=row_sum[:, i:i + 1])\
                    .then_inc(S["p_ready"], 1)

            def norm_output(t):
                act.wait_ge(S["o_taken"], t + 1)
                nc.scalar.activation(o_sq[:, :, :], o_row[:, :, :], ACT.Square).then_inc(S["o_sq_ready"], 1)
                act.wait_ge(S["o_ssq"], t + 1)
                nc.scalar.activation(head_ssq[:, :], head_ssq[:, :], ACT.Sqrt, bias=eps[:, 0:1], scale=1.0 / HD)\
                    .then_inc(S["o_sqrt"], 1)

            def output_out(t):
                act.wait_ge(S["ot_done"], t + 1)
                for c in range(C4):
                    last = copy(mix_a[:, c, t * P:(t + 1) * P], bank[6][:, c * P:(c + 1) * P], vecs[:, c:c + 1])
                last.then_inc(S["mix_ready"], 1)

            soft(0)
            for w in range(NT * H):
                if w + 1 < NT * H:
                    soft(w + 1)
                n = after_sections(w)
                if n is not None:
                    ada_evac(n)
                t = w // H
                act.wait_ge(S["pt_done"], w + 1)
                if w >= 2:
                    act.wait_ge(S["pv_done"], w - 1)
                copy(probs_t[w % 2][:, 0:t + 1, :],
                     bank[2 + w % 2][:, 0:(t + 1) * P].rearrange("p (b n) -> p b n", n=P)).then_inc(S["pt_ready"], 1)
                if w % H == 1 and w > H:
                    norm_output(t - 1)
                if w % H == 2 and w > H:
                    output_out(t - 1)
            norm_output(NT - 1)
            output_out(NT - 1)

            for j in range(6):
                act.wait_ge(S["expand_done"], j + 5)
                half = slice((j % 2) * SECS, (j % 2 + 1) * SECS)
                if j < 4:
                    copy((ga1_s if j < 2 else sh2_s)[0:B, half], bank[j % 2][0:B, :])
                    copy((ga1_p if j < 2 else sh2_p)[:, half], bank[2 + j % 2][:, :]).then_inc(S["mod2_act"], 1)

            act.wait_ge(S["softmax_in"], 2)
            nc.scalar.activation(p_new[:, :, :], p_new[:, :, :], ACT.Exp).then_inc(S["pnew_ready"], 1)
            act.wait_ge(S["softmax_in"], 3)
            for b in range(B):
                nc.scalar.activation(scores[:, b, :, :], scores[:, b, :, :], ACT.Exp).then_inc(S["exp_ready"], 1)

            def second_norm(t):
                n = P if t < NT else B
                act.wait_ge(S["x1_ready"], t + 1)
                step(nc.scalar.activation(junk2[0:n, :], x_r[0:n, t, :], ACT.Square, accum_out=ssq[0:n, t:t + 1]))
                nc.scalar.activation(ssq[0:n, t:t + 1], ssq[0:n, t:t + 1], ACT.Sqrt, bias=eps[0:n, 0:1], scale=1.0 / D)\
                    .then_inc(S["norm_sqrt"], 1)
                act.wait_ge(S["h2_ready"], t + 1)
                act.dma_start(h2_dram[t * 2 * P:t * 2 * P + 2 * n, :].rearrange("(p a) d -> p (a d)", a=2),
                              h_row[t % 2][0:n, :]).then_inc(h2_out[t % 2], 16)
                act.wait_ge(S["h2_psum"], t + 1)
                if t:
                    act.wait_ge(S["lg_done"], t)
                for q in range(2):
                    last = copy(h2_t[:, 4 * q:4 * q + 4, 0:n],
                                bank[6 + q][:, :].rearrange("p (k n) -> p k n", k=4)[:, :, 0:n])
                last.then_inc(S["h2t_ready"], 1)

            for t in range(NT):
                second_norm(t)
            act.wait_ge(S["samp_norm_dve"], 1)
            nc.scalar.activation(o_q[:, :, :], o_t[:, :, :], ACT.Square).then_inc(S["samp_norm_act"], 1)
            act.wait_ge(S["samp_norm_psum"], 2)
            nc.scalar.activation(o_r[:, :, :], bank[2][:, 128:128 + C4 * B].rearrange("p (c b) -> p c b", c=C4),
                                 ACT.Sqrt, bias=eps[:, 0:1], scale=1.0 / HD).then_inc(S["samp_norm_act"], 1)
            second_norm(NT)
            act.wait_ge(S["route_in"], 1)
            nc.scalar.activation(ge[:, :, :], ge[:, :, :], ACT.Exp).then_inc(S["route_exp"], 1)
            act.wait_ge(S["route_in"], 2)
            nc.scalar.activation(el[:, :, :], el[:, :, :], ACT.Exp).then_inc(S["route_exp"], 1)

            def x_out(xs):
                return copy(xe_t[xs][:, :, :, :],
                            bank[xs][:, :].rearrange("p (c a n) -> p c a n", c=4, a=2))

            def gate_silu(xs):
                return nc.scalar.activation(sig[xs][:, :], bank[2 + xs][0:SLOTS, 0:DE], ACT.Silu)

            with act.Fori(0, NE // 4) as g:
                for s in range(4):
                    xs, e1 = s % 2, 4 * g + s + 1
                    act.wait_ge(S["xe_done"], e1)
                    if s >= 2:
                        act.wait_ge(S["gu_done"], e1 - 2)
                    x_out(xs).then_inc(S["xet_ready"], 1)
                    act.wait_ge(S["gu_done"], e1)
                    gate_silu(xs).then_inc(S["sig_ready"], 1)
            count = act.value_load(max_count[0:1, 0:1], min_val=0, max_val=2 * (T + B))
            with act.If(count > cap):
                with act.Fori(NE, PASSES * NE) as n:
                    act.wait_ge(S["xe_done"], n + 1)
                    x_out(0).then_inc(S["xet_ready"], 1)
                    act.wait_ge(S["gu_done"], n + 1)
                    gate_silu(0).then_inc(S["sig_ready"], 1)

            for j in range(6):
                act.wait_ge(S["expand_done"], j + 11)
                half = slice((j % 2) * SECS, (j % 2 + 1) * SECS)
                if j < 4:
                    copy((ga2_s if j < 2 else shf_s)[0:B, half], bank[j % 2][0:B, :])
                    copy((ga2_p if j < 2 else shf_p)[:, half], bank[2 + j % 2][:, :]).then_inc(S["mod3_ready"], 1)
            for i, t in enumerate((0, 1, 2, 3, NT)):
                n = P if t < NT else B
                act.wait_ge(S["x1_ready"], i + 6)
                step(nc.scalar.activation(junk2[0:n, :], x_r[0:n, t, :], ACT.Square, accum_out=ssq[0:n, t:t + 1]))
                nc.scalar.activation(ssq[0:n, t:t + 1], ssq[0:n, t:t + 1], ACT.Sqrt, bias=eps[0:n, 0:1], scale=1.0 / D)\
                    .then_inc(S["norm_sqrt"], 1)
            act.wait_ge(S["outs"], 16 * 7)

        @block.vector
        def _(dve):
            V = nc.vector
            steps = [0]

            def step(ins):
                steps[0] += 1
                ins.then_inc(S["dve_step"], 1)
                dve.wait_ge(S["dve_step"], steps[0])

            def spread(ap, shape):
                return ap.to_broadcast(shape)

            step(V.memset(c_t[:, :, :], 0.0))
            dve.wait_ge(S["pt_loaded"], 16)
            V.tensor_copy(pt_exp[:, :, :], spread(pt_int[:, :].rearrange("b (j o) -> b j o", o=1), [B, NPG, 4]))\
                .then_inc(S["setup_ready"], 1)
            dve.wait_ge(S["consts_ready"], 1)
            step(V.tensor_single_scalar(lane[:, :], lane[:, :], 3, ALU.bitwise_and))
            step(V.tensor_copy(quarter[:, 8:9], lane[:, :]))
            for s in range(NCH):
                last = V.tensor_scalar(quarter[:, s:s + 1], quarter[:, 8:9], float(NCH), float(s), ALU.mult, ALU.add)
            step(last)
            dve.wait_ge(S["setup_psum"], 1)
            ids = bank[6][:, 32:32 + B]
            V.tensor_scalar(f_index[:, :], ids, 4.0, quarter[:, 8:9], ALU.mult, ALU.add).then_inc(S["setup_ready"], 1)
            for s in range(NCH):
                last = V.tensor_scalar(kv_index[:, :].rearrange("p (b s) -> p s b", s=NCH)[:, s, :], ids,
                                       4.0 * NCH, quarter[:, s:s + 1], ALU.mult, ALU.add)
            last.then_inc(S["setup_ready"], 1)
            dve.wait_ge(S["setup_psum"], 2)
            V.tensor_copy(c_t[:, :, 0:B + 1], bank[7][:, 0:KD * 9].rearrange("p (k n) -> p k n", k=KD))\
                .then_inc(S["setup_ready"], 1)
            dve.wait_ge(S["setup_psum"], 3)
            V.tensor_copy(vecs[:, :], bank[6][:, 0:20]).then_inc(S["setup_ready"], 1)
            dve.wait_ge(S["rstd_sq"], 1)
            step(V.reciprocal(rstd[:, :], ssq[:, :]))
            dve.wait_ge(S["g_loaded"], 16)
            for m in range(2):
                dve.wait_ge(S["expand_done"], m + 3)
                lo = slice(m * SECS, (m + 1) * SECS)
                V.scalar_tensor_tensor(sc1_s[0:B, lo], bank[2 + m][0:B, :], 1.0, g1_b[0:B, lo], ALU.add, ALU.mult)
                step(V.scalar_tensor_tensor(sc1_p[:, lo], bank[4 + m][:, :], 1.0, g1_b[:, lo], ALU.add, ALU.mult))
            dve.wait_ge(S["sh_ready"], 2)
            for i in range(5):
                t, n = (NT, B) if i == 0 else (i - 1, P)
                sc, sh = (sc1_s, sh1_s) if i == 0 else (sc1_p, sh1_p)
                if i >= 2:
                    dve.wait_ge(S["h_psum"], i - 1)
                r = h_row[i % 2]
                step(V.scalar_tensor_tensor(r[0:n, :], x_a[0:n, t, :], rstd[0:n, t:t + 1], sc[0:n, :], ALU.mult, ALU.mult))
                V.tensor_tensor(r[0:n, :], r[0:n, :], sh[0:n, :], ALU.add).then_inc(S["h_row_ready"], 1)

            def k_chunk(n):
                b, s = divmod(n, NCH)
                dve.wait_ge(kv_loaded[n % RING], 16 * (n // RING + 1))
                if s == 0:
                    dve.wait_ge(qb_loaded[b % 2], 16 * (b // 2 + 1))
                if n:
                    dve.wait_ge(S["k_used"], n)
                q = q_b[:, b % 2, :].rearrange("p (o c) -> p o c", o=1)
                step(V.tensor_tensor(prod[:, :, :].rearrange("p (r h) d -> p r (h d)", r=CH),
                                     kv[:, n % RING, :, :].rearrange("p (r h) d -> p r (h d)", r=CH),
                                     spread(q, [P, CH, HW]), ALU.mult))
                V.reduce_sum(scores[:, b, s * CH:(s + 1) * CH, :].rearrange("p r h -> p (r h)"),
                             prod[:, :, :], AX.X).then_inc(S["k_used"], 1)
            next_k = [0]

            def k_chunks(m):
                for _ in range(m):
                    if next_k[0] < NKV:
                        k_chunk(next_k[0])
                        next_k[0] += 1

            k_chunks(NEW_AT)
            dve.wait_ge(S["row_evac"], 2)
            step(V.tensor_tensor(qk_prod[:, :], qk_new[:, 0, :], qk_new[:, 1, :], ALU.mult))
            step(V.memset(news[:, :, :], NEG))
            step(V.reduce_sum(top[0:B, 0, :], qk_prod[:, :].rearrange("p (h d) -> p h d", h=H), AX.X))
            V.tensor_scalar(news[0:B, :, :], spread(top[0:B, 0:1, :], [B, B, H]), SCALE, None, ALU.mult)\
                .then_inc(S["select_in"], 1)
            dve.wait_ge(S["f_done"], 1)
            dve.wait_ge(S["vec_loaded"], 64)
            V.tensor_scalar(f_t[:, 0:T], bank[4][0:H, :], b_f[:, 0:1], None, ALU.add)
            step(V.tensor_scalar(f_t[:, T:T + B], bank[5][0:H, 0:B], b_f[:, 0:1], None, ALU.add))
            step(V.tensor_scalar(f_a[:, :], f_t[:, :], -1.0, None, ALU.mult))
            V.tensor_tensor(f_a[:, :], f_a[:, :], f_t[:, :], ALU.max).then_inc(S["f_taken"], 1)
            k_chunks(1)
            dve.wait_ge(S["ln_ready"], 1)
            step(V.scalar_tensor_tensor(f_t[:, :], f_t[:, :], 0.0, f_a[:, :], ALU.min, ALU.subtract))
            step(V.tensor_tensor_scan(cum[:, :], f_t[:, 0:T], f_t[:, 0:T], 0.0, ALU.add, ALU.bypass))
            V.tensor_scalar(neg_cum[:, 0:T], cum[:, :], -1.0, None, ALU.mult).then_inc(S["lf_ready"], 1)
            k_chunks(DIAG_AT - NEW_AT - 1)
            dve.wait_ge(S["lf_evac"], 2)
            V.tensor_copy(lf_diag[:, :, :], spread(lf_rows[0:B, NT:NT + 1, :], [B, B, H])).then_inc(S["select_in"], 1)
            for m in range(4):
                dve.wait_ge(S["acc_done"], 16 + m + 1)
                dve.wait_ge(S["acc_act"], 12 + m + 1)
                V.tensor_tensor(conv_in[:, m, 2:2 + T], bank[m][:, :], conv_in[:, m, 2:2 + T], ALU.mult)\
                    .then_inc(S["acc_dve"], 1)
                k_chunks(1)
            dve.wait_ge(S["samp_t"], 2)
            dve.wait_ge(S["samp_u"], 1)
            new_in = conv_in[:, :, T + 2:T + 2 + B]
            V.tensor_tensor(new_in, bank[6][:, 0:C4 * B].rearrange("p (c b) -> p c b", c=C4), new_in, ALU.mult)\
                .then_inc(S["samp_g"], 1)
            dve.wait_ge(S["samp_g"], 1)
            dve.wait_ge(S["acc_dve"], 4)
            dve.wait_ge(S["st_evac"], 1)
            for j in range(3):
                src = state_t[:, :, :, j] if j < 2 else new_in
                w = spread(vecs[:, 8 + 4 * j:12 + 4 * j].rearrange("p (c o) -> p c o", o=1), [P, C4, B])
                out = mix_c[:, :, T:T + B] if j == 0 else y_tmp[:, :, :]
                step(V.tensor_tensor(out, src, w, ALU.mult))
                if j:
                    step(V.tensor_tensor(mix_c[:, :, T:T + B], mix_c[:, :, T:T + B], y_tmp[:, :, :], ALU.add))
            for m in range(4):
                out = mix_c[:, m, 0:T]
                step(V.tensor_scalar(out, conv_in[:, m, 0:T], vecs[:, 8 + m:9 + m], None, ALU.mult))
                for j in (1, 2):
                    step(V.scalar_tensor_tensor(out, conv_in[:, m, j:j + T], vecs[:, 8 + 4 * j + m:9 + 4 * j + m], out,
                                                ALU.mult, ALU.add))
            for m in range(4):
                dve.wait_ge(S["acc_done"], 20 + m + 1)
                V.tensor_tensor(mix_c[:, m, 0:T], bank[m][:, :], mix_c[:, m, 0:T], ALU.mult).then_inc(S["acc_dve"], 1)
                k_chunks(1)
            dve.wait_ge(S["samp_t"], 3)
            V.tensor_tensor(mix_c[:, :, T:T + B], bank[6][:, 0:C4 * B].rearrange("p (c b) -> p c b", c=C4),
                            mix_c[:, :, T:T + B], ALU.mult).then_inc(S["samp_g"], 1)
            for c in range(C4):
                dve.wait_ge(S["cn_sqrt"], c + 1)
                step(V.reciprocal(rt_c[:, :], rt_c[:, :]))
                V.scalar_tensor_tensor(mix_c[:, c, :], mix_c[:, c, :], vecs[:, 4 + c:5 + c], rt_c[:, :],
                                       ALU.mult, ALU.mult).then_inc(S["mix_ready_c"], 1)

            def row_max(w):
                t = w // H
                n = (t + 1) * P
                dve.wait_ge(S["s_done"], w + 1)
                step(V.tensor_tensor(bank[w % 2][:, t * P:n], bank[w % 2][:, t * P:n], causal[:, :], ALU.add))
                if w >= 2:
                    dve.wait_ge(S["p_ready"], w - 1)
                V.reduce_max(neg_max[:, w % 2:w % 2 + 1], bank[w % 2][:, 0:n], AX.X, negate=True)\
                    .then_inc(S["max_ready"], 1)

            def attention_output(t):
                dve.wait_ge(S["pv_done"], H * (t + 1))
                sums = row_sum[:, (t % 2) * H:(t % 2 + 1) * H]
                step(V.reciprocal(sums, sums))
                if t:
                    dve.wait_ge(S["ot_done"], t)
                V.tensor_tensor(o_row[:, :, :], bank[4 + t % 2][:, :].rearrange("p (h d) -> p h d", h=H),
                                spread(sums.rearrange("p (h o) -> p h o", o=1), [P, H, HD]), ALU.mult)\
                    .then_inc(S["o_taken"], 1)

            def attention_norm(t):
                dve.wait_ge(S["o_sq_ready"], t + 1)
                V.reduce_sum(head_ssq[:, :], o_sq[:, :, :], AX.X).then_inc(S["o_ssq"], 1)
                dve.wait_ge(S["o_sqrt"], t + 1)
                step(V.reciprocal(head_ssq[:, :], head_ssq[:, :]))
                V.tensor_tensor(o_row[:, :, :], o_row[:, :, :],
                                spread(head_ssq[:, :].rearrange("p (h o) -> p h o", o=1), [P, H, HD]), ALU.mult)\
                    .then_inc(S["o_ready"], 1)

            for w in range(NT * H):
                row_max(w)
                if w % H == 1 and w > H:
                    attention_output(w // H - 1)
                if w % H == 2 and w > H:
                    attention_norm(w // H - 1)
                if w % H != 7:
                    k_chunks(1)
            attention_output(NT - 1)
            attention_norm(NT - 1)
            k_chunks(NKV)

            dve.wait_ge(S["g_loaded"], 32)
            for j in (4, 5):
                dve.wait_ge(S["expand_done"], j + 5)
                lo = slice((j % 2) * SECS, (j % 2 + 1) * SECS)
                V.scalar_tensor_tensor(sc2_s[0:B, lo], bank[j % 2][0:B, :], 1.0, g_b[0:B, lo], ALU.add, ALU.mult)
                V.scalar_tensor_tensor(sc2_p[:, lo], bank[2 + j % 2][:, :], 1.0, g_b[:, lo], ALU.add, ALU.mult)\
                    .then_inc(S["mod2_dve"], 1)
            dve.wait_ge(S["mod2_dve"], 2)
            dve.wait_ge(S["mod2_act"], 4)
            V.memset(bank[0][:, :], 0.0)
            V.memset(bank[1][:, :], 0.0).then_inc(S["zeroed"], 1)

            flat = scores[:, :, :, :].rearrange("p b i h -> p (b i h)")
            dve.wait_ge(S["k_used"], NKV)
            dve.wait_ge(S["select_done"], 3)
            step(V.scalar_tensor_tensor(flat, flat, SCALE, decay[:, :, :, :].rearrange("p b i h -> p (b i h)"),
                                        ALU.mult, ALU.add))
            step(V.reduce_max(top[:, :, :], scores[:, :, :, :].rearrange("p b i h -> p b h i"), AX.X))
            dve.wait_ge(S["select_done"], 1)
            V.tensor_tensor(top[:, :, :], top[:, :, :], news[:, :, :], ALU.max).then_inc(S["softmax_in"], 1)
            dve.wait_ge(S["top_ready"], 1)
            V.tensor_tensor(p_new[:, :, :], news[:, :, :], top_all[:, :, :], ALU.subtract).then_inc(S["softmax_in"], 1)
            V.tensor_tensor(scores[:, :, :, :], scores[:, :, :, :],
                            spread(top_all[:, :, :].rearrange("p b (o h) -> p b o h", o=1), [P, B, PPP, H]),
                            ALU.subtract).then_inc(S["softmax_in"], 1)

            def residual(t):
                n = P if t < NT else B
                ga, sc, sh = (ga1_p, sc2_p, sh2_p) if t < NT else (ga1_s, sc2_s, sh2_s)
                for half in range(2):
                    lo = slice(half * 512, (half + 1) * 512)
                    dve.wait_ge(S["wo_done"], 2 * t + half + 1)
                    V.tensor_tensor(prod_o[0:n, lo], bank[4 + half][0:n, :], ga[0:n, lo], ALU.mult)\
                        .then_inc(S["wo_taken"], 1)
                dve.wait_ge(S["wo_taken"], 2 * t + 2)
                if t == 0:
                    dve.wait_ge(S["x_loaded"], 64)
                V.tensor_tensor(x_r[0:n, t, :], x_r[0:n, t, :], prod_o[0:n, :], ALU.add).then_inc(S["x1_ready"], 1)
                dve.wait_ge(S["norm_sqrt"], t + 1)
                step(V.reciprocal(rstd[0:n, t:t + 1], ssq[0:n, t:t + 1]))
                if t >= 2:
                    dve.wait_ge(h2_out[t % 2], 16 * (t // 2))
                    dve.wait_ge(S["h2_psum"], t - 1)
                r = h_row[t % 2]
                step(V.scalar_tensor_tensor(r[0:n, :], x_r[0:n, t, :], rstd[0:n, t:t + 1], sc[0:n, :], ALU.mult, ALU.mult))
                V.tensor_tensor(r[0:n, :], r[0:n, :], sh[0:n, :], ALU.add).then_inc(S["h2_ready"], 1)

            def own_heads(b):
                dve.wait_ge(S["pvs_done"], b + 1)
                if b >= 2:
                    dve.wait_ge(S["ot2_done"], b - 1)
                V.tensor_tensor(o_m[b % 2][:, :], bank[b % 2][:, :], head_mask[:, :], ALU.mult).then_inc(S["om_ready"], 1)

            def logits(t):
                n = P if t < NT else B
                dve.wait_ge(S["lg_done"], t + 1)
                V.tensor_tensor(lg[0:n, t, :], bank[3][0:n, t * 36:(t + 1) * 36], b_r[0:n, :], ALU.add)\
                    .then_inc(S["lg_taken"], 1)

            dve.wait_ge(S["wr_loaded"], 64)
            step(V.memset(lg[:, :, :], 0.0))
            for t in range(NT):
                residual(t)
                if t == 0:
                    dve.wait_ge(S["exp_ready"], B)
                    step(V.reduce_sum(p_sum[:, :, :], scores[:, :, :, :].rearrange("p b i h -> p b h i"), AX.X))
                    V.tensor_tensor(p_sum[:, :, :], p_sum[:, :, :], p_new[:, :, :], ALU.add).then_inc(S["softmax_in"], 1)
                own_heads(2 * t)
                logits(t)
                own_heads(2 * t + 1)
            dve.wait_ge(S["samp_norm_psum"], 1)
            dve.wait_ge(S["ot2_done"], B)
            c3 = lambda lo: bank[2][:, lo:lo + C4 * B].rearrange("p (c b) -> p c b", c=C4)
            step(V.reciprocal(o_r[:, :, :], c3(64)))
            V.tensor_tensor(o_t[:, :, :], c3(0), o_r[:, :, :], ALU.mult).then_inc(S["samp_norm_dve"], 1)
            dve.wait_ge(S["samp_norm_act"], 2)
            step(V.reciprocal(o_r[:, :, :], o_r[:, :, :]))
            step(V.tensor_tensor(o_t[:, :, :], o_t[:, :, :], o_r[:, :, :], ALU.mult))
            V.tensor_tensor(mix_a[:, :, T:T + B], o_t[:, :, :],
                            spread(vecs[:, 0:C4].rearrange("p (c o) -> p c o", o=1), [P, C4, B]), ALU.mult)\
                .then_inc(S["samp_norm_dve"], 1)
            residual(NT)
            logits(NT)

            dve.wait_ge(S["lg_taken"], 5)
            dve.wait_ge(h2_out[0], 48)
            dve.wait_ge(h2_out[1], 32)
            dve.wait_ge(S["h2_psum"], 5)
            one = lambda i: st[:, i, :]
            wide = lambda i, n: spread(st[:, i, :].rearrange("p (t o) -> p t o", o=1), [P, 5, n])
            gl = lg[:, :, 0:NG]
            step(V.reduce_max(one(0), gl, AX.X))
            V.tensor_tensor(ge[:, :, :], gl, wide(0, NG), ALU.subtract).then_inc(S["route_in"], 1)

            def first_of(out, values, top_value, n):
                step(V.reduce_max(one(top_value), values, AX.X))
                step(V.tensor_tensor(out, values, wide(top_value, n), ALU.is_equal))
                d = spread(desc[:, 8 - n:8].rearrange("p (o n) -> p o n", o=1), [P, 5, n])
                step(V.tensor_tensor(out, out, d, ALU.mult))
                step(V.reduce_max(one(11), out, AX.X))
                step(V.tensor_tensor(out, out, wide(11, n), ALU.is_equal))

            dve.wait_ge(S["route_consts"], 1)
            first_of(g_oh[:, :, :], gl, 1, NG)
            wide_g = spread(g_oh[:, :, :].rearrange("p t (g o) -> p t g o", o=1), [P, 5, NG, EPG])
            step(V.tensor_tensor(els[:, :, :, :], lg[:, :, NG:NG + NE].rearrange("p t (g e) -> p t g e", g=NG), wide_g, ALU.mult))
            step(V.reduce_sum(el[:, :, :], els[:, :, :, :].rearrange("p t g e -> p t e g"), AX.X))
            step(V.reduce_max(one(2), el[:, :, :], AX.X))
            V.tensor_tensor(el[:, :, :], el[:, :, :], wide(2, EPG), ALU.subtract).then_inc(S["route_in"], 1)
            dve.wait_ge(S["route_exp"], 1)
            step(V.reduce_sum(one(3), ge[:, :, :], AX.X))
            step(V.reciprocal(one(3), one(3)))
            dve.wait_ge(S["route_exp"], 2)
            first_of(e_c[:, 0, :, :], el[:, :, :], 4, EPG)
            step(V.tensor_tensor(e_t[:, :, :], el[:, :, :], e_c[:, 0, :, :], ALU.mult))
            step(V.tensor_tensor(el[:, :, :], el[:, :, :], e_t[:, :, :], ALU.subtract))
            step(V.tensor_tensor(el[:, :, :], el[:, :, :], e_c[:, 0, :, :], ALU.subtract))
            first_of(e_c[:, 1, :, :], el[:, :, :], 5, EPG)
            step(V.tensor_tensor(one(6), one(4), one(5), ALU.add))
            step(V.reciprocal(one(6), one(6)))
            step(V.tensor_tensor(one(6), one(6), one(3), ALU.mult))
            for c in range(2):
                step(V.tensor_tensor(one(7 + c), one(4 + c), one(6), ALU.mult))
                step(V.tensor_tensor(oh[:, c, :, :].rearrange("p t (g e) -> p t g e", g=NG), wide_g,
                                     spread(e_c[:, c, :, :].rearrange("p t (o e) -> p t o e", o=1), [P, 5, NG, EPG]),
                                     ALU.mult))
            V.tensor_tensor(both[:, :, :], oh[:, 0, :, :], oh[:, 1, :, :], ALU.add).then_inc(S["route_in"], 1)
            for c in range(2):
                step(V.tensor_scalar(one(9), tok2[:, :], 2.0, 2.0 * c - FAR, ALU.mult, ALU.add))
                for k, s in ((1, 9), (2, 7 + c)):
                    V.tensor_tensor(vals[:, c, :, k * NE:(k + 1) * NE], oh[:, c, :, :], wide(s, NE), ALU.mult)
                step(V.tensor_tensor(vals[:, c, :, 0:NE], oh[:, c, :, :],
                                     spread(tok2[:, :].rearrange("p (t o) -> p t o", o=1), [P, 5, NE]), ALU.mult))
            dve.wait_ge(S["rank_done"], 1)
            step(V.tensor_copy(rank_e[:, :, :], bank[0][:, 0:5 * NE].rearrange("p (t e) -> p t e", t=5)))
            step(V.reduce_max(cnt_max[:, 0:1], bank[1][:, 0:NE], AX.X))
            V.tensor_copy(max_count[0:1, 0:1], cnt_max[0:1, 0:1]).then_inc(S["count_ready"], 1)
            for c in range(2):
                step(V.tensor_tensor(els[:, :, :, :].rearrange("p t g e -> p t (g e)"), rank_e[:, :, :], oh[:, c, :, :], ALU.mult))
                step(V.reduce_sum(rank[:, c, :], els[:, :, :, :].rearrange("p t g e -> p t (g e)"), AX.X))

            def slots():
                for c in range(2):
                    last = V.tensor_tensor(slot_is[:, c, :, :],
                                           spread(slot_no[:, :].rearrange("p (o n) -> p o n", o=1), [P, 5, P]),
                                           spread(rank[:, c, :].rearrange("p (t o) -> p t o", o=1), [P, 5, P]), ALU.is_equal)
                return last

            def read_tables():
                V.tensor_scalar(g_idx[:, :], bank[2][:, 0:NE], half_no[:, 0:1], None, ALU.add)
                V.tensor_scalar(s_idx[:, :], bank[2][:, NE:2 * NE], far_half[:, 0:1], None, ALU.add)
                return V.tensor_copy(tabs[:, :], bank[2][:, 2 * NE:3 * NE])

            slots().then_inc(S["vals_ready"], 1)
            dve.wait_ge(S["tabs_done"], 1)
            read_tables().then_inc(S["tabs_ready"], 1)
            V.memset(cnt[:, :], 0.0).then_inc(S["y_ready"], 2)

            def hidden(xs):
                return V.tensor_tensor(hid[xs][:, :], sig[xs][:, :], bank[2 + xs][SLOTS:2 * SLOTS, 0:DE], ALU.mult)

            def hidden_out(xs):
                return V.tensor_copy(hid_t[xs][:, :, :], bank[2 + xs][:, 256:256 + 2 * SLOTS].rearrange("p (k n) -> p k n", k=2))

            def weighted(xs, e):
                return V.tensor_scalar(y_e[xs][:, :], bank[4 + xs][:, :], tabs[:, bass.ds(e, 1)], None, ALU.mult)

            def four_experts(g):
                for s in range(4):
                    xs, e = s % 2, 4 * g + s
                    dve.wait_ge(S["sig_ready"], e + 1)
                    hidden(xs).then_inc(S["hid_ready"], 1)
                    dve.wait_ge(S["hidt_done"], e + 1)
                    hidden_out(xs).then_inc(S["hidt_ready"], 1)
                    dve.wait_ge(S["y_done"], e + 1)
                    if not isinstance(e, int) or e >= 2:
                        dve.wait_ge(y_stored[xs], (2 * g + s // 2) * 16)
                    weighted(xs, e).then_inc(S["y_ready"], 1)

            four_experts(0)
            with dve.Fori(1, NE // 4) as g:
                four_experts(g)
            count = dve.value_load(max_count[0:1, 0:1], min_val=0, max_val=2 * (T + B))
            with dve.If(count > cap):
                with dve.Fori(1, PASSES) as p:
                    dve.wait_ge(y_stored[0], (p - 1) * NE * 16 + STORED)
                    dve.wait_ge(y_stored[1], STORED)
                    V.tensor_scalar(slot_no[:, :], slot_no[:, :], float(SLOTS), None, ALU.add).then_inc(S["ov_slots"], 1)
                    dve.wait_ge(S["ov_slots"], p)
                    slots().then_inc(S["vals_ready"], 1)
                    dve.wait_ge(S["tabs_done"], p + 1)
                    read_tables().then_inc(S["tabs_ready"], 1)
                    dve.wait_ge(S["tabs_done"], 2)
                    dve.wait_ge(S["tabs_ready"], p + 1)
                    with dve.Fori(0, NE) as e:
                        n = p * NE + e
                        dve.wait_ge(S["sig_ready"], n + 1)
                        hidden(0).then_inc(S["hid_ready"], 1)
                        dve.wait_ge(S["hidt_done"], n + 1)
                        hidden_out(0).then_inc(S["hidt_ready"], 1)
                        dve.wait_ge(S["y_done"], n + 1)
                        dve.wait_ge(y_stored[0], (n - NE) * 16 + STORED)
                        weighted(0, e).then_inc(S["y_ready"], 1)

            dve.wait_ge(S["g_loaded"], 48)
            for j in (4, 5):
                dve.wait_ge(S["expand_done"], j + 11)
                lo = slice((j % 2) * SECS, (j % 2 + 1) * SECS)
                V.scalar_tensor_tensor(scf_s[0:B, lo], bank[j % 2][0:B, :], 1.0, gf_b[0:B, lo], ALU.add, ALU.mult)
                step(V.scalar_tensor_tensor(scf_p[:, lo], bank[2 + j % 2][:, :], 1.0, gf_b[:, lo], ALU.add, ALU.mult))
            dve.wait_ge(S["mod3_ready"], 4)
            for i, t in enumerate((0, 1, 2, 3, NT)):
                n = P if t < NT else B
                ga, sc, sh = (ga2_p, scf_p, shf_p) if t < NT else (ga2_s, scf_s, shf_s)
                dve.wait_ge(yg_loaded[i], 16)
                y = y_g[i]
                step(V.tensor_tensor(y[0:n, 0, :], y[0:n, 0, :], y[0:n, 1, :], ALU.add))
                step(V.tensor_tensor(y[0:n, 0, :], y[0:n, 0, :], ga[0:n, :], ALU.mult))
                V.tensor_tensor(x_r[0:n, t, :], x_r[0:n, t, :], y[0:n, 0, :], ALU.add).then_inc(S["x1_ready"], 1)
                dve.wait_ge(S["norm_sqrt"], i + 6)
                step(V.reciprocal(rstd[0:n, t:t + 1], ssq[0:n, t:t + 1]))
                if i >= 2:
                    dve.wait_ge(y_out[i % 2], 16 * (i // 2))
                r = h_row[i % 2]
                step(V.scalar_tensor_tensor(r[0:n, :], x_r[0:n, t, :], rstd[0:n, t:t + 1], sc[0:n, :], ALU.mult, ALU.mult))
                V.tensor_tensor(r[0:n, :], r[0:n, :], sh[0:n, :], ALU.add).then_inc(S["fin_ready"], 1)

        @block.gpsimd
        def _(pool):
            G = nc.gpsimd
            steps = [0]

            def step(ins):
                steps[0] += 1
                ins.then_inc(S["pool_step"], 1)
                pool.wait_ge(S["pool_step"], steps[0])

            G.iota(lane[:, :], [[0, 1]], base=0, channel_multiplier=1).then_inc(S["consts_ready"], 1)
            G.memset(ones[:, :], 1.0)
            G.memset(eps[:, :], EPS)
            G.memset(ssq[:, :], 1.0)
            G.memset(h_t[:, :, T + B:HP], 0.0).then_inc(S["consts_ready"], 1)
            G.memset(ident[:, :], 0.0)
            G.memset(block64[:, :], 0.0)
            G.memset(sel[:, :, :], 0.0)
            G.memset(head_mask[:, :], 0.0)
            step(G.memset(causal[:, :], 0.0))
            G.memset(block64[0:64, 0:64], 1.0)
            step(G.memset(block64[64:128, 64:128], 1.0))
            G.affine_select(out=ident[:, :], in_=ident[:, :], compare_op=ALU.not_equal, fill=1.0, base=0,
                            pattern=[[-1, P]], channel_multiplier=1)
            G.affine_select(out=causal[:, :], in_=causal[:, :], compare_op=ALU.is_ge, fill=NEG, base=0,
                            pattern=[[-1, P]], channel_multiplier=1)
            G.affine_select(out=later[:, :], in_=ones[:, :], compare_op=ALU.is_gt, fill=0.0, base=0,
                            pattern=[[-1, P]], channel_multiplier=1)
            G.affine_select(out=earlier[:, :], in_=ones[:, :], compare_op=ALU.is_gt, fill=0.0, base=0,
                            pattern=[[1, P]], channel_multiplier=-1)
            for j in range(4):
                G.affine_select(out=sel[:, :, :], in_=sel[:, :, :], compare_op=ALU.not_equal, fill=1.0, base=-32 * j,
                                pattern=[[-1, B + 1], [0, P]], channel_multiplier=1)
                hm = head_mask[:, :].rearrange("p (h d) -> p h d", h=H)
                step(G.affine_select(out=hm, in_=hm, compare_op=ALU.not_equal, fill=1.0, base=-32 * j,
                                     pattern=[[-1, H], [0, HD]], channel_multiplier=1))
            G.memset(conv_in[:, :, 0:2], 0.0).then_inc(S["consts_ready"], 1)
            pool.wait_ge(S["consts_ready"], 3)
            G.memset(small_one[:, :], 1.0).then_inc(S["consts_ready"], 1)

            pool.wait_ge(S["setup_ready"], 3)
            f_view = decay[:, :, :, :].rearrange("p b i h -> p b (i h)")
            for b in range(B):
                pool.indirect_dma_start(f_view[:, b, :], None, f_rows, bass.IndirectOffsetOnAxis(f_index[:, b:b + 1], 0))\
                    .then_inc(S["f_loaded"], 16)

            def cache_chunk(g):
                n = g % NKV
                if g >= RING:
                    pool.wait_ge(*((S["k_used"], g - RING + 1) if g - RING < NKV else (S["v_used"], g - RING - NKV + 1)))
                pool.indirect_dma_start(kv_flat[:, g % RING, :], None, k_rows if g < NKV else v_rows,
                                        bass.IndirectOffsetOnAxis(kv_index[:, n:n + 1], 0))\
                    .then_inc(kv_loaded[g % RING], 16)

            for n in range(NKV):
                b, s = divmod(n, NCH)
                if s == 0:
                    if b == 0:
                        pool.wait_ge(S["h_row_ready"], 5)
                        pool.wait_ge(S["q_stored"], 16)
                    if b >= 2:
                        pool.wait_ge(S["k_used"], NCH * (b - 1))
                    pool.dma_start(q_b[:, b % 2, :], q_rows_dram[b:b + 1, :].to_broadcast([P, HW]))\
                        .then_inc(qb_loaded[b % 2], 16)
                cache_chunk(n)
                if 8 <= n < 13:
                    if n == 8:
                        pool.wait_ge(S["f_loaded"], 16 * B)
                    d = 1 << (n - 8)
                    if n > 8:
                        pool.wait_ge(S["decay_sum"], n - 8)
                    G.tensor_tensor(decay[:, :, 0:PPP - d, :], decay[:, :, 0:PPP - d, :], decay[:, :, d:PPP, :], ALU.add)\
                        .then_inc(S["decay_sum"], 1)
                if n == NEW_AT + RING - 1:
                    pool.wait_ge(S["select_in"], 1)
                    G.affine_select(out=news[0:B, :, :], in_=news[0:B, :, :], compare_op=ALU.is_equal, fill=NEG, base=0,
                                    pattern=[[-1, B], [0, H]], channel_multiplier=1).then_inc(S["select_done"], 1)
                if n == DIAG_AT + RING - 1:
                    pool.wait_ge(S["select_in"], 2)
                    G.affine_select(out=lf_diag[:, :, :], in_=lf_diag[:, :, :], compare_op=ALU.is_equal, fill=0.0, base=0,
                                    pattern=[[-1, B], [0, H]], channel_multiplier=1).then_inc(S["select_done"], 1)
            pool.wait_ge(S["tail_evac"], 1)
            wide_tail = tail[:, :, :].rearrange("p b (o h) -> p b o h", o=1)
            step(G.tensor_tensor(decay[:, :, 0:PPP - 1, :], decay[:, :, 1:PPP, :],
                                 wide_tail.to_broadcast([P, B, PPP - 1, H]), ALU.add))
            G.tensor_copy(decay[:, :, PPP - 1, :], tail[:, :, :]).then_inc(S["select_done"], 1)
            for g in range(NKV, NKV + RING):
                cache_chunk(g)
            pool.wait_ge(S["softmax_in"], 1)
            G.partition_all_reduce(top_all[:, :, :].rearrange("p b h -> p (b h)"), top[:, :, :].rearrange("p b h -> p (b h)"),
                                   P, RED.max).then_inc(S["top_ready"], 1)
            for g in range(NKV + RING, 2 * NKV):
                cache_chunk(g)

            pool.wait_ge(S["h2_psum"], 5)
            pool.wait_ge(S["lg_taken"], 5)
            pool.wait_ge(h2_out[0], 48)
            pool.wait_ge(h2_out[1], 32)
            G.iota(slot_no[:, :], [[0, 2], [1, SLOTS]], base=0, channel_multiplier=0, allow_small_or_imprecise_dtypes=True)
            G.iota(tok2[:, :], [[2 * P, 5]], base=0, channel_multiplier=2, allow_small_or_imprecise_dtypes=True)
            G.iota(desc[:, :], [[-1, EPG]], base=EPG, channel_multiplier=0, allow_small_or_imprecise_dtypes=True)
            step(G.memset(mark[:, :], 0.0))
            G.memset(half_no[0:SLOTS, :], 0.0)
            step(G.memset(half_no[SLOTS:P, :], 1.0))
            G.memset(far_half[0:SLOTS, :], FAR)
            G.memset(far_half[SLOTS:P, :], FAR + 1.0).then_inc(S["route_consts"], 1)
            pool.wait_ge(S["route_consts"], 1)

            def gather(xs, col):
                return pool.indirect_dma_start(x_e[xs][:, :], None, h2_dram, bass.IndirectOffsetOnAxis(col, 0))

            def scatter(xs, col):
                return pool.indirect_dma_start(y_dram, bass.IndirectOffsetOnAxis(col, 0), y_e[xs][:, :], None,
                                               bounds_check=4 * (T + B) - 1, oob_is_err=False)

            def columns(e):
                G.tensor_copy(e_cols[:, 0:1], g_idx[:, bass.ds(e, 1)])
                return G.tensor_copy(e_cols[:, 1:2], s_idx[:, bass.ds(e, 1)])

            def hold(signal, value, held):
                pool.wait_ge(S["ov_held"], held)
                pool.wait_ge(signal, value)
                G.tensor_tensor(mark[:, :], mark[:, :], mark[:, :], ALU.add).then_inc(S["ov_held"], 1)

            pool.wait_ge(S["tabs_ready"], 1)
            pool.wait_ge(h2_out[0], 48)
            pool.wait_ge(h2_out[1], 32)
            for e in range(NE):
                xs = e % 2
                if e >= 2:
                    pool.wait_ge(S["xe_done"], e - 1)
                gather(xs, g_idx[:, e:e + 1]).then_inc(xe_loaded[xs], 16)
                if e >= 2:
                    pool.wait_ge(S["y_ready"], e + 1)
                    scatter(xs, s_idx[:, e - 2:e - 1]).then_inc(y_stored[xs], 16)
            for e in (NE - 2, NE - 1):
                pool.wait_ge(S["y_ready"], e + 3)
                scatter(e % 2, s_idx[:, e:e + 1]).then_inc(y_stored[e % 2], 16)
            count = pool.value_load(max_count[0:1, 0:1], min_val=0, max_val=2 * (T + B))
            with pool.If(count > cap):
                pool.sem_inc(S["ov_held"], 1)
                with pool.Fori(1, PASSES) as p:
                    with pool.Fori(0, NE) as e:
                        n = p * NE + e
                        pool.wait_ge(S["tabs_ready"], p + 1)
                        pool.wait_ge(y_stored[0], (n - NE) * 16 + STORED)
                        columns(e).then_inc(S["ov_cols"], 1)
                        hold(S["ov_cols"], n - NE + 1, 2 * (n - NE) + 1)
                        gather(0, e_cols[:, 0:1]).then_inc(xe_loaded[0], 16)
                        hold(S["y_ready"], n + 3, 2 * (n - NE) + 2)
                        scatter(0, e_cols[:, 1:2]).then_inc(y_stored[0], 16)
                pool.wait_ge(y_stored[0], (PASSES - 1) * NE * 16 + STORED)
            pool.wait_ge(y_stored[0], STORED)
            pool.wait_ge(y_stored[1], STORED)
            pool.sem_inc(S["y_all"], 1)

        @block.sync
        def _(sp):
            def unit(u):
                if u >= 3:
                    f = u - 3
                    if f < 8:
                        sp.wait_ge(S["unit_used"], f + 1)
                    elif f < 20:
                        s, half = divmod(f - 8, 2)
                        if half == 0:
                            sp.wait_ge(S["unit_used"], 8 + s + 1)
                        else:
                            sp.wait_ge(S["acc_done"], 4 * (s + 1))
                    else:
                        sp.wait_ge(S["unit_used"], 14 + f - 20 + 1)
                half = u % 2
                if u < 8:
                    v, lo = chunk_sec[u // 2]
                elif u < 20:
                    v, lo = w_in_v, sec_col[(u - 8) // 2]
                else:
                    v, lo = chunk_sec[4 + (u - 20) // 2]
                sp.dma_start(w_unit[:, u % 3], v[:, 4 * half:4 * half + 4, lo:lo + SECS]).then_inc(unit_loaded[u % 3], 16)

            row = lambda a: a.rearrange("(o n) -> o n", o=1)
            sp.dma_start(c_row[0:B, :], c_sample).then_inc(S["c_loaded"], 16)
            sp.dma_start(c_row[B:B + 1, :], c_prompt).then_inc(S["c_loaded"], 16)
            sp.dma_start(pt_int[:, :], page_table).then_inc(S["pt_loaded"], 16)
            sp.dma_start(b_row_a[:, :], b_ada[0:1, 0:4 * SECS]).then_inc(S["ba_loaded"], 16)
            unit(0)
            unit(1)
            sp.dma_start(x_a[0:B, NT, :], x_sample.rearrange("b t d -> (b t) d")).then_inc(S["x_loaded"], 16)
            sp.dma_start(x_a[:, 0:NT, :], x_prompt.rearrange("b (t p) d -> (b p) t d", p=P)).then_inc(S["x_loaded"], 16)
            unit(2)
            sp.dma_start(g1_b[:, :], g_norm1.to_broadcast([P, D])).then_inc(S["g_loaded"], 16)
            sp.dma_start(vec_rows[0:4, :], g_attn_out.rearrange("l (c a) d -> (l c) (a d)", a=2)).then_inc(S["vec_loaded"], 16)
            sp.dma_start(vec_rows[4:8, :], g_conv_out.rearrange("l (c a) d -> (l c) (a d)", a=2)).then_inc(S["vec_loaded"], 16)
            sp.dma_start(vec_rows[8:20, :], conv_w.rearrange("l j (c p) -> (l j c) p", p=P)).then_inc(S["vec_loaded"], 16)
            sp.dma_start(b_f[:, :], b_forget.rearrange("l h -> h l")).then_inc(S["vec_loaded"], 16)
            sp.dma_start(conv_sample[0, :, 0, :], state_conv[0, :, 1, :]).then_inc(S["state_out"], 16)
            for u in range(3, 8):
                unit(u)
            for u in range(8, 20):
                unit(u)
                if u == 11:
                    sp.wait_ge(S["h_row_ready"], 5)
                    sp.dma_start(w_f[:, :, :], w_in_v[:, :, f_col:f_col + H]).then_inc(S["wf_loaded"], 16)
                    sp.dma_start(state_rows[:, :], state_conv.rearrange("l b j c -> (l b j) c")).then_inc(S["st_loaded"], 16)
            for n in range(12):
                for half in range(2):
                    unit(20 + 2 * n + half)
                if n >= 2:
                    sp.wait_ge(S["ada_done"], 4 + n - 1)
                else:
                    sp.wait_ge(S["acc_done"], 24)
                    sp.wait_ge(S["samp_done"], 6)
                src = b_ada[0:1, (4 + n) * SECS:(5 + n) * SECS] if n < 8 else row(b_ada_final[(n - 8) * SECS:(n - 7) * SECS])
                sp.dma_start(b_row[:, (n % 2) * SECS:(n % 2 + 1) * SECS], src).then_inc(b_loaded[n % 2], 16)
            sp.wait_ge(S["pv_done"], NT * H)
            sp.dma_start(wo[:, :, :], w_out_v).then_inc(S["wo_loaded"], 16)
            sp.wait_ge(S["ada_done"], 16)
            for lo, n, src in ((0, NG, w_router_group), (NG, NE, w_router_expert)):
                sp.dma_start(w_r[:, :, lo:lo + n], src.rearrange("l (p k) n -> (l p) k n", k=KD)).then_inc(S["wr_loaded"], 16)
            for lo, n, src in ((0, NG, b_router_group), (NG, NE, b_router_expert)):
                sp.dma_start(b_r[:, lo:lo + n], src.to_broadcast([P, n])).then_inc(S["wr_loaded"], 16)
            sp.wait_ge(S["ot_done"], NT)
            sp.dma_start(g_b[:, :], g_norm2.to_broadcast([P, D])).then_inc(S["g_loaded"], 16)
            sp.wait_ge(S["k_used"], NKV)
            sp.dma_start(x_r[0:B, NT, :], x_sample.rearrange("b t d -> (b t) d")).then_inc(S["x_loaded"], 16)
            sp.dma_start(x_r[:, 0:NT, :], x_prompt.rearrange("b (t p) d -> (b p) t d", p=P)).then_inc(S["x_loaded"], 16)

            wg = w_expert_gate.rearrange("l e (a p c) f -> (l e) p a (c f)", a=2, c=4)
            wu = w_expert_up.rearrange("l e (a p c) f -> (l e) p a (c f)", a=2, c=4)
            wd = w_expert_down.rearrange("l e (p k) n -> (l e) p (k n)", k=2)

            def gate_up(e, s):
                for o, src in ((0, wg), (2048, wu)):
                    sp.dma_start(exp_w[s][:, o:o + 2048].rearrange("p (a n) -> p a n", a=2), pick(src, e))\
                        .then_inc(gate_loaded[s], 16)

            def down(e, s):
                sp.dma_start(exp_w[s][:, 4096:6144], pick(wd, e)).then_inc(down_loaded[s], 16)

            def pick(src, e):
                if isinstance(e, int):
                    return src[e]
                v = src[bass.ds(e, 1)]
                return v.rearrange("o p a n -> (o p) a n") if len(v.shape) == 4 else v.rearrange("o p n -> (o p) n")

            free = {1: (S["v_used"], NKV), 2: (S["wo_done"], 10), 3: (S["lg_done"], 5), 0: (S["h2_ready"], 5)}
            for s in (1, 2, 3, 0):
                sp.wait_ge(*free[s])
                if s == 3:
                    sp.wait_ge(S["x1_ready"], 5)
                gate_up(s, s)
                down(s, s)
            sp.wait_ge(S["expand_done"], 10)
            with sp.Fori(1, NE // 4) as g:
                for s in range(4):
                    e = 4 * g + s
                    sp.wait_ge(S["gu_done"], e - 3)
                    gate_up(e, s)
                    sp.wait_ge(S["y_done"], e - 3)
                    down(e, s)
            sp.wait_ge(S["count_ready"], 1)
            count = sp.value_load(max_count[0:1, 0:1], min_val=0, max_val=2 * (T + B))
            with sp.If(count > cap):
                with sp.Fori(1, PASSES) as p:
                    with sp.Fori(0, NE) as e:
                        sp.wait_ge(S["y_done"], p * NE + e)
                        gate_up(e, 0)
                        down(e, 0)

            sp.dma_start(gf_b[:, :], row(g_final).to_broadcast([P, D])).then_inc(S["g_loaded"], 16)
            sp.wait_ge(S["y_all"], 1)
            sp.wait_ge(S["y_done"], NE)
            tok_rows = lambda lo, n: y_dram[4 * lo:4 * (lo + n), :].rearrange("(p a) d -> p (a d)", a=4)
            for i, t in enumerate((0, 1, 2, 3, NT)):
                n = P if t < NT else B
                sp.dma_start(y_g[i][0:n, :, :].rearrange("p a d -> p (a d)"), tok_rows(t * P, n)).then_inc(yg_loaded[i], 16)
            for i, t in enumerate((0, 1, 2, 3, NT)):
                n = P if t < NT else B
                dst = y_prompt[0, t * P:(t + 1) * P, :] if t < NT else y_sample.rearrange("b t d -> (b t) d")
                sp.wait_ge(S["fin_ready"], i + 1)
                sp.dma_start(dst, h_row[i % 2][0:n, :]).then_inc(y_out[i % 2], 16)
            sp.wait_ge(y_out[0], 48)
            sp.wait_ge(y_out[1], 32)
            sp.wait_ge(S["outs"], 16 * 7)
            sp.wait_ge(S["state_out"], 16)
            sp.wait_ge(krow_out[0], 32)
            sp.wait_ge(krow_out[1], 32)


_INS = ["x_prompt", "x_sample", "c_prompt", "c_sample", "cache_k", "cache_v", "cache_logf", "state_conv",
        "page_table", "w_ada", "b_ada", "g_norm1", "w_in", "b_forget", "conv_w", "g_attn_out", "g_conv_out",
        "w_out", "g_norm2", "w_router_group", "b_router_group", "w_router_expert", "b_router_expert",
        "w_expert_gate", "w_expert_up", "w_expert_down", "w_ada_final", "b_ada_final", "g_final"]
_OUTS = [(1, T, D), (B, 1, D), (1, 1, T, H, HD), (1, 1, T, H, HD), (1, 1, T, H), (1, 1, 2, HW),
         (1, B, 1, H, HD), (1, B, 1, H, HD), (1, B, 1, H), (1, B, 2, HW)]


def kernel(**inputs):
    import numpy as _np
    import concourse.bacc as _bacc
    from concourse import mybir as _mybir
    from concourse.bass_utils import run_bass_kernel_spmd as _run

    nc = _bacc.Bacc("TRN2", target_bir_lowering=False, num_devices=1)
    arrays, args = {}, []
    for name in _INS:
        a = _np.ascontiguousarray(inputs[name])
        arrays[f"in_{name}_dram"] = a
        args.append(nc.dram_tensor(f"in_{name}_dram", a.shape, _mybir.dt.from_np(a.dtype), kind="ExternalInput").ap())
    for i, shape in enumerate(_OUTS):
        args.append(nc.dram_tensor(f"out_{i}_dram", shape, F32, kind="ExternalOutput").ap())
    build(nc, *args)
    r = _run(nc, [arrays], core_ids=[0])
    return tuple(r.results[0][f"out_{i}_dram"] for i in range(len(_OUTS)))
```

```python
from contextlib import ExitStack

import concourse.bass as bass
from concourse import mybir

F32 = mybir.dt.float32
I32 = mybir.dt.int32
ALU = mybir.AluOpType
ACT = mybir.ActivationFunctionType
AX = mybir.AxisListType
RED = bass.bass_isa.ReduceOp

P = 128
D = 1024
KD = D // P
T = 512
NT = T // P
B = 8
H, HD = 8, 64
HW = H * HD
C4 = HW // P
NPG, PG = 32, 128
PPP = PG * NPG // P
CH = 4
NCH = PPP // CH
NKV = B * NCH
RING = 4
SCALE = HD ** -0.5
EPS = 1e-6
NEG = -1.0e30
NG, EPG = 4, 8
NE = NG * EPG
DE = 256
SLOTS = 64
PASSES = -(-(T + B) // SLOTS)
FAR = 4096.0
HP = T + B + 24
SECS = 512


def build(nc, x_prompt, x_sample, c_prompt, c_sample, cache_k, cache_v, cache_logf, state_conv,
          page_table, w_ada, b_ada, g_norm1, w_in, b_forget, conv_w, g_attn_out, g_conv_out,
          w_out, g_norm2, w_router_group, b_router_group, w_router_expert, b_router_expert,
          w_expert_gate, w_expert_up, w_expert_down, w_ada_final, b_ada_final, g_final,
          y_prompt, y_sample, k_prompt, v_prompt, logf_prompt, conv_prompt, k_sample, v_sample,
          logf_sample, conv_sample, cap=SLOTS):
    ctx = ExitStack()
    with ctx:
        def sb(name, shape, dt=F32):
            return ctx.enter_context(nc.sbuf_tensor(name, shape, dt))

        def sem(name):
            return ctx.enter_context(nc.semaphore(name))

        q_rows_dram = nc.dram_tensor("q_rows_scratch", [B, HW], F32, kind="Internal").ap()
        h2_dram = nc.dram_tensor("h2_scratch", [2 * (T + B), D // 2], F32, kind="Internal").ap()
        y_dram = nc.dram_tensor("expert_rows_scratch", [4 * (T + B), D // 2], F32, kind="Internal").ap()

        n_pool = cache_k.shape[1]
        k_rows = cache_k.rearrange("l n (g r) h d -> (l n g) (r h d)", r=CH)
        v_rows = cache_v.rearrange("l n (g r) h d -> (l n g) (r h d)", r=CH)
        f_rows = cache_logf.rearrange("l n (g r) h -> (l n g) (r h)", r=PPP)
        w_ada_v = w_ada.rearrange("l (k p) n -> (l p) k n", p=P)
        w_fin_v = w_ada_final.rearrange("(k p) n -> p k n", p=P)
        w_in_v = w_in.rearrange("l (k p) n -> (l p) k n", p=P)
        w_out_v = w_out.rearrange("l (k p) n -> (l p) k n", p=P)
        f_col = 3 * HW
        sec_col = [0, HW, 2 * HW, f_col + H, f_col + H + 2 * HW, f_col + H + HW]

        R_x = sb("R_x", [P, 5120])
        R_part = sb("R_part", [P, 6144])
        R_h = sb("R_h", [P, KD * HP])
        R_cm = sb("R_cm", [P, 8264])
        R_kv = sb("R_kv", [P, RING * CH * HW])
        R_w = sb("R_w", [P, 6144])
        R_q = sb("R_q", [P, 8192])
        R_t = sb("R_t", [P, 3584])

        def view(region, lo, dims, parts=P):
            n = 1
            for d in dims:
                n *= d
            v = region[0:parts, lo:lo + n]
            if len(dims) == 1:
                return v
            names = "abcd"[:len(dims)]
            return v.rearrange(f"p ({' '.join(names)}) -> p {' '.join(names)}",
                               **{c: d for c, d in zip(names[1:], dims[1:])})

        ident = sb("ident", [P, P])
        block64 = sb("block64", [P, P])
        later = sb("later", [P, P])
        earlier = sb("earlier", [P, P])
        ones = sb("ones", [P, P])
        causal = sb("causal", [P, P])
        sel = sb("sel", [P, B + 1, P])
        head_mask = sb("head_mask", [P, HW])
        vecs = sb("vecs", [P, 20])
        kv_index = sb("kv_index", [P, NKV], I32)
        f_index = sb("f_index", [P, B], I32)
        v_new = sb("v_new", [B, HW])
        eps = sb("eps", [P, 1])
        ssq = sb("ssq", [P, 5])
        rstd = sb("rstd", [P, 5])
        b_f = sb("b_f", [H, 1])
        neg_max = sb("neg_max", [P, 2])
        row_sum = sb("row_sum", [P, 2 * H])
        head_ssq = sb("head_ssq", [P, H])
        quarter = sb("quarter", [P, 10])
        max_count = sb("max_count", [1, 1], I32)
        small_one = sb("small_one", [P, 1])
        e_cols = sb("e_cols", [P, 2], I32)

        sh1_p, sc1_p, sh1_s, sc1_s, g1_b = (view(R_q, i * 1024, [1024]) for i in range(5))
        part_a = view(R_q, 5120, [4, 512])
        x_a = view(R_x, 0, [5, D])
        c_row = view(R_part, 0, [D], B + 1)
        c_t = view(R_q, 7680, [KD, 32])
        b_row_a = view(R_part, 1280, [2048], 1)
        vec_rows = view(R_part, 3328, [P], 20)
        pt_int = view(R_part, 3456, [NPG], B).bitcast(I32)
        pt_exp = view(R_part, 3488, [NPG, 4], B)
        lane = view(R_part, 3616, [1]).bitcast(I32)
        h_row = [view(R_t, i * 1024, [D]) for i in range(2)]
        junk = view(R_t, 2048, [D])
        h_t = view(R_h, 0, [KD, HP])
        q_t, k_t, v_r = (view(R_q, i * 2048, [C4, T]) for i in range(3))
        s_part = view(R_q, 6144, [3, HW])
        qk_new = view(R_part, 4096, [2, HW], B)
        u_part = view(R_part, 5120, [HW])
        qk_prod = view(R_part, 5632, [HW], B)
        conv_in = view(R_cm, 0, [C4, T + B + 2])
        mix_c = view(R_cm, 2088, [C4, T + B])
        scores = view(R_cm, 4168, [B, PPP, H])
        decay = view(R_cm, 6216, [B, PPP, H])
        prod = view(R_x, 0, [CH * H, HD])
        q_b = view(R_x, 2048, [2, HW])
        f_t = view(R_x, 3072, [T + B], H)
        f_a = view(R_x, 3592, [T + B], H)
        cum = view(R_x, 4112, [T], H)
        neg_cum = f_a
        w_f = view(R_x, 4624, [KD, H])
        k_row = [view(R_t, i * 512, [HW]) for i in range(NT)]
        c_rows = view(R_t, 1024, [HW], 2 + B)
        sq_c = view(R_part, 4096, [T])
        rt_c = view(R_part, 4608, [T])
        probs = [view(R_t, i * 512, [T]) for i in range(2)]
        probs_t = [view(R_t, 1024 + i * 512, [NT, P]) for i in range(2)]
        o_row = view(R_t, 2048, [H, HD])
        o_sq = view(R_t, 2560, [H, HD])
        news = view(R_t, 3072, [B, H])
        top = view(R_t, 3136, [B, H])
        top_all = view(R_t, 3200, [B, H])
        p_new = view(R_t, 3264, [B, H])
        p_sum = view(R_t, 3328, [B, H])
        lf_rows = view(R_t, 3392, [5, H])
        lf_diag = view(R_t, 3432, [B, H], B)
        tail = view(R_t, 3496, [B, H])
        state_t = view(R_part, 3620, [C4, B, 2])
        state_rows = view(R_part, 1280, [HW], 2 * B)
        y_tmp = view(R_part, 3684, [C4, B])
        kv = view(R_kv, 0, [RING, CH * H, HD])
        v_ring = view(R_kv, 0, [RING, CH, HW])
        kv_flat = view(R_kv, 0, [RING, CH * HW])
        w_unit = view(R_w, 0, [3, 4, SECS])
        part = view(R_part, 0, [12, SECS])
        mix_a = view(R_h, 0, [C4, T + B])
        o_m = [view(R_h, 2080 + i * 512, [HW]) for i in range(2)]
        o_t = view(R_h, 3104, [C4, B])
        o_q = view(R_h, 3136, [C4, B])
        o_r = view(R_h, 3168, [C4, B])
        b_row = view(R_h, 3200, [1024], 1)
        x_r = view(R_x, 0, [5, D])
        wo = view(R_q, 0, [KD, D])
        ga1_p, sh2_p, sc2_p, ga1_s, sh2_s, sc2_s = (view(R_w, i * 1024, [D]) for i in range(6))
        g_b = view(R_cm, 0, [D])
        prod_o = view(R_t, 2048, [D])
        junk2 = view(R_part, 0, [D])
        h2_t = view(R_part, 1024, [KD, P])
        w_r = view(R_h, 3200, [KD, NG + NE])
        b_r = view(R_h, 3488, [NG + NE])
        lg = view(R_h, 3524, [5, NG + NE])
        slot_is = view(R_t, 0, [2, 5, P])
        vals = view(R_t, 1280, [2, 5, 3 * NE])
        oh = view(R_t, 2240, [2, 5, NE])
        both = view(R_t, 2560, [5, NE])
        rank_e = view(R_t, 2720, [5, NE])
        els = view(R_t, 2880, [5, NG, EPG])
        el = view(R_t, 3040, [5, EPG])
        e_c = view(R_t, 3080, [2, 5, EPG])
        e_t = view(R_t, 3160, [5, EPG])
        ge = view(R_t, 3200, [5, NG])
        g_oh = view(R_t, 3220, [5, NG])
        st = view(R_t, 3240, [12, 5])
        rank = view(R_t, 3300, [2, 5])
        slot_no = view(R_t, 3310, [P])
        tok2 = view(R_t, 3438, [5])
        desc = view(R_t, 3443, [EPG])
        half_no = view(R_t, 3451, [1])
        far_half = view(R_t, 3452, [1])
        tmp5 = view(R_t, 3453, [5])
        cnt = view(R_t, 3458, [NE])
        cnt_max = view(R_t, 3490, [1])
        tabs = view(R_part, 2048, [NE])
        g_idx = view(R_part, 2080, [NE]).bitcast(I32)
        mark = view(R_part, 2144, [1])
        s_idx = view(R_part, 2112, [NE]).bitcast(I32)
        exp_w = [view(r, 0, [6144]) for r in (R_w, R_kv, R_q, R_cm)]
        x_e = [view(R_h, i * 512, [512]) for i in range(2)]
        xe_t = [view(R_h, 1024 + i * 512, [4, 2, SLOTS]) for i in range(2)]
        sig = [view(R_h, 2048 + i * 256, [DE], SLOTS) for i in range(2)]
        hid = [view(R_h, 2560 + i * 256, [DE], SLOTS) for i in range(2)]
        hid_t = [view(R_h, 3072 + i * 128, [2, SLOTS]) for i in range(2)]
        y_e = [view(R_h, 3328 + i * 512, [512]) for i in range(2)]
        y_g = [view(R_w, i * 2048, [2, D]) for i in range(3)] + [view(R_kv, i * 2048, [2, D]) for i in range(2)]
        ga2_p, ga2_s = (view(R_kv, 6144 + i * 1024, [D]) for i in range(2))
        shf_p, shf_s = (view(R_q, 6144 + i * 1024, [D]) for i in range(2))
        scf_p, scf_s = (view(R_cm, 6216 + i * 1024, [D]) for i in range(2))
        gf_b = view(R_part, 1024, [D])

        bank = [ctx.enter_context(nc.psum_tensor(f"bank{i}", [P, 512], F32)) for i in range(8)]

        names = """wo_part_done ov_held unit_used ada_done consts_ready setup_ready setup_psum c_silu
            vec_loaded ba_loaded part_ready sh_ready expand_done h_row_ready ht_ready h_psum samp_evac
            samp_done row_evac row_done samp_u samp_g samp_t acc_act acc_dve acc_done krow_evac
            krow_done wf_loaded f_done lf_ready lf_done st_loaded st_done lf_evac crow_done crow_evac
            st_evac sq_ready cn_done cn_sqrt decay_sum select_done tail_done p_ready s_done pt_ready
            pt_done o_taken pv_done o_ready mix_ready ot_done tail_evac mod2_act wo_attn_loaded wo_conv_loaded mix_ready_c
            wo_taken samp_norm_dve wo_done h2_ready h2t_ready h2_psum mod2_dve wr_loaded lg_done
            exp_ready zeroed pnew_ready om_ready v_used pvs_done ot2_done softmax_in samp_norm_psum
            samp_norm_act route_in rank_done vals_ready tabs_done xe_done xet_ready gu_done hid_ready
            hidt_done hidt_ready y_ready y_done tabs_ready mod3_ready act_step c_loaded x_loaded
            rstd_sq q_stored outs f_taken ln_ready max_ready o_sq_ready o_ssq o_sqrt x1_ready
            norm_sqrt route_exp sig_ready dve_step pt_loaded g_loaded k_used select_in top_ready
            lg_taken route_consts count_ready ov_slots fin_ready pool_step f_loaded ov_cols y_all
            state_out""".split()
        S = {n: sem(n) for n in names}
        unit_loaded = [sem(f"unit_loaded{i}") for i in range(3)]
        b_loaded = [sem(f"bias_loaded{i}") for i in range(2)]
        kv_loaded = [sem(f"kv_loaded{i}") for i in range(RING)]
        qb_loaded = [sem(f"qb_loaded{i}") for i in range(2)]
        krow_out = [sem(f"krow_out{i}") for i in range(2)]
        h2_out = [sem(f"h2_out{i}") for i in range(2)]
        gate_loaded = [sem(f"gate_loaded{i}") for i in range(4)]
        down_loaded = [sem(f"down_loaded{i}") for i in range(4)]
        xe_loaded = [sem(f"xe_loaded{i}") for i in range(2)]
        y_stored = [sem(f"y_stored{i}") for i in range(2)]
        yg_loaded = [sem(f"yg_loaded{i}") for i in range(5)]
        y_out = [sem(f"y_out{i}") for i in range(2)]

        block = ctx.enter_context(nc.Block())
        sel8 = sel[:, 0:B, 0]
        chunk_sec = [(w_ada_v, n * SECS) for n in range(12)] + [(w_fin_v, n * SECS) for n in range(4)]
        STORED = 16 * (NE // 2)
        NEW_AT, DIAG_AT = 16, 29

        ADA_AT = {w: n for n, w in enumerate((0, 1, 3, 4, 6, 8, 10, 12, 14, 16, 19, 22))}
        SPREAD_AT = {w: j for j, w in enumerate((24, 25, 28, 29, 30, 31))}
        SOFTMAX_AT = 27

        @block.tensor
        def _(pe):
            def use_unit(u):
                pe.wait_ge(unit_loaded[u % 3], 16 * (u // 3 + 1))
                return w_unit[:, u % 3]

            def ada_chunk(n, psum, brow):
                for half in range(2):
                    u = (2 * n if n < 4 else 12 + 2 * n) + half
                    w = use_unit(u)
                    for j in range(4):
                        last = nc.tensor.matmul(psum[32 * j:32 * j + 32, :], c_t[:, 4 * half + j, :], w[:, j, :],
                                                start=(half == 0), stop=(half == 1 and j > 0))
                    last.then_inc(S["unit_used"], 1)
                nc.tensor.matmul(psum[0:32, :], ones[0:1, 0:32], brow, start=False, stop=True)\
                    .then_inc(S["ada_done"], 1)

            pe.wait_ge(S["consts_ready"], 4)
            pe.wait_ge(S["setup_ready"], 1)
            nc.tensor.matmul(bank[6][:, 32:32 + B], pt_exp[:, :, :].rearrange("p a b -> p (a b)"), ident[0:B, 0:B], start=True, stop=True)\
                .then_inc(S["setup_psum"], 1)
            pe.wait_ge(S["c_silu"], 1)
            for k in range(KD):
                last = nc.tensor.transpose(bank[7][:, 9 * k:9 * k + 9], c_row[:, k * P:(k + 1) * P],
                                           ident[0:B + 1, 0:B + 1])
            last.then_inc(S["setup_psum"], 1)
            pe.wait_ge(S["vec_loaded"], 64)
            pe.wait_ge(S["setup_ready"], 3)
            nc.tensor.transpose(bank[6][:, 0:20], vec_rows[:, :], ident[0:20, 0:20]).then_inc(S["setup_psum"], 1)
            pe.wait_ge(S["setup_ready"], 4)
            pe.wait_ge(S["ba_loaded"], 16)

            def expand_first(n):
                pe.wait_ge(S["part_ready"], n + 1)
                if n >= 2:
                    pe.wait_ge(S["sh_ready"], n - 1)
                nc.tensor.matmul(bank[2 + n % 2][0:B, :], sel8, part_a[:, n, :], start=True, stop=True)
                nc.tensor.matmul(bank[4 + n % 2][:, :], sel[:, B, :], part_a[:, n, :], start=True, stop=True)\
                    .then_inc(S["expand_done"], 1)

            for n in range(4):
                if n >= 2:
                    pe.wait_ge(S["part_ready"], n - 1)
                ada_chunk(n, bank[n % 2], b_row_a[:, n * SECS:(n + 1) * SECS])
                if n:
                    expand_first(n - 1)
            expand_first(3)

            def transpose_h(i):
                pe.wait_ge(S["h_row_ready"], i + 1)
                if i == 0:
                    for k in range(KD):
                        last = nc.tensor.transpose(bank[6][:, 64 + 8 * k:72 + 8 * k],
                                                   h_row[0][0:B, k * P:(k + 1) * P], ident[0:B, 0:B])
                else:
                    if i >= 3:
                        pe.wait_ge(S["ht_ready"], i - 1)
                    for k in range(KD):
                        last = nc.tensor.transpose(bank[(2 if i % 2 else 4) + k // 4][:, (k % 4) * P:(k % 4 + 1) * P],
                                                   h_row[i % 2][:, k * P:(k + 1) * P], ident[:])
                last.then_inc(S["h_psum"], 1)

            def sample_section(s):
                pe.wait_ge(S["ht_ready"], 1)
                pe.wait_ge(S["consts_ready"], 2)
                if s:
                    pe.wait_ge(S["samp_evac"], s)
                for half in range(2):
                    w = use_unit(8 + 2 * s + half)
                    for j in range(4):
                        last = nc.tensor.matmul(bank[7][32 * j:32 * j + 32, :],
                                                h_t[:, 4 * half + j, T:T + 32], w[:, j, :],
                                                start=(half == 0), stop=(half == 1))
                last.then_inc(S["samp_done"], 1)

            def sample_rows(s):
                pe.wait_ge(S["samp_evac"], s + 1)
                if s:
                    pe.wait_ge(S["row_evac"], s)
                nc.tensor.matmul(bank[6][0:B, :], sel8, s_part[:, s, :], start=True, stop=True)\
                    .then_inc(S["row_done"], 1)

            def sample_columns(s):
                pe.wait_ge(S["samp_evac"], s + 1)
                pe.wait_ge(*{3: (S["row_evac"], 3), 4: (S["samp_u"], 1), 5: (S["samp_g"], 1)}[s])
                for c in range(C4):
                    last = nc.tensor.matmul(bank[6][:, c * B:(c + 1) * B], u_part[:, c * P:(c + 1) * P], sel8,
                                            start=True, stop=True)
                last.then_inc(S["samp_t"], 1)

            def prompt_section(s):
                for half in range(2):
                    w = use_unit(8 + 2 * s + half)
                    for m in range(4):
                        if half == 0:
                            if 1 <= s <= 4:
                                pe.wait_ge(S["acc_act"], 4 * (s - 1) + m + 1)
                            if s == 5:
                                pe.wait_ge(S["acc_dve"], m + 1)
                        for j in range(4):
                            k = 4 * half + j
                            if s == 2:
                                l, r = h_t[:, k, m * P:(m + 1) * P], w[:, j, :]
                            else:
                                l, r = w[:, j, m * P:(m + 1) * P], h_t[:, k, 0:T]
                            last = nc.tensor.matmul(bank[m][:, :], l, r, start=(k == 0), stop=(k == KD - 1))
                        if half:
                            last.then_inc(S["acc_done"], 1)
                    if half == 0:
                        last.then_inc(S["unit_used"], 1)

            transpose_h(0)
            sample_section(0)
            transpose_h(1)
            sample_rows(0)
            for i in range(2, 5):
                transpose_h(i)
            pe.wait_ge(S["ht_ready"], 5)
            prompt_section(0)
            for s in (1, 2):
                sample_section(s)
                prompt_section(s)
                sample_rows(s)
            pe.wait_ge(S["acc_act"], 8)
            for t in range(NT):
                if t >= 2:
                    pe.wait_ge(S["krow_evac"], t - 1)
                for c in range(C4):
                    last = nc.tensor.transpose(bank[4 + t % 2][:, c * P:(c + 1) * P],
                                               k_t[:, c, t * P:(t + 1) * P], ident[:])
                last.then_inc(S["krow_done"], 1)
            pe.wait_ge(S["krow_evac"], 4)
            pe.wait_ge(S["wf_loaded"], 16)
            for k in range(KD):
                nc.tensor.matmul(bank[4][0:H, :], w_f[:, k, :], h_t[:, k, 0:T], start=(k == 0), stop=(k == KD - 1))
            for k in range(KD):
                last = nc.tensor.matmul(bank[5][0:H, 0:B], w_f[:, k, :], h_t[:, k, T:T + B],
                                        start=(k == 0), stop=(k == KD - 1))
            last.then_inc(S["f_done"], 1)
            sample_section(3)
            prompt_section(3)
            sample_columns(3)
            pe.wait_ge(S["lf_ready"], 1)
            for t in range(NT):
                nc.tensor.transpose(bank[4][:, t * H:(t + 1) * H], f_t[:, t * P:(t + 1) * P], ident[0:H, 0:H])
            nc.tensor.transpose(bank[4][0:B, 32:32 + H], f_t[:, T:T + B], ident[0:H, 0:H]).then_inc(S["lf_done"], 1)
            pe.wait_ge(S["st_loaded"], 16)
            for c in range(C4):
                last = nc.tensor.transpose(bank[5][:, c * 16:(c + 1) * 16], state_rows[:, c * P:(c + 1) * P],
                                           ident[0:16, 0:16])
            last.then_inc(S["st_done"], 1)
            sample_section(4)
            prompt_section(4)
            sample_columns(4)
            sample_section(5)
            prompt_section(5)
            sample_columns(5)
            pe.wait_ge(S["acc_dve"], 4)
            pe.wait_ge(S["samp_g"], 1)
            pe.wait_ge(S["lf_evac"], 2)
            for c in range(C4):
                last = nc.tensor.transpose(bank[4][0:2 + B, c * P:(c + 1) * P], conv_in[:, c, T:T + 2 + B], ident[:])
            last.then_inc(S["crow_done"], 1)
            def score(w):
                t, h = divmod(w, H)
                n, c, o = (t + 1) * P, h // 2, (h % 2) * HD
                if w >= 3:
                    pe.wait_ge(S["p_ready"], w - 2)
                out = bank[w % 3][:, 0:n]
                nc.tensor.matmul(out, q_t[o:o + HD, c, t * P:(t + 1) * P], k_t[o:o + HD, c, 0:n], start=True, stop=False)
                nc.tensor.matmul(out, sel[0:H, h, :], neg_cum[:, 0:n], start=False, stop=True).then_inc(S["s_done"], 1)

            def turn(w):
                t = w // H
                pe.wait_ge(S["p_ready"], w + 1)
                if w >= 2:
                    pe.wait_ge(S["pt_ready"], w - 1)
                for b in range(t + 1):
                    last = nc.tensor.transpose(bank[3 + w % 2][:, b * P:(b + 1) * P],
                                               probs[w % 2][:, b * P:(b + 1) * P], ident[:])
                last.then_inc(S["pt_done"], 1)

            def weigh(w):
                t, h = divmod(w, H)
                pe.wait_ge(S["pt_ready"], w + 1)
                if h == 0 and t:
                    pe.wait_ge(S["o_taken"], t)
                for b in range(t + 1):
                    last = nc.tensor.matmul(bank[5][:, h * HD:(h + 1) * HD], probs_t[w % 2][:, b, :],
                                            v_r[:, b, h * HD:(h + 1) * HD], start=(b == 0), stop=(b == t))
                last.then_inc(S["pv_done"], 1)

            def turn_output(t):
                pe.wait_ge(S["o_ready"], t + 1)
                if t == 2:
                    pe.wait_ge(S["mod2_act"], 2)
                if t == 3:
                    pe.wait_ge(S["mod2_dve"], 2)
                if t:
                    pe.wait_ge(S["mix_ready"], t)
                for c in range(C4):
                    last = nc.tensor.transpose(bank[6][:, c * P:(c + 1) * P],
                                               o_row[:, :, :].rearrange("p a b -> p (a b)")[:, c * P:(c + 1) * P],
                                               ident[:])
                last.then_inc(S["ot_done"], 1)

            def conv_sums(i):
                pe.wait_ge(S["sq_ready"], i + 1)
                n = C4 * B if i == 0 else T
                nc.tensor.matmul(bank[6][:, 0:n], block64[:], sq_c[:, 0:n], start=True, stop=True)\
                    .then_inc(S["cn_done"], 1)

            def tail_sums():
                pe.wait_ge(S["cn_sqrt"], 1 + C4)
                pe.wait_ge(S["decay_sum"], 5)
                pe.wait_ge(S["select_done"], 2)
                nc.tensor.matmul(bank[6][:, 0:B * H], later[:], decay[:, :, 0, :], start=True, stop=False)
                nc.tensor.matmul(bank[6][:, 0:B * H], ones[0:B, :], lf_diag[:, :, :].rearrange("p a b -> p (a b)"),
                                 start=False, stop=True).then_inc(S["tail_done"], 1)

            def spread_chunk(j):
                if j == 0:
                    pe.wait_ge(S["part_ready"], 16)
                    pe.wait_ge(S["mix_ready"], 2)
                elif j < 5:
                    pe.wait_ge(S["mod2_act"], j)
                if j == 2:
                    pe.wait_ge(S["mix_ready"], 3)
                if j == 5:
                    pe.wait_ge(S["mod2_dve"], 1)
                nc.tensor.matmul(bank[6][0:B, :], sel8, part[:, j, :], start=True, stop=True)
                nc.tensor.matmul(bank[7][:, :], sel[:, B, :], part[:, j, :], start=True, stop=True)\
                    .then_inc(S["expand_done"], 1)

            pe.wait_ge(S["acc_dve"], 8)
            pe.wait_ge(S["samp_evac"], 6)
            pe.wait_ge(S["samp_g"], 2)
            pe.wait_ge(S["crow_evac"], 1)
            pe.wait_ge(S["st_evac"], 1)
            score(0)
            score(1)
            for w in range(NT * H):
                turn(w)
                if w + 2 < NT * H:
                    score(w + 2)
                weigh(w)
                if w < 1 + C4:
                    conv_sums(w)
                if w == 1 + C4:
                    tail_sums()
                if w in SPREAD_AT:
                    spread_chunk(SPREAD_AT[w])
                if w in ADA_AT:
                    n = ADA_AT[w]
                    if n:
                        pe.wait_ge(S["part_ready"], 4 + n)
                    pe.wait_ge(b_loaded[n % 2], 16 * (n // 2 + 1))
                    ada_chunk(4 + n, bank[7], b_row[:, (n % 2) * SECS:(n % 2 + 1) * SECS])
                if w % H == 3 and w > H:
                    if w // H == 1:
                        pe.wait_ge(S["tail_evac"], 1)
                    turn_output(w // H - 1)
            turn_output(NT - 1)

            def out_part(t, half, k0):
                if t == 0 and half == 0:
                    pe.wait_ge(S["wo_attn_loaded" if k0 < C4 else "wo_conv_loaded"], 16)
                    pe.wait_ge(S["mix_ready"], NT)
                    pe.wait_ge(S["mix_ready_c"], 1 + C4)
                if t and k0 == 0:
                    pe.wait_ge(S["wo_taken"], 2 * t)
                for k in (k0, k0 + 1):
                    m = (mix_a[:, k, t * P:(t + 1) * P] if k < C4 else mix_c[:, k - C4, t * P:(t + 1) * P])
                    last = nc.tensor.matmul(bank[4 + half][:, :], m, wo[:, k, half * 512:(half + 1) * 512],
                                            start=(k == 0), stop=(k == KD - 1))
                if k0 == KD - 2:
                    last.then_inc(S["wo_done"], 1)

            def out_samples():
                pe.wait_ge(S["om_ready"], B)
                pe.wait_ge(S["samp_norm_dve"], 2)
                for half in range(2):
                    for k in range(KD):
                        m = mix_a[:, k, T:T + B] if k < C4 else mix_c[:, k - C4, T:T + B]
                        last = nc.tensor.matmul(bank[half][32 * (k % 4):32 * (k % 4) + B, :], m,
                                                wo[:, k, half * 512:(half + 1) * 512], start=(k < 4), stop=(k >= 4))
                    last.then_inc(S["wo_part_done"], 1)
                pe.wait_ge(S["wo_taken"], 2 * NT)
                for half, taken in enumerate((S["samp_norm_dve"], S["samp_norm_act"])):
                    pe.wait_ge(taken, 3)
                    nc.tensor.matmul(bank[4 + half][0:B, :], sel8, o_m[half][:, :], start=True, stop=True)\
                        .then_inc(S["wo_done"], 1)

            def turn_rows(t):
                n = P if t < NT else B
                pe.wait_ge(S["h2_ready"], t + 1)
                if t:
                    pe.wait_ge(S["h2t_ready"], t)
                h = h_row[t % 2][0:n, :].rearrange("p (a k) -> p k a", k=KD)
                for k in range(KD):
                    last = nc.tensor.transpose(bank[6 + k // 4][:, (k % 4) * P:(k % 4) * P + n], h[:, k, :], ident[0:n, 0:n])
                last.then_inc(S["h2_psum"], 1)

            def route(t):
                n = P if t < NT else B
                pe.wait_ge(S["h2t_ready"], t + 1)
                if t == 0:
                    pe.wait_ge(S["wr_loaded"], 64)
                for k in range(KD):
                    last = nc.tensor.matmul(bank[3][0:n, t * 36:(t + 1) * 36], h2_t[:, k, 0:n], w_r[:, k, :],
                                            start=(k == 0), stop=(k == KD - 1))
                last.then_inc(S["lg_done"], 1)

            def value_chunk(g):
                b, c = divmod(g, NCH)
                if c == 0:
                    pe.wait_ge(S["exp_ready"], b + 1)
                    if b == 0:
                        pe.wait_ge(S["zeroed"], 1)
                    if b >= 2:
                        pe.wait_ge(S["om_ready"], b - 1)
                n = NKV + g
                pe.wait_ge(kv_loaded[n % RING], 16 * (n // RING + 1))
                for j in range(CH):
                    last = nc.tensor.matmul(bank[b % 2][32 * j:32 * j + H, :], scores[:, b, c * CH + j, :],
                                            v_ring[:, n % RING, j, :], start=(c == 0),
                                            stop=(c == NCH - 1 and j > 0))
                last.then_inc(S["v_used"], 1)
                if c == NCH - 1:
                    pe.wait_ge(S["pnew_ready"], 1)
                    nc.tensor.matmul(bank[b % 2][0:H, :], p_new[0:B, b, :], v_new[:], start=False, stop=True)\
                        .then_inc(S["pvs_done"], 1)

            def gather_values(b):
                pe.wait_ge(S["om_ready"], b + 1)
                for c in range(C4):
                    last = nc.tensor.matmul(bank[2][:, c * B + b:c * B + b + 1], o_m[b % 2][:, c * P:(c + 1) * P],
                                            ones[:, 0:1], start=True, stop=True)
                last.then_inc(S["ot2_done"], 1)

            for g in range(NKV):
                value_chunk(g)
                t, j = divmod(g, 2 * NCH)
                if j < KD:
                    out_part(t, j // 4, 2 * (j % 4))
                if j == 12:
                    turn_rows(t)
                if j == 15:
                    route(t)
                if g % NCH == 2 and g >= NCH:
                    gather_values(g // NCH - 1)
            gather_values(B - 1)
            pe.wait_ge(S["softmax_in"], 4)
            for c in range(C4):
                for hh in range(2):
                    last = nc.tensor.matmul(bank[2][hh * HD:(hh + 1) * HD, 64 + c * B:64 + (c + 1) * B],
                                            ones[:, 0:HD], p_sum[:, :, 2 * c + hh], start=True, stop=True)
            last.then_inc(S["samp_norm_psum"], 1)
            pe.wait_ge(S["samp_norm_act"], 1)
            nc.tensor.matmul(bank[2][:, 128:128 + C4 * B], block64[:], o_q[:, :, :].rearrange("p a b -> p (a b)"),
                             start=True, stop=True).then_inc(S["samp_norm_psum"], 1)
            out_samples()
            turn_rows(NT)
            route(NT)

            pe.wait_ge(S["route_in"], 3)
            for t in range(5):
                n = P if t < NT else B
                for u in range(t + 1):
                    l = ones[:, 0:n] if u < t else earlier[0:n, 0:n]
                    m = P if u < NT else B
                    nc.tensor.matmul(bank[0][0:n, t * NE:(t + 1) * NE], l, both[0:m, u, :],
                                     start=(u == 0), stop=(u == t))
            for u in range(5):
                m = P if u < NT else B
                last = nc.tensor.matmul(bank[1][:, 0:NE], ones[0:m, :], both[0:m, u, :], start=(u == 0), stop=(u == 4))
            last.then_inc(S["rank_done"], 1)

            def tables(wait_on, count, done):
                pe.wait_ge(wait_on, count)
                for c in range(2):
                    for t in range(5):
                        m = P if t < NT else B
                        last = nc.tensor.matmul(bank[2][:, 0:3 * NE], slot_is[0:m, c, t, :], vals[0:m, c, t, :],
                                                start=(c == 0 and t == 0), stop=(c == 1 and t == 4))
                last.then_inc(done, 1)

            tables(S["vals_ready"], 1, S["tabs_done"])

            def gate_up(s, xs):
                gw = exp_w[s][:, 0:2048].rearrange("p (a c f) -> p a c f", a=2, c=4)
                uw = exp_w[s][:, 2048:4096].rearrange("p (a c f) -> p a c f", a=2, c=4)
                for a in range(2):
                    for c in range(4):
                        k = 4 * a + c
                        nc.tensor.matmul(bank[2 + xs][0:SLOTS, 0:DE], xe_t[xs][:, c, a, :], gw[:, a, c, :],
                                         start=(k == 0), stop=(k == 7))
                        last = nc.tensor.matmul(bank[2 + xs][SLOTS:2 * SLOTS, 0:DE], xe_t[xs][:, c, a, :],
                                                uw[:, a, c, :], start=(k == 0), stop=(k == 7))
                return last

            def transpose_x(xs):
                x4 = x_e[xs][:, :].rearrange("p (a c) -> p c a", c=4)
                for c in range(4):
                    last = nc.tensor.transpose(bank[xs][:, c * P:(c + 1) * P], x4[:, c, :], ident[:])
                return last

            def transpose_hidden(xs):
                h2 = hid[xs][:, :].rearrange("p (a k) -> p k a", k=2)
                for k in range(2):
                    last = nc.tensor.matmul(bank[2 + xs][:, 256 + k * SLOTS:256 + (k + 1) * SLOTS], h2[:, k, :],
                                            ident[0:SLOTS, 0:SLOTS], start=True, stop=True)
                return last

            def down(s, xs):
                dw = exp_w[s][:, 4096:6144].rearrange("p (k n) -> p k n", k=2)
                for k in range(2):
                    for half in range(2):
                        last = nc.tensor.matmul(bank[4 + xs][half * SLOTS:(half + 1) * SLOTS, :], hid_t[xs][:, k, :],
                                                dw[:, k, half * 512:(half + 1) * 512], start=(k == 0), stop=(k == 1))
                return last

            def front_of(g, s):
                xs, e1 = s % 2, 4 * g + s + 1
                pe.wait_ge(xe_loaded[xs], (2 * g + s // 2 + 1) * 16)
                transpose_x(xs).then_inc(S["xe_done"], 1)
                pe.wait_ge(S["xet_ready"], e1)
                pe.wait_ge(gate_loaded[s], (g + 1) * 32)
                gate_up(s, xs).then_inc(S["gu_done"], 1)

            def back_of(g, s):
                xs, e1 = s % 2, 4 * g + s + 1
                pe.wait_ge(S["hid_ready"], e1)
                transpose_hidden(xs).then_inc(S["hidt_done"], 1)
                pe.wait_ge(S["hidt_ready"], e1)
                pe.wait_ge(down_loaded[s], (g + 1) * 16)
                pe.wait_ge(S["y_ready"], e1)
                down(s, xs).then_inc(S["y_done"], 1)

            pe.wait_ge(S["tabs_ready"], 1)
            front_of(0, 0)
            front_of(0, 1)
            back_of(0, 0)
            front_of(0, 2)
            back_of(0, 1)
            front_of(0, 3)
            back_of(0, 2)
            with pe.Fori(1, NE // 4) as g:
                for s in range(4):
                    front_of(g, s)
                    if s == 0:
                        back_of(g - 1, 3)
                    else:
                        back_of(g, s - 1)
            back_of(NE // 4 - 1, 3)

            count = pe.value_load(max_count[0:1, 0:1], min_val=0, max_val=2 * (T + B))
            with pe.If(count > cap):
                with pe.Fori(1, PASSES) as p:
                    tables(S["vals_ready"], p + 1, S["tabs_done"])
                    with pe.Fori(0, NE) as e:
                        n = p * NE + e
                        pe.wait_ge(xe_loaded[0], (n - NE) * 16 + NE * 8 + 16)
                        transpose_x(0).then_inc(S["xe_done"], 1)
                        pe.wait_ge(S["xet_ready"], n + 1)
                        pe.wait_ge(gate_loaded[0], (n - NE) * 32 + NE * 8 + 32)
                        gate_up(0, 0).then_inc(S["gu_done"], 1)
                        pe.wait_ge(S["hid_ready"], n + 1)
                        transpose_hidden(0).then_inc(S["hidt_done"], 1)
                        pe.wait_ge(S["hidt_ready"], n + 1)
                        pe.wait_ge(down_loaded[0], (n - NE) * 16 + NE * 4 + 16)
                        pe.wait_ge(S["y_ready"], n + 1)
                        down(0, 0).then_inc(S["y_done"], 1)

            for j in range(6):
                if j >= 2:
                    pe.wait_ge(S["mod3_ready"], j - 1)
                nc.tensor.matmul(bank[j % 2][0:B, :], sel8, part[:, 6 + j, :], start=True, stop=True)
                nc.tensor.matmul(bank[2 + j % 2][:, :], sel[:, B, :], part[:, 6 + j, :], start=True, stop=True)\
                    .then_inc(S["expand_done"], 1)

        @block.scalar
        def _(act):
            steps = [0]

            def step(ins):
                steps[0] += 1
                ins.then_inc(S["act_step"], 1)
                act.wait_ge(S["act_step"], steps[0])

            def copy(out, in_, scale=1.0):
                return nc.scalar.activation(out, in_, ACT.Copy, scale=scale)

            act.wait_ge(S["c_loaded"], 32)
            nc.scalar.activation(c_row[:, :], c_row[:, :], ACT.Silu).then_inc(S["c_silu"], 1)
            act.wait_ge(S["x_loaded"], 32)
            act.wait_ge(S["consts_ready"], 2)
            for t in (NT, 0, 1, 2, 3):
                n = P if t < NT else B
                step(nc.scalar.activation(junk[0:n, :], x_a[0:n, t, :], ACT.Square, accum_out=ssq[0:n, t:t + 1]))
            nc.scalar.activation(ssq[:, :], ssq[:, :], ACT.Sqrt, bias=eps[:, 0:1], scale=1.0 / D)\
                .then_inc(S["rstd_sq"], 1)
            for n in range(4):
                act.wait_ge(S["ada_done"], n + 1)
                copy(part_a[:, n, :], bank[n % 2][:, :]).then_inc(S["part_ready"], 1)
                if n in (1, 2):
                    m = n - 1
                    act.wait_ge(S["expand_done"], m + 1)
                    copy(sh1_s[0:B, m * SECS:(m + 1) * SECS], bank[2 + m][0:B, :])
                    copy(sh1_p[:, m * SECS:(m + 1) * SECS], bank[4 + m][:, :]).then_inc(S["sh_ready"], 1)
            for i in range(5):
                act.wait_ge(S["h_psum"], i + 1)
                if i == 0:
                    copy(h_t[:, :, T:T + B], bank[6][:, 64:128].rearrange("p (k n) -> p k n", k=KD))\
                        .then_inc(S["ht_ready"], 1)
                    continue
                lo = (i - 1) * P
                for q in range(2):
                    last = copy(h_t[:, 4 * q:4 * q + 4, lo:lo + P],
                                bank[(2 if i % 2 else 4) + q][:, :].rearrange("p (k n) -> p k n", k=4))
                last.then_inc(S["ht_ready"], 1)
                if i == 1:
                    act.wait_ge(S["samp_done"], 1)
                    copy(s_part[:, 0, :], bank[7][:, :]).then_inc(S["samp_evac"], 1)
                    act.wait_ge(S["row_done"], 1)
                    copy(qk_new[:, 0, :], bank[6][0:B, :]).then_inc(S["row_evac"], 1)
                    act.wait_ge(S["row_evac"], 1)
                    act.dma_start(q_rows_dram[:, :], qk_new[:, 0, :]).then_inc(S["q_stored"], 16)

            def acc(s, m):
                act.wait_ge(S["acc_done"], 4 * s + m + 1)

            for m in range(4):
                acc(0, m)
                copy(q_t[:, m, :], bank[m][:, :], SCALE).then_inc(S["acc_act"], 1)
            for s in (1, 2):
                act.wait_ge(S["samp_done"], s + 1)
                copy(s_part[:, s, :], bank[7][:, :]).then_inc(S["samp_evac"], 1)
                for m in range(4):
                    acc(s, m)
                    copy((k_t if s == 1 else v_r)[:, m, :], bank[m][:, :]).then_inc(S["acc_act"], 1)
                act.wait_ge(S["row_done"], s + 1)
                new = qk_new[:, 1, :] if s == 1 else v_new[:, :]
                copy(new, bank[6][0:B, :]).then_inc(S["row_evac"], 1)
                act.wait_ge(S["row_evac"], s + 1)
                dst = (k_sample if s == 1 else v_sample).rearrange("l b t h d -> (l b t) (h d)")
                act.dma_start(dst, new).then_inc(S["outs"], 16)
            act.wait_ge(S["acc_act"], 12)
            act.dma_start(v_prompt.rearrange("l b (t p) h d -> (l b p) t (h d)", p=P), v_r[:, :, :])\
                .then_inc(S["outs"], 16)
            kp = k_prompt.rearrange("l b (t p) h d -> (l b t) p (h d)", p=P)
            for t in range(NT):
                act.wait_ge(S["krow_done"], t + 1)
                copy(k_row[t][:, :], bank[4 + t % 2][:, :]).then_inc(S["krow_evac"], 1)
                act.wait_ge(S["krow_evac"], t + 1)
                act.dma_start(kp[t, :, :], k_row[t][:, :]).then_inc(krow_out[t % 2], 16)
            act.wait_ge(S["f_taken"], 1)
            step(nc.scalar.activation(f_a[:, :], f_a[:, :], ACT.Exp, scale=-1.0))
            nc.scalar.activation(f_a[:, :], f_a[:, :], ACT.Ln, bias=ones[0:H, 0:1]).then_inc(S["ln_ready"], 1)
            act.wait_ge(S["samp_done"], 4)
            act.wait_ge(S["consts_ready"], 3)
            copy(u_part[:, :], bank[7][:, :]).then_inc(S["samp_evac"], 1)
            for m in range(4):
                acc(3, m)
                copy(conv_in[:, m, 2:2 + T], bank[m][:, :]).then_inc(S["acc_act"], 1)
            act.wait_ge(S["samp_t"], 1)
            copy(conv_in[:, :, T + 2:T + 2 + B], bank[6][:, 0:C4 * B].rearrange("p (c b) -> p c b", c=C4))\
                .then_inc(S["samp_u"], 1)
            act.wait_ge(S["lf_done"], 1)
            copy(lf_rows[:, 0:NT, :], bank[4][:, 0:NT * H].rearrange("p (t h) -> p t h", t=NT))\
                .then_inc(S["lf_evac"], 1)
            copy(lf_rows[0:B, NT, :], bank[4][0:B, 32:32 + H]).then_inc(S["lf_evac"], 1)
            act.wait_ge(S["lf_evac"], 2)
            act.dma_start(logf_prompt.rearrange("l b (t p) h -> (l b p) t h", p=P), lf_rows[:, 0:NT, :])\
                .then_inc(S["outs"], 16)
            act.dma_start(logf_sample.rearrange("l b t h -> (l b t) h"), lf_rows[0:B, NT, :])\
                .then_inc(S["outs"], 16)
            act.wait_ge(S["st_done"], 1)
            copy(state_t[:, :, :, :], bank[5][:, 0:C4 * 16].rearrange("p (c b j) -> p c b j", c=C4, b=B))\
                .then_inc(S["st_evac"], 1)
            for s in (4, 5):
                act.wait_ge(S["samp_done"], s + 1)
                act.wait_ge(S["samp_t"], s - 3)
                copy(u_part[:, :], bank[7][:, :]).then_inc(S["samp_evac"], 1)
            act.wait_ge(S["crow_done"], 1)
            act.wait_ge(krow_out[0], 32)
            act.wait_ge(krow_out[1], 32)
            copy(c_rows[:, :], bank[4][0:2 + B, :]).then_inc(S["crow_evac"], 1)
            act.wait_ge(S["crow_evac"], 1)
            act.dma_start(conv_prompt.rearrange("l b j c -> (l b j) c"), c_rows[0:2, :]).then_inc(S["outs"], 16)
            act.dma_start(conv_sample[0, :, 1, :], c_rows[2:2 + B, :]).then_inc(S["outs"], 16)
            act.wait_ge(S["outs"], 16 * 7)
            act.wait_ge(krow_out[0], 32)
            act.wait_ge(krow_out[1], 32)

            def conv_square(i):
                act.wait_ge(S["acc_dve"], 4 + C4)
                act.wait_ge(S["samp_g"], 2)
                if i:
                    act.wait_ge(S["cn_done"], i)
                src = mix_c[:, :, T:T + B] if i == 0 else mix_c[:, i - 1, 0:T]
                dst = sq_c[:, 0:C4 * B].rearrange("p (c b) -> p c b", c=C4) if i == 0 else sq_c[:, 0:T]
                nc.scalar.activation(dst, src, ACT.Square).then_inc(S["sq_ready"], 1)

            def conv_sqrt(i):
                act.wait_ge(S["cn_done"], i + 1)
                if i:
                    act.wait_ge(S["mix_ready_c"], i)
                n = C4 * B if i == 0 else T
                nc.scalar.activation(rt_c[:, 0:n], bank[6][:, 0:n], ACT.Sqrt, bias=eps[:, 0:1], scale=1.0 / HD)\
                    .then_inc(S["cn_sqrt"], 1)

            def ada_evac(n):
                act.wait_ge(S["ada_done"], 4 + n + 1)
                copy(part[:, n, :], bank[7][:, :]).then_inc(S["part_ready"], 1)

            def spread_evac(j):
                act.wait_ge(S["expand_done"], 4 + j + 1)
                half = slice((j % 2) * SECS, (j % 2 + 1) * SECS)
                copy((ga1_s if j < 2 else sh2_s)[0:B, half], bank[6][0:B, :])
                copy((ga1_p if j < 2 else sh2_p)[:, half], bank[7][:, :]).then_inc(S["mod2_act"], 1)

            def soft(w):
                t = w // H
                n = (t + 1) * P
                act.wait_ge(S["max_ready"], w + 1)
                if w >= 2:
                    act.wait_ge(S["pt_done"], w - 1)
                i = (t % 2) * H + w % H
                nc.scalar.activation(probs[w % 2][:, 0:n], bank[w % 3][:, 0:n], ACT.Exp,
                                     bias=neg_max[:, w % 2:w % 2 + 1], accum_out=row_sum[:, i:i + 1])\
                    .then_inc(S["p_ready"], 1)

            def square_output(t):
                act.wait_ge(S["o_taken"], t + 1)
                nc.scalar.activation(o_sq[:, :, :], o_row[:, :, :], ACT.Square).then_inc(S["o_sq_ready"], 1)

            def norm_output(t):
                act.wait_ge(S["o_ssq"], t + 1)
                nc.scalar.activation(head_ssq[:, :], head_ssq[:, :], ACT.Sqrt, bias=eps[:, 0:1], scale=1.0 / HD)\
                    .then_inc(S["o_sqrt"], 1)

            def output_out(t):
                act.wait_ge(S["ot_done"], t + 1)
                for c in range(C4):
                    last = copy(mix_a[:, c, t * P:(t + 1) * P], bank[6][:, c * P:(c + 1) * P], vecs[:, c:c + 1])
                last.then_inc(S["mix_ready"], 1)

            conv_square(0)
            for w in range(NT * H):
                soft(w)
                t = w // H
                act.wait_ge(S["pt_done"], w + 1)
                if w >= 2:
                    act.wait_ge(S["pv_done"], w - 1)
                copy(probs_t[w % 2][:, 0:t + 1, :],
                     bank[3 + w % 2][:, 0:(t + 1) * P].rearrange("p (b n) -> p b n", n=P)).then_inc(S["pt_ready"], 1)
                if w < 1 + C4:
                    conv_sqrt(w)
                if w < C4:
                    conv_square(w + 1)
                if w == 1 + C4:
                    act.wait_ge(S["tail_done"], 1)
                    copy(tail[:, :, :], bank[6][:, 0:B * H].rearrange("p (b h) -> p b h", b=B))\
                        .then_inc(S["tail_evac"], 1)
                if w - 1 in ADA_AT:
                    ada_evac(ADA_AT[w - 1])
                if SPREAD_AT.get(w - 1, 4) < 4:
                    spread_evac(SPREAD_AT[w - 1])
                if w % H == 0 and w:
                    square_output(t - 1)
                if w % H == 1 and w > H:
                    norm_output(t - 1)
                if w % H == 3 and w > H:
                    output_out(t - 1)
                if w >= NT * H - 2:
                    if w == NT * H - 2:
                        act.wait_ge(S["softmax_in"], 3)
                        nc.scalar.activation(p_new[:, :, :], p_new[:, :, :], ACT.Exp).then_inc(S["pnew_ready"], 1)
                    for b in range(4 * (w % 2), 4 * (w % 2) + 4):
                        nc.scalar.activation(scores[:, b, :, :], scores[:, b, :, :], ACT.Exp)\
                            .then_inc(S["exp_ready"], 1)
            square_output(NT - 1)
            norm_output(NT - 1)
            output_out(NT - 1)

            def second_norm(t):
                n = P if t < NT else B
                act.wait_ge(S["x1_ready"], t + 1)
                step(nc.scalar.activation(junk2[0:n, :], x_r[0:n, t, :], ACT.Square, accum_out=ssq[0:n, t:t + 1]))
                nc.scalar.activation(ssq[0:n, t:t + 1], ssq[0:n, t:t + 1], ACT.Sqrt, bias=eps[0:n, 0:1], scale=1.0 / D)\
                    .then_inc(S["norm_sqrt"], 1)
                act.wait_ge(S["h2_ready"], t + 1)
                act.dma_start(h2_dram[t * 2 * P:t * 2 * P + 2 * n, :].rearrange("(p a) d -> p (a d)", a=2),
                              h_row[t % 2][0:n, :]).then_inc(h2_out[t % 2], 16)
                act.wait_ge(S["h2_psum"], t + 1)
                if t:
                    act.wait_ge(S["lg_done"], t)
                for q in range(2):
                    last = copy(h2_t[:, 4 * q:4 * q + 4, 0:n],
                                bank[6 + q][:, :].rearrange("p (k n) -> p k n", k=4)[:, :, 0:n])
                last.then_inc(S["h2t_ready"], 1)

            for t in range(NT):
                second_norm(t)
            act.wait_ge(S["samp_norm_dve"], 1)
            nc.scalar.activation(o_q[:, :, :], o_t[:, :, :], ACT.Square).then_inc(S["samp_norm_act"], 1)
            act.wait_ge(S["samp_norm_psum"], 2)
            nc.scalar.activation(o_r[:, :, :], bank[2][:, 128:128 + C4 * B].rearrange("p (c b) -> p c b", c=C4),
                                 ACT.Sqrt, bias=eps[:, 0:1], scale=1.0 / HD).then_inc(S["samp_norm_act"], 1)
            act.wait_ge(S["wo_part_done"], 2)
            act.wait_ge(S["ot2_done"], B)
            copy(o_m[1][:, :], bank[1][:, :]).then_inc(S["samp_norm_act"], 1)
            second_norm(NT)
            act.wait_ge(S["route_in"], 1)
            nc.scalar.activation(ge[:, :, :], ge[:, :, :], ACT.Exp).then_inc(S["route_exp"], 1)
            act.wait_ge(S["route_in"], 2)
            nc.scalar.activation(el[:, :, :], el[:, :, :], ACT.Exp).then_inc(S["route_exp"], 1)

            def x_out(xs):
                return copy(xe_t[xs][:, :, :, :],
                            bank[xs][:, :].rearrange("p (c a n) -> p c a n", c=4, a=2))

            def gate_silu(xs):
                return nc.scalar.activation(sig[xs][:, :], bank[2 + xs][0:SLOTS, 0:DE], ACT.Silu)

            with act.Fori(0, NE // 4) as g:
                for s in range(4):
                    xs, e1 = s % 2, 4 * g + s + 1
                    act.wait_ge(S["xe_done"], e1)
                    if s >= 2:
                        act.wait_ge(S["gu_done"], e1 - 2)
                    x_out(xs).then_inc(S["xet_ready"], 1)
                    act.wait_ge(S["gu_done"], e1)
                    gate_silu(xs).then_inc(S["sig_ready"], 1)
            count = act.value_load(max_count[0:1, 0:1], min_val=0, max_val=2 * (T + B))
            with act.If(count > cap):
                with act.Fori(NE, PASSES * NE) as n:
                    act.wait_ge(S["xe_done"], n + 1)
                    x_out(0).then_inc(S["xet_ready"], 1)
                    act.wait_ge(S["gu_done"], n + 1)
                    gate_silu(0).then_inc(S["sig_ready"], 1)

            for j in range(6):
                act.wait_ge(S["expand_done"], j + 11)
                half = slice((j % 2) * SECS, (j % 2 + 1) * SECS)
                if j < 4:
                    copy((ga2_s if j < 2 else shf_s)[0:B, half], bank[j % 2][0:B, :])
                    copy((ga2_p if j < 2 else shf_p)[:, half], bank[2 + j % 2][:, :]).then_inc(S["mod3_ready"], 1)
            for i, t in enumerate((0, 1, 2, 3, NT)):
                n = P if t < NT else B
                act.wait_ge(S["x1_ready"], i + 6)
                step(nc.scalar.activation(junk2[0:n, :], x_r[0:n, t, :], ACT.Square, accum_out=ssq[0:n, t:t + 1]))
                nc.scalar.activation(ssq[0:n, t:t + 1], ssq[0:n, t:t + 1], ACT.Sqrt, bias=eps[0:n, 0:1], scale=1.0 / D)\
                    .then_inc(S["norm_sqrt"], 1)
            act.wait_ge(S["outs"], 16 * 7)

        @block.vector
        def _(dve):
            V = nc.vector
            steps = [0]

            def step(ins):
                steps[0] += 1
                ins.then_inc(S["dve_step"], 1)
                dve.wait_ge(S["dve_step"], steps[0])

            def spread(ap, shape):
                return ap.to_broadcast(shape)

            step(V.memset(c_t[:, :, :], 0.0))
            dve.wait_ge(S["pt_loaded"], 16)
            V.tensor_copy(pt_exp[:, :, :], spread(pt_int[:, :].rearrange("b (j o) -> b j o", o=1), [B, NPG, 4]))\
                .then_inc(S["setup_ready"], 1)
            dve.wait_ge(S["consts_ready"], 1)
            step(V.tensor_single_scalar(lane[:, :], lane[:, :], 3, ALU.bitwise_and))
            step(V.tensor_copy(quarter[:, 8:9], lane[:, :]))
            for s in range(NCH):
                last = V.tensor_scalar(quarter[:, s:s + 1], quarter[:, 8:9], float(NCH), float(s), ALU.mult, ALU.add)
            step(last)
            dve.wait_ge(S["setup_psum"], 1)
            ids = bank[6][:, 32:32 + B]
            V.tensor_scalar(f_index[:, :], ids, 4.0, quarter[:, 8:9], ALU.mult, ALU.add).then_inc(S["setup_ready"], 1)
            for s in range(NCH):
                last = V.tensor_scalar(kv_index[:, :].rearrange("p (b s) -> p s b", s=NCH)[:, s, :], ids,
                                       4.0 * NCH, quarter[:, s:s + 1], ALU.mult, ALU.add)
            last.then_inc(S["setup_ready"], 1)
            dve.wait_ge(S["setup_psum"], 2)
            V.tensor_copy(c_t[:, :, 0:B + 1], bank[7][:, 0:KD * 9].rearrange("p (k n) -> p k n", k=KD))\
                .then_inc(S["setup_ready"], 1)
            dve.wait_ge(S["setup_psum"], 3)
            V.tensor_copy(vecs[:, :], bank[6][:, 0:20]).then_inc(S["setup_ready"], 1)
            dve.wait_ge(S["rstd_sq"], 1)
            step(V.reciprocal(rstd[:, :], ssq[:, :]))
            dve.wait_ge(S["g_loaded"], 16)
            for m in range(2):
                dve.wait_ge(S["expand_done"], m + 3)
                lo = slice(m * SECS, (m + 1) * SECS)
                V.scalar_tensor_tensor(sc1_s[0:B, lo], bank[2 + m][0:B, :], 1.0, g1_b[0:B, lo], ALU.add, ALU.mult)
                step(V.scalar_tensor_tensor(sc1_p[:, lo], bank[4 + m][:, :], 1.0, g1_b[:, lo], ALU.add, ALU.mult))
            dve.wait_ge(S["sh_ready"], 2)
            for i in range(5):
                t, n = (NT, B) if i == 0 else (i - 1, P)
                sc, sh = (sc1_s, sh1_s) if i == 0 else (sc1_p, sh1_p)
                if i >= 2:
                    dve.wait_ge(S["h_psum"], i - 1)
                r = h_row[i % 2]
                step(V.scalar_tensor_tensor(r[0:n, :], x_a[0:n, t, :], rstd[0:n, t:t + 1], sc[0:n, :], ALU.mult, ALU.mult))
                V.tensor_tensor(r[0:n, :], r[0:n, :], sh[0:n, :], ALU.add).then_inc(S["h_row_ready"], 1)

            def k_chunk(n):
                b, s = divmod(n, NCH)
                dve.wait_ge(kv_loaded[n % RING], 16 * (n // RING + 1))
                if s == 0:
                    dve.wait_ge(qb_loaded[b % 2], 16 * (b // 2 + 1))
                if n:
                    dve.wait_ge(S["k_used"], n)
                q = q_b[:, b % 2, :].rearrange("p (o c) -> p o c", o=1)
                step(V.tensor_tensor(prod[:, :, :].rearrange("p (r h) d -> p r (h d)", r=CH),
                                     kv[:, n % RING, :, :].rearrange("p (r h) d -> p r (h d)", r=CH),
                                     spread(q, [P, CH, HW]), ALU.mult))
                V.reduce_sum(scores[:, b, s * CH:(s + 1) * CH, :].rearrange("p r h -> p (r h)"),
                             prod[:, :, :], AX.X).then_inc(S["k_used"], 1)
            next_k = [0]

            def k_chunks(m):
                for _ in range(m):
                    if next_k[0] < NKV:
                        k_chunk(next_k[0])
                        next_k[0] += 1

            k_chunks(NEW_AT)
            dve.wait_ge(S["row_evac"], 2)
            step(V.tensor_tensor(qk_prod[:, :], qk_new[:, 0, :], qk_new[:, 1, :], ALU.mult))
            step(V.memset(news[:, :, :], NEG))
            step(V.reduce_sum(top[0:B, 0, :], qk_prod[:, :].rearrange("p (h d) -> p h d", h=H), AX.X))
            V.tensor_scalar(news[0:B, :, :], spread(top[0:B, 0:1, :], [B, B, H]), SCALE, None, ALU.mult)\
                .then_inc(S["select_in"], 1)
            k_chunks(4)
            dve.wait_ge(S["f_done"], 1)
            dve.wait_ge(S["vec_loaded"], 64)
            V.tensor_scalar(f_t[:, 0:T], bank[4][0:H, :], b_f[:, 0:1], None, ALU.add)
            step(V.tensor_scalar(f_t[:, T:T + B], bank[5][0:H, 0:B], b_f[:, 0:1], None, ALU.add))
            step(V.tensor_scalar(f_a[:, :], f_t[:, :], -1.0, None, ALU.mult))
            V.tensor_tensor(f_a[:, :], f_a[:, :], f_t[:, :], ALU.max).then_inc(S["f_taken"], 1)
            k_chunks(1)
            dve.wait_ge(S["ln_ready"], 1)
            step(V.scalar_tensor_tensor(f_t[:, :], f_t[:, :], 0.0, f_a[:, :], ALU.min, ALU.subtract))
            step(V.tensor_tensor_scan(cum[:, :], f_t[:, 0:T], f_t[:, 0:T], 0.0, ALU.add, ALU.bypass))
            V.tensor_scalar(neg_cum[:, 0:T], cum[:, :], -1.0, None, ALU.mult).then_inc(S["lf_ready"], 1)
            k_chunks(DIAG_AT - NEW_AT - 5)
            dve.wait_ge(S["lf_evac"], 2)
            V.tensor_copy(lf_diag[:, :, :], spread(lf_rows[0:B, NT:NT + 1, :], [B, B, H])).then_inc(S["select_in"], 1)
            for m in range(4):
                dve.wait_ge(S["acc_done"], 16 + m + 1)
                dve.wait_ge(S["acc_act"], 12 + m + 1)
                V.tensor_tensor(conv_in[:, m, 2:2 + T], bank[m][:, :], conv_in[:, m, 2:2 + T], ALU.mult)\
                    .then_inc(S["acc_dve"], 1)
                k_chunks(1)
            dve.wait_ge(S["samp_t"], 2)
            dve.wait_ge(S["samp_u"], 1)
            new_in = conv_in[:, :, T + 2:T + 2 + B]
            V.tensor_tensor(new_in, bank[6][:, 0:C4 * B].rearrange("p (c b) -> p c b", c=C4), new_in, ALU.mult)\
                .then_inc(S["samp_g"], 1)
            dve.wait_ge(S["samp_g"], 1)
            dve.wait_ge(S["acc_dve"], 4)
            dve.wait_ge(S["st_evac"], 1)
            for j in range(3):
                src = state_t[:, :, :, j] if j < 2 else new_in
                w = spread(vecs[:, 8 + 4 * j:12 + 4 * j].rearrange("p (c o) -> p c o", o=1), [P, C4, B])
                out = mix_c[:, :, T:T + B] if j == 0 else y_tmp[:, :, :]
                step(V.tensor_tensor(out, src, w, ALU.mult))
                if j:
                    step(V.tensor_tensor(mix_c[:, :, T:T + B], mix_c[:, :, T:T + B], y_tmp[:, :, :], ALU.add))
            for m in range(4):
                out = mix_c[:, m, 0:T]
                step(V.tensor_scalar(out, conv_in[:, m, 0:T], vecs[:, 8 + m:9 + m], None, ALU.mult))
                for j in (1, 2):
                    step(V.scalar_tensor_tensor(out, conv_in[:, m, j:j + T], vecs[:, 8 + 4 * j + m:9 + 4 * j + m], out,
                                                ALU.mult, ALU.add))
            for m in range(4):
                dve.wait_ge(S["acc_done"], 20 + m + 1)
                V.tensor_tensor(mix_c[:, m, 0:T], bank[m][:, :], mix_c[:, m, 0:T], ALU.mult).then_inc(S["acc_dve"], 1)
                k_chunks(1)
            dve.wait_ge(S["samp_t"], 3)
            V.tensor_tensor(mix_c[:, :, T:T + B], bank[6][:, 0:C4 * B].rearrange("p (c b) -> p c b", c=C4),
                            mix_c[:, :, T:T + B], ALU.mult).then_inc(S["samp_g"], 1)

            def conv_norm(i):
                dve.wait_ge(S["cn_sqrt"], i + 1)
                n = C4 * B if i == 0 else T
                step(V.reciprocal(rt_c[:, 0:n], rt_c[:, 0:n]))
                if i == 0:
                    m = mix_c[:, :, T:T + B]
                    step(V.tensor_tensor(m, m, rt_c[:, 0:n].rearrange("p (c b) -> p c b", c=C4), ALU.mult))
                    V.tensor_tensor(m, m, spread(vecs[:, 4:8].rearrange("p (c o) -> p c o", o=1), [P, C4, B]), ALU.mult)\
                        .then_inc(S["mix_ready_c"], 1)
                else:
                    m = mix_c[:, i - 1, 0:T]
                    V.scalar_tensor_tensor(m, m, vecs[:, 3 + i:4 + i], rt_c[:, 0:n], ALU.mult, ALU.mult)\
                        .then_inc(S["mix_ready_c"], 1)

            def row_max(w):
                t = w // H
                n = (t + 1) * P
                dve.wait_ge(S["s_done"], w + 1)
                step(V.tensor_tensor(bank[w % 3][:, t * P:n], bank[w % 3][:, t * P:n], causal[:, :], ALU.add))
                if w >= 2:
                    dve.wait_ge(S["p_ready"], w - 1)
                V.reduce_max(neg_max[:, w % 2:w % 2 + 1], bank[w % 3][:, 0:n], AX.X, negate=True)\
                    .then_inc(S["max_ready"], 1)

            def attention_output(t):
                dve.wait_ge(S["pv_done"], H * (t + 1))
                sums = row_sum[:, (t % 2) * H:(t % 2 + 1) * H]
                step(V.reciprocal(sums, sums))
                if t:
                    dve.wait_ge(S["ot_done"], t)
                V.tensor_tensor(o_row[:, :, :], bank[5][:, :].rearrange("p (h d) -> p h d", h=H),
                                spread(sums.rearrange("p (h o) -> p h o", o=1), [P, H, HD]), ALU.mult)\
                    .then_inc(S["o_taken"], 1)

            def attention_squares(t):
                dve.wait_ge(S["o_sq_ready"], t + 1)
                V.reduce_sum(head_ssq[:, :], o_sq[:, :, :], AX.X).then_inc(S["o_ssq"], 1)

            def attention_norm(t):
                dve.wait_ge(S["o_sqrt"], t + 1)
                step(V.reciprocal(head_ssq[:, :], head_ssq[:, :]))
                V.tensor_tensor(o_row[:, :, :], o_row[:, :, :],
                                spread(head_ssq[:, :].rearrange("p (h o) -> p h o", o=1), [P, H, HD]), ALU.mult)\
                    .then_inc(S["o_ready"], 1)

            def spread_scale(j):
                if j == 4:
                    dve.wait_ge(S["g_loaded"], 32)
                dve.wait_ge(S["expand_done"], j + 5)
                lo = slice((j % 2) * SECS, (j % 2 + 1) * SECS)
                V.scalar_tensor_tensor(sc2_s[0:B, lo], bank[6][0:B, :], 1.0, g_b[0:B, lo], ALU.add, ALU.mult)
                V.scalar_tensor_tensor(sc2_p[:, lo], bank[7][:, :], 1.0, g_b[:, lo], ALU.add, ALU.mult)\
                    .then_inc(S["mod2_dve"], 1)

            def sample_softmax(i):
                flat = scores[:, :, :, :].rearrange("p b i h -> p (b i h)")
                if i == 0:
                    dve.wait_ge(S["k_used"], NKV)
                    dve.wait_ge(S["select_done"], 3)
                    step(V.scalar_tensor_tensor(flat, flat, SCALE, decay[:, :, :, :].rearrange("p b i h -> p (b i h)"),
                                                ALU.mult, ALU.add))
                if i == 1:
                    step(V.reduce_max(top[:, :, :], scores[:, :, :, :].rearrange("p b i h -> p b h i"), AX.X))
                    V.tensor_tensor(top[:, :, :], top[:, :, :], news[:, :, :], ALU.max).then_inc(S["softmax_in"], 1)
                if i == 2:
                    dve.wait_ge(S["top_ready"], 1)
                    V.tensor_tensor(p_new[:, :, :], news[:, :, :], top_all[:, :, :], ALU.subtract)\
                        .then_inc(S["softmax_in"], 1)
                    V.tensor_tensor(scores[:, :, :, :], scores[:, :, :, :],
                                    spread(top_all[:, :, :].rearrange("p b (o h) -> p b o h", o=1), [P, B, PPP, H]),
                                    ALU.subtract).then_inc(S["softmax_in"], 1)

            for w in range(NT * H):
                row_max(w)
                if w % H == 0 and w:
                    attention_output(w // H - 1)
                if w % H == 1 and w > H:
                    attention_squares(w // H - 1)
                if w % H == 2 and w > H:
                    attention_norm(w // H - 1)
                k_chunks(1)
                if w < 1 + C4:
                    conv_norm(w)
                if w >= SOFTMAX_AT:
                    sample_softmax(w - SOFTMAX_AT)
                if SPREAD_AT.get(w - 1) == 4:
                    spread_scale(4)
            spread_scale(5)
            attention_output(NT - 1)
            attention_squares(NT - 1)
            attention_norm(NT - 1)

            dve.wait_ge(S["p_ready"], NT * H)
            V.memset(bank[0][:, :], 0.0)
            V.memset(bank[1][:, :], 0.0).then_inc(S["zeroed"], 1)

            def residual(t):
                n = P if t < NT else B
                ga, sc, sh = (ga1_p, sc2_p, sh2_p) if t < NT else (ga1_s, sc2_s, sh2_s)
                for half in range(2):
                    lo = slice(half * 512, (half + 1) * 512)
                    dve.wait_ge(S["wo_done"], 2 * t + half + 1)
                    V.tensor_tensor(prod_o[0:n, lo], bank[4 + half][0:n, :], ga[0:n, lo], ALU.mult)\
                        .then_inc(S["wo_taken"], 1)
                dve.wait_ge(S["wo_taken"], 2 * t + 2)
                if t == 0:
                    dve.wait_ge(S["x_loaded"], 64)
                V.tensor_tensor(x_r[0:n, t, :], x_r[0:n, t, :], prod_o[0:n, :], ALU.add).then_inc(S["x1_ready"], 1)
                dve.wait_ge(S["norm_sqrt"], t + 1)
                step(V.reciprocal(rstd[0:n, t:t + 1], ssq[0:n, t:t + 1]))
                if t >= 2:
                    dve.wait_ge(h2_out[t % 2], 16 * (t // 2))
                    dve.wait_ge(S["h2_psum"], t - 1)
                r = h_row[t % 2]
                step(V.scalar_tensor_tensor(r[0:n, :], x_r[0:n, t, :], rstd[0:n, t:t + 1], sc[0:n, :], ALU.mult, ALU.mult))
                V.tensor_tensor(r[0:n, :], r[0:n, :], sh[0:n, :], ALU.add).then_inc(S["h2_ready"], 1)

            def own_heads(b):
                dve.wait_ge(S["pvs_done"], b + 1)
                if b >= 2:
                    dve.wait_ge(S["ot2_done"], b - 1)
                V.tensor_tensor(o_m[b % 2][:, :], bank[b % 2][:, :], head_mask[:, :], ALU.mult).then_inc(S["om_ready"], 1)

            def logits(t):
                n = P if t < NT else B
                dve.wait_ge(S["lg_done"], t + 1)
                V.tensor_tensor(lg[0:n, t, :], bank[3][0:n, t * 36:(t + 1) * 36], b_r[0:n, :], ALU.add)\
                    .then_inc(S["lg_taken"], 1)

            dve.wait_ge(S["wr_loaded"], 64)
            step(V.memset(lg[:, :, :], 0.0))
            for t in range(NT):
                residual(t)
                if t == 0:
                    dve.wait_ge(S["exp_ready"], B)
                    step(V.reduce_sum(p_sum[:, :, :], scores[:, :, :, :].rearrange("p b i h -> p b h i"), AX.X))
                    V.tensor_tensor(p_sum[:, :, :], p_sum[:, :, :], p_new[:, :, :], ALU.add).then_inc(S["softmax_in"], 1)
                own_heads(2 * t)
                own_heads(2 * t + 1)
                logits(t)
            dve.wait_ge(S["samp_norm_psum"], 1)
            dve.wait_ge(S["ot2_done"], B)
            c3 = lambda lo: bank[2][:, lo:lo + C4 * B].rearrange("p (c b) -> p c b", c=C4)
            step(V.reciprocal(o_r[:, :, :], c3(64)))
            V.tensor_tensor(o_t[:, :, :], c3(0), o_r[:, :, :], ALU.mult).then_inc(S["samp_norm_dve"], 1)
            dve.wait_ge(S["samp_norm_act"], 2)
            step(V.reciprocal(o_r[:, :, :], o_r[:, :, :]))
            step(V.tensor_tensor(o_t[:, :, :], o_t[:, :, :], o_r[:, :, :], ALU.mult))
            V.tensor_tensor(mix_a[:, :, T:T + B], o_t[:, :, :],
                            spread(vecs[:, 0:C4].rearrange("p (c o) -> p c o", o=1), [P, C4, B]), ALU.mult)\
                .then_inc(S["samp_norm_dve"], 1)
            dve.wait_ge(S["wo_part_done"], 1)
            V.tensor_copy(o_m[0][:, :], bank[0][:, :]).then_inc(S["samp_norm_dve"], 1)
            residual(NT)
            logits(NT)

            dve.wait_ge(S["lg_taken"], 5)
            dve.wait_ge(h2_out[0], 48)
            dve.wait_ge(h2_out[1], 32)
            dve.wait_ge(S["h2_psum"], 5)
            one = lambda i: st[:, i, :]
            wide = lambda i, n: spread(st[:, i, :].rearrange("p (t o) -> p t o", o=1), [P, 5, n])
            gl = lg[:, :, 0:NG]
            step(V.reduce_max(one(0), gl, AX.X))
            V.tensor_tensor(ge[:, :, :], gl, wide(0, NG), ALU.subtract).then_inc(S["route_in"], 1)

            def first_of(out, values, top_value, n):
                step(V.reduce_max(one(top_value), values, AX.X))
                step(V.tensor_tensor(out, values, wide(top_value, n), ALU.is_equal))
                d = spread(desc[:, 8 - n:8].rearrange("p (o n) -> p o n", o=1), [P, 5, n])
                step(V.tensor_tensor(out, out, d, ALU.mult))
                step(V.reduce_max(one(11), out, AX.X))
                step(V.tensor_tensor(out, out, wide(11, n), ALU.is_equal))

            dve.wait_ge(S["route_consts"], 1)
            first_of(g_oh[:, :, :], gl, 1, NG)
            wide_g = spread(g_oh[:, :, :].rearrange("p t (g o) -> p t g o", o=1), [P, 5, NG, EPG])
            step(V.tensor_tensor(els[:, :, :, :], lg[:, :, NG:NG + NE].rearrange("p t (g e) -> p t g e", g=NG), wide_g, ALU.mult))
            step(V.reduce_sum(el[:, :, :], els[:, :, :, :].rearrange("p t g e -> p t e g"), AX.X))
            step(V.reduce_max(one(2), el[:, :, :], AX.X))
            V.tensor_tensor(el[:, :, :], el[:, :, :], wide(2, EPG), ALU.subtract).then_inc(S["route_in"], 1)
            dve.wait_ge(S["route_exp"], 1)
            step(V.reduce_sum(one(3), ge[:, :, :], AX.X))
            step(V.reciprocal(one(3), one(3)))
            dve.wait_ge(S["route_exp"], 2)
            first_of(e_c[:, 0, :, :], el[:, :, :], 4, EPG)
            step(V.tensor_tensor(e_t[:, :, :], el[:, :, :], e_c[:, 0, :, :], ALU.mult))
            step(V.tensor_tensor(el[:, :, :], el[:, :, :], e_t[:, :, :], ALU.subtract))
            step(V.tensor_tensor(el[:, :, :], el[:, :, :], e_c[:, 0, :, :], ALU.subtract))
            first_of(e_c[:, 1, :, :], el[:, :, :], 5, EPG)
            step(V.tensor_tensor(one(6), one(4), one(5), ALU.add))
            step(V.reciprocal(one(6), one(6)))
            step(V.tensor_tensor(one(6), one(6), one(3), ALU.mult))
            for c in range(2):
                step(V.tensor_tensor(one(7 + c), one(4 + c), one(6), ALU.mult))
                step(V.tensor_tensor(oh[:, c, :, :].rearrange("p t (g e) -> p t g e", g=NG), wide_g,
                                     spread(e_c[:, c, :, :].rearrange("p t (o e) -> p t o e", o=1), [P, 5, NG, EPG]),
                                     ALU.mult))
            V.tensor_tensor(both[:, :, :], oh[:, 0, :, :], oh[:, 1, :, :], ALU.add).then_inc(S["route_in"], 1)
            for c in range(2):
                step(V.tensor_scalar(one(9), tok2[:, :], 2.0, 2.0 * c - FAR, ALU.mult, ALU.add))
                for k, s in ((1, 9), (2, 7 + c)):
                    V.tensor_tensor(vals[:, c, :, k * NE:(k + 1) * NE], oh[:, c, :, :], wide(s, NE), ALU.mult)
                step(V.tensor_tensor(vals[:, c, :, 0:NE], oh[:, c, :, :],
                                     spread(tok2[:, :].rearrange("p (t o) -> p t o", o=1), [P, 5, NE]), ALU.mult))
            dve.wait_ge(S["rank_done"], 1)
            step(V.tensor_copy(rank_e[:, :, :], bank[0][:, 0:5 * NE].rearrange("p (t e) -> p t e", t=5)))
            step(V.reduce_max(cnt_max[:, 0:1], bank[1][:, 0:NE], AX.X))
            V.tensor_copy(max_count[0:1, 0:1], cnt_max[0:1, 0:1]).then_inc(S["count_ready"], 1)
            for c in range(2):
                step(V.tensor_tensor(els[:, :, :, :].rearrange("p t g e -> p t (g e)"), rank_e[:, :, :], oh[:, c, :, :], ALU.mult))
                step(V.reduce_sum(rank[:, c, :], els[:, :, :, :].rearrange("p t g e -> p t (g e)"), AX.X))

            def slots():
                for c in range(2):
                    last = V.tensor_tensor(slot_is[:, c, :, :],
                                           spread(slot_no[:, :].rearrange("p (o n) -> p o n", o=1), [P, 5, P]),
                                           spread(rank[:, c, :].rearrange("p (t o) -> p t o", o=1), [P, 5, P]), ALU.is_equal)
                return last

            def read_tables():
                V.tensor_scalar(g_idx[:, :], bank[2][:, 0:NE], half_no[:, 0:1], None, ALU.add)
                V.tensor_scalar(s_idx[:, :], bank[2][:, NE:2 * NE], far_half[:, 0:1], None, ALU.add)
                return V.tensor_copy(tabs[:, :], bank[2][:, 2 * NE:3 * NE])

            slots().then_inc(S["vals_ready"], 1)
            dve.wait_ge(S["tabs_done"], 1)
            read_tables().then_inc(S["tabs_ready"], 1)
            V.memset(cnt[:, :], 0.0).then_inc(S["y_ready"], 2)

            def hidden(xs):
                return V.tensor_tensor(hid[xs][:, :], sig[xs][:, :], bank[2 + xs][SLOTS:2 * SLOTS, 0:DE], ALU.mult)

            def hidden_out(xs):
                return V.tensor_copy(hid_t[xs][:, :, :], bank[2 + xs][:, 256:256 + 2 * SLOTS].rearrange("p (k n) -> p k n", k=2))

            def weighted(xs, e):
                return V.tensor_scalar(y_e[xs][:, :], bank[4 + xs][:, :], tabs[:, bass.ds(e, 1)], None, ALU.mult)

            def four_experts(g):
                for s in range(4):
                    xs, e = s % 2, 4 * g + s
                    dve.wait_ge(S["sig_ready"], e + 1)
                    hidden(xs).then_inc(S["hid_ready"], 1)
                    dve.wait_ge(S["hidt_done"], e + 1)
                    hidden_out(xs).then_inc(S["hidt_ready"], 1)
                    dve.wait_ge(S["y_done"], e + 1)
                    if not isinstance(e, int) or e >= 2:
                        dve.wait_ge(y_stored[xs], (2 * g + s // 2) * 16)
                    weighted(xs, e).then_inc(S["y_ready"], 1)

            four_experts(0)
            with dve.Fori(1, NE // 4) as g:
                four_experts(g)
            count = dve.value_load(max_count[0:1, 0:1], min_val=0, max_val=2 * (T + B))
            with dve.If(count > cap):
                with dve.Fori(1, PASSES) as p:
                    dve.wait_ge(y_stored[0], (p - 1) * NE * 16 + STORED)
                    dve.wait_ge(y_stored[1], STORED)
                    V.tensor_scalar(slot_no[:, :], slot_no[:, :], float(SLOTS), None, ALU.add).then_inc(S["ov_slots"], 1)
                    dve.wait_ge(S["ov_slots"], p)
                    slots().then_inc(S["vals_ready"], 1)
                    dve.wait_ge(S["tabs_done"], p + 1)
                    read_tables().then_inc(S["tabs_ready"], 1)
                    dve.wait_ge(S["tabs_done"], 2)
                    dve.wait_ge(S["tabs_ready"], p + 1)
                    with dve.Fori(0, NE) as e:
                        n = p * NE + e
                        dve.wait_ge(S["sig_ready"], n + 1)
                        hidden(0).then_inc(S["hid_ready"], 1)
                        dve.wait_ge(S["hidt_done"], n + 1)
                        hidden_out(0).then_inc(S["hidt_ready"], 1)
                        dve.wait_ge(S["y_done"], n + 1)
                        dve.wait_ge(y_stored[0], (n - NE) * 16 + STORED)
                        weighted(0, e).then_inc(S["y_ready"], 1)

            dve.wait_ge(S["g_loaded"], 48)
            for j in (4, 5):
                dve.wait_ge(S["expand_done"], j + 11)
                lo = slice((j % 2) * SECS, (j % 2 + 1) * SECS)
                V.scalar_tensor_tensor(scf_s[0:B, lo], bank[j % 2][0:B, :], 1.0, gf_b[0:B, lo], ALU.add, ALU.mult)
                step(V.scalar_tensor_tensor(scf_p[:, lo], bank[2 + j % 2][:, :], 1.0, gf_b[:, lo], ALU.add, ALU.mult))
            dve.wait_ge(S["mod3_ready"], 4)
            for i, t in enumerate((0, 1, 2, 3, NT)):
                n = P if t < NT else B
                ga, sc, sh = (ga2_p, scf_p, shf_p) if t < NT else (ga2_s, scf_s, shf_s)
                dve.wait_ge(yg_loaded[i], 16)
                y = y_g[i]
                step(V.tensor_tensor(y[0:n, 0, :], y[0:n, 0, :], y[0:n, 1, :], ALU.add))
                step(V.tensor_tensor(y[0:n, 0, :], y[0:n, 0, :], ga[0:n, :], ALU.mult))
                V.tensor_tensor(x_r[0:n, t, :], x_r[0:n, t, :], y[0:n, 0, :], ALU.add).then_inc(S["x1_ready"], 1)
                dve.wait_ge(S["norm_sqrt"], i + 6)
                step(V.reciprocal(rstd[0:n, t:t + 1], ssq[0:n, t:t + 1]))
                if i >= 2:
                    dve.wait_ge(y_out[i % 2], 16 * (i // 2))
                r = h_row[i % 2]
                step(V.scalar_tensor_tensor(r[0:n, :], x_r[0:n, t, :], rstd[0:n, t:t + 1], sc[0:n, :], ALU.mult, ALU.mult))
                V.tensor_tensor(r[0:n, :], r[0:n, :], sh[0:n, :], ALU.add).then_inc(S["fin_ready"], 1)

        @block.gpsimd
        def _(pool):
            G = nc.gpsimd
            steps = [0]

            def step(ins):
                steps[0] += 1
                ins.then_inc(S["pool_step"], 1)
                pool.wait_ge(S["pool_step"], steps[0])

            G.iota(lane[:, :], [[0, 1]], base=0, channel_multiplier=1).then_inc(S["consts_ready"], 1)
            G.memset(ones[:, :], 1.0)
            G.memset(eps[:, :], EPS)
            G.memset(ssq[:, :], 1.0)
            G.memset(h_t[:, :, T + B:HP], 0.0).then_inc(S["consts_ready"], 1)
            G.memset(ident[:, :], 0.0)
            G.memset(block64[:, :], 0.0)
            G.memset(sel[:, :, :], 0.0)
            G.memset(head_mask[:, :], 0.0)
            step(G.memset(causal[:, :], 0.0))
            G.memset(block64[0:64, 0:64], 1.0)
            step(G.memset(block64[64:128, 64:128], 1.0))
            G.affine_select(out=ident[:, :], in_=ident[:, :], compare_op=ALU.not_equal, fill=1.0, base=0,
                            pattern=[[-1, P]], channel_multiplier=1)
            G.affine_select(out=causal[:, :], in_=causal[:, :], compare_op=ALU.is_ge, fill=NEG, base=0,
                            pattern=[[-1, P]], channel_multiplier=1)
            G.affine_select(out=later[:, :], in_=ones[:, :], compare_op=ALU.is_gt, fill=0.0, base=0,
                            pattern=[[-1, P]], channel_multiplier=1)
            G.affine_select(out=earlier[:, :], in_=ones[:, :], compare_op=ALU.is_gt, fill=0.0, base=0,
                            pattern=[[1, P]], channel_multiplier=-1)
            for j in range(4):
                G.affine_select(out=sel[:, :, :], in_=sel[:, :, :], compare_op=ALU.not_equal, fill=1.0, base=-32 * j,
                                pattern=[[-1, B + 1], [0, P]], channel_multiplier=1)
                hm = head_mask[:, :].rearrange("p (h d) -> p h d", h=H)
                step(G.affine_select(out=hm, in_=hm, compare_op=ALU.not_equal, fill=1.0, base=-32 * j,
                                     pattern=[[-1, H], [0, HD]], channel_multiplier=1))
            G.memset(conv_in[:, :, 0:2], 0.0).then_inc(S["consts_ready"], 1)
            pool.wait_ge(S["consts_ready"], 3)
            G.memset(small_one[:, :], 1.0).then_inc(S["consts_ready"], 1)

            pool.wait_ge(S["setup_ready"], 3)
            f_view = decay[:, :, :, :].rearrange("p b i h -> p b (i h)")
            for b in range(B):
                pool.indirect_dma_start(f_view[:, b, :], None, f_rows, bass.IndirectOffsetOnAxis(f_index[:, b:b + 1], 0))\
                    .then_inc(S["f_loaded"], 16)

            def cache_chunk(g):
                n = g % NKV
                if g >= RING:
                    pool.wait_ge(*((S["k_used"], g - RING + 1) if g - RING < NKV else (S["v_used"], g - RING - NKV + 1)))
                pool.indirect_dma_start(kv_flat[:, g % RING, :], None, k_rows if g < NKV else v_rows,
                                        bass.IndirectOffsetOnAxis(kv_index[:, n:n + 1], 0))\
                    .then_inc(kv_loaded[g % RING], 16)

            for n in range(NKV):
                b, s = divmod(n, NCH)
                if s == 0:
                    if b == 0:
                        pool.wait_ge(S["h_row_ready"], 5)
                        pool.wait_ge(S["q_stored"], 16)
                    if b >= 2:
                        pool.wait_ge(S["k_used"], NCH * (b - 1))
                    pool.dma_start(q_b[:, b % 2, :], q_rows_dram[b:b + 1, :].to_broadcast([P, HW]))\
                        .then_inc(qb_loaded[b % 2], 16)
                cache_chunk(n)
                if 8 <= n < 13:
                    if n == 8:
                        pool.wait_ge(S["f_loaded"], 16 * B)
                    d = 1 << (n - 8)
                    if n > 8:
                        pool.wait_ge(S["decay_sum"], n - 8)
                    G.tensor_tensor(decay[:, :, 0:PPP - d, :], decay[:, :, 0:PPP - d, :], decay[:, :, d:PPP, :], ALU.add)\
                        .then_inc(S["decay_sum"], 1)
                if n == NEW_AT + RING - 1:
                    pool.wait_ge(S["select_in"], 1)
                    G.affine_select(out=news[0:B, :, :], in_=news[0:B, :, :], compare_op=ALU.is_equal, fill=NEG, base=0,
                                    pattern=[[-1, B], [0, H]], channel_multiplier=1).then_inc(S["select_done"], 1)
                if n == DIAG_AT + RING - 1:
                    pool.wait_ge(S["select_in"], 2)
                    G.affine_select(out=lf_diag[:, :, :], in_=lf_diag[:, :, :], compare_op=ALU.is_equal, fill=0.0, base=0,
                                    pattern=[[-1, B], [0, H]], channel_multiplier=1).then_inc(S["select_done"], 1)
            pool.wait_ge(S["tail_evac"], 1)
            wide_tail = tail[:, :, :].rearrange("p b (o h) -> p b o h", o=1)
            step(G.tensor_tensor(decay[:, :, 0:PPP - 1, :], decay[:, :, 1:PPP, :],
                                 wide_tail.to_broadcast([P, B, PPP - 1, H]), ALU.add))
            G.tensor_copy(decay[:, :, PPP - 1, :], tail[:, :, :]).then_inc(S["select_done"], 1)
            for g in range(NKV, NKV + RING):
                cache_chunk(g)
            pool.wait_ge(S["softmax_in"], 1)
            G.partition_all_reduce(top_all[:, :, :].rearrange("p b h -> p (b h)"), top[:, :, :].rearrange("p b h -> p (b h)"),
                                   P, RED.max).then_inc(S["top_ready"], 1)
            for g in range(NKV + RING, 2 * NKV):
                cache_chunk(g)

            pool.wait_ge(S["h2_psum"], 5)
            pool.wait_ge(S["lg_taken"], 5)
            pool.wait_ge(h2_out[0], 48)
            pool.wait_ge(h2_out[1], 32)
            G.iota(slot_no[:, :], [[0, 2], [1, SLOTS]], base=0, channel_multiplier=0, allow_small_or_imprecise_dtypes=True)
            G.iota(tok2[:, :], [[2 * P, 5]], base=0, channel_multiplier=2, allow_small_or_imprecise_dtypes=True)
            G.iota(desc[:, :], [[-1, EPG]], base=EPG, channel_multiplier=0, allow_small_or_imprecise_dtypes=True)
            step(G.memset(mark[:, :], 0.0))
            G.memset(half_no[0:SLOTS, :], 0.0)
            step(G.memset(half_no[SLOTS:P, :], 1.0))
            G.memset(far_half[0:SLOTS, :], FAR)
            G.memset(far_half[SLOTS:P, :], FAR + 1.0).then_inc(S["route_consts"], 1)
            pool.wait_ge(S["route_consts"], 1)

            def gather(xs, col):
                return pool.indirect_dma_start(x_e[xs][:, :], None, h2_dram, bass.IndirectOffsetOnAxis(col, 0))

            def scatter(xs, col):
                return pool.indirect_dma_start(y_dram, bass.IndirectOffsetOnAxis(col, 0), y_e[xs][:, :], None,
                                               bounds_check=4 * (T + B) - 1, oob_is_err=False)

            def columns(e):
                G.tensor_copy(e_cols[:, 0:1], g_idx[:, bass.ds(e, 1)])
                return G.tensor_copy(e_cols[:, 1:2], s_idx[:, bass.ds(e, 1)])

            def hold(signal, value, held):
                pool.wait_ge(S["ov_held"], held)
                pool.wait_ge(signal, value)
                G.tensor_tensor(mark[:, :], mark[:, :], mark[:, :], ALU.add).then_inc(S["ov_held"], 1)

            pool.wait_ge(S["tabs_ready"], 1)
            pool.wait_ge(h2_out[0], 48)
            pool.wait_ge(h2_out[1], 32)
            for e in range(NE):
                xs = e % 2
                if e >= 2:
                    pool.wait_ge(S["xe_done"], e - 1)
                gather(xs, g_idx[:, e:e + 1]).then_inc(xe_loaded[xs], 16)
                if e >= 2:
                    pool.wait_ge(S["y_ready"], e + 1)
                    scatter(xs, s_idx[:, e - 2:e - 1]).then_inc(y_stored[xs], 16)
            for e in (NE - 2, NE - 1):
                pool.wait_ge(S["y_ready"], e + 3)
                scatter(e % 2, s_idx[:, e:e + 1]).then_inc(y_stored[e % 2], 16)
            count = pool.value_load(max_count[0:1, 0:1], min_val=0, max_val=2 * (T + B))
            with pool.If(count > cap):
                pool.sem_inc(S["ov_held"], 1)
                with pool.Fori(1, PASSES) as p:
                    with pool.Fori(0, NE) as e:
                        n = p * NE + e
                        pool.wait_ge(S["tabs_ready"], p + 1)
                        pool.wait_ge(y_stored[0], (n - NE) * 16 + STORED)
                        columns(e).then_inc(S["ov_cols"], 1)
                        hold(S["ov_cols"], n - NE + 1, 2 * (n - NE) + 1)
                        gather(0, e_cols[:, 0:1]).then_inc(xe_loaded[0], 16)
                        hold(S["y_ready"], n + 3, 2 * (n - NE) + 2)
                        scatter(0, e_cols[:, 1:2]).then_inc(y_stored[0], 16)
                pool.wait_ge(y_stored[0], (PASSES - 1) * NE * 16 + STORED)
            pool.wait_ge(y_stored[0], STORED)
            pool.wait_ge(y_stored[1], STORED)
            pool.sem_inc(S["y_all"], 1)

        @block.sync
        def _(sp):
            def unit(u):
                if u >= 3:
                    f = u - 3
                    if f < 8:
                        sp.wait_ge(S["unit_used"], f + 1)
                    elif f < 20:
                        s, half = divmod(f - 8, 2)
                        if half == 0:
                            sp.wait_ge(S["unit_used"], 8 + s + 1)
                        else:
                            sp.wait_ge(S["acc_done"], 4 * (s + 1))
                    else:
                        sp.wait_ge(S["unit_used"], 14 + f - 20 + 1)
                half = u % 2
                if u < 8:
                    v, lo = chunk_sec[u // 2]
                elif u < 20:
                    v, lo = w_in_v, sec_col[(u - 8) // 2]
                else:
                    v, lo = chunk_sec[4 + (u - 20) // 2]
                sp.dma_start(w_unit[:, u % 3], v[:, 4 * half:4 * half + 4, lo:lo + SECS]).then_inc(unit_loaded[u % 3], 16)

            row = lambda a: a.rearrange("(o n) -> o n", o=1)
            sp.dma_start(c_row[0:B, :], c_sample).then_inc(S["c_loaded"], 16)
            sp.dma_start(c_row[B:B + 1, :], c_prompt).then_inc(S["c_loaded"], 16)
            sp.dma_start(pt_int[:, :], page_table).then_inc(S["pt_loaded"], 16)
            sp.dma_start(b_row_a[:, :], b_ada[0:1, 0:4 * SECS]).then_inc(S["ba_loaded"], 16)
            unit(0)
            unit(1)
            sp.dma_start(x_a[0:B, NT, :], x_sample.rearrange("b t d -> (b t) d")).then_inc(S["x_loaded"], 16)
            sp.dma_start(x_a[:, 0:NT, :], x_prompt.rearrange("b (t p) d -> (b p) t d", p=P)).then_inc(S["x_loaded"], 16)
            unit(2)
            sp.dma_start(g1_b[:, :], g_norm1.to_broadcast([P, D])).then_inc(S["g_loaded"], 16)
            sp.dma_start(vec_rows[0:4, :], g_attn_out.rearrange("l (c a) d -> (l c) (a d)", a=2)).then_inc(S["vec_loaded"], 16)
            sp.dma_start(vec_rows[4:8, :], g_conv_out.rearrange("l (c a) d -> (l c) (a d)", a=2)).then_inc(S["vec_loaded"], 16)
            sp.dma_start(vec_rows[8:20, :], conv_w.rearrange("l j (c p) -> (l j c) p", p=P)).then_inc(S["vec_loaded"], 16)
            sp.dma_start(b_f[:, :], b_forget.rearrange("l h -> h l")).then_inc(S["vec_loaded"], 16)
            sp.dma_start(conv_sample[0, :, 0, :], state_conv[0, :, 1, :]).then_inc(S["state_out"], 16)
            for u in range(3, 8):
                unit(u)
            for u in range(8, 20):
                unit(u)
                if u == 11:
                    sp.wait_ge(S["h_row_ready"], 5)
                    sp.dma_start(w_f[:, :, :], w_in_v[:, :, f_col:f_col + H]).then_inc(S["wf_loaded"], 16)
                    sp.dma_start(state_rows[:, :], state_conv.rearrange("l b j c -> (l b j) c")).then_inc(S["st_loaded"], 16)
            for n in range(12):
                for half in range(2):
                    unit(20 + 2 * n + half)
                if n >= 2:
                    sp.wait_ge(S["ada_done"], 4 + n - 1)
                else:
                    sp.wait_ge(S["acc_done"], 24)
                    sp.wait_ge(S["samp_done"], 6)
                src = b_ada[0:1, (4 + n) * SECS:(5 + n) * SECS] if n < 8 else row(b_ada_final[(n - 8) * SECS:(n - 7) * SECS])
                sp.dma_start(b_row[:, (n % 2) * SECS:(n % 2 + 1) * SECS], src).then_inc(b_loaded[n % 2], 16)
            sp.wait_ge(S["crow_done"], 1)
            sp.wait_ge(S["acc_dve"], 8)
            sp.wait_ge(S["samp_g"], 2)
            sp.dma_start(g_b[:, :], g_norm2.to_broadcast([P, D])).then_inc(S["g_loaded"], 16)
            sp.wait_ge(S["ada_done"], 16)
            for lo, n, src in ((0, NG, w_router_group), (NG, NE, w_router_expert)):
                sp.dma_start(w_r[:, :, lo:lo + n], src.rearrange("l (p k) n -> (l p) k n", k=KD)).then_inc(S["wr_loaded"], 16)
            for lo, n, src in ((0, NG, b_router_group), (NG, NE, b_router_expert)):
                sp.dma_start(b_r[:, lo:lo + n], src.to_broadcast([P, n])).then_inc(S["wr_loaded"], 16)
            sp.wait_ge(S["s_done"], NT * H)
            sp.dma_start(wo[:, 0:C4, :], w_out_v[:, 0:C4, :]).then_inc(S["wo_attn_loaded"], 16)
            sp.wait_ge(S["pv_done"], NT * H)
            sp.dma_start(wo[:, C4:KD, :], w_out_v[:, C4:KD, :]).then_inc(S["wo_conv_loaded"], 16)
            sp.wait_ge(S["k_used"], NKV)
            sp.dma_start(x_r[0:B, NT, :], x_sample.rearrange("b t d -> (b t) d")).then_inc(S["x_loaded"], 16)
            sp.dma_start(x_r[:, 0:NT, :], x_prompt.rearrange("b (t p) d -> (b p) t d", p=P)).then_inc(S["x_loaded"], 16)

            wg = w_expert_gate.rearrange("l e (a p c) f -> (l e) p a (c f)", a=2, c=4)
            wu = w_expert_up.rearrange("l e (a p c) f -> (l e) p a (c f)", a=2, c=4)
            wd = w_expert_down.rearrange("l e (p k) n -> (l e) p (k n)", k=2)

            def gate_up(e, s):
                for o, src in ((0, wg), (2048, wu)):
                    sp.dma_start(exp_w[s][:, o:o + 2048].rearrange("p (a n) -> p a n", a=2), pick(src, e))\
                        .then_inc(gate_loaded[s], 16)

            def down(e, s):
                sp.dma_start(exp_w[s][:, 4096:6144], pick(wd, e)).then_inc(down_loaded[s], 16)

            def pick(src, e):
                if isinstance(e, int):
                    return src[e]
                v = src[bass.ds(e, 1)]
                return v.rearrange("o p a n -> (o p) a n") if len(v.shape) == 4 else v.rearrange("o p n -> (o p) n")

            free = {1: (S["v_used"], NKV), 2: (S["wo_part_done"], 2), 3: (S["wo_part_done"], 2), 0: (S["h2_ready"], 5)}
            for s in (1, 2, 3, 0):
                sp.wait_ge(*free[s])
                gate_up(s, s)
                down(s, s)
            with sp.Fori(1, NE // 4) as g:
                for s in range(4):
                    e = 4 * g + s
                    sp.wait_ge(S["gu_done"], e - 3)
                    gate_up(e, s)
                    sp.wait_ge(S["y_done"], e - 3)
                    down(e, s)
            sp.wait_ge(S["count_ready"], 1)
            count = sp.value_load(max_count[0:1, 0:1], min_val=0, max_val=2 * (T + B))
            with sp.If(count > cap):
                with sp.Fori(1, PASSES) as p:
                    with sp.Fori(0, NE) as e:
                        sp.wait_ge(S["y_done"], p * NE + e)
                        gate_up(e, 0)
                        down(e, 0)

            sp.dma_start(gf_b[:, :], row(g_final).to_broadcast([P, D])).then_inc(S["g_loaded"], 16)
            sp.wait_ge(S["y_all"], 1)
            sp.wait_ge(S["y_done"], NE)
            tok_rows = lambda lo, n: y_dram[4 * lo:4 * (lo + n), :].rearrange("(p a) d -> p (a d)", a=4)
            for i, t in enumerate((0, 1, 2, 3, NT)):
                n = P if t < NT else B
                sp.dma_start(y_g[i][0:n, :, :].rearrange("p a d -> p (a d)"), tok_rows(t * P, n)).then_inc(yg_loaded[i], 16)
            for i, t in enumerate((0, 1, 2, 3, NT)):
                n = P if t < NT else B
                dst = y_prompt[0, t * P:(t + 1) * P, :] if t < NT else y_sample.rearrange("b t d -> (b t) d")
                sp.wait_ge(S["fin_ready"], i + 1)
                sp.dma_start(dst, h_row[i % 2][0:n, :]).then_inc(y_out[i % 2], 16)
            sp.wait_ge(y_out[0], 48)
            sp.wait_ge(y_out[1], 32)
            sp.wait_ge(S["outs"], 16 * 7)
            sp.wait_ge(S["state_out"], 16)
            sp.wait_ge(krow_out[0], 32)
            sp.wait_ge(krow_out[1], 32)


_INS = ["x_prompt", "x_sample", "c_prompt", "c_sample", "cache_k", "cache_v", "cache_logf", "state_conv",
        "page_table", "w_ada", "b_ada", "g_norm1", "w_in", "b_forget", "conv_w", "g_attn_out", "g_conv_out",
        "w_out", "g_norm2", "w_router_group", "b_router_group", "w_router_expert", "b_router_expert",
        "w_expert_gate", "w_expert_up", "w_expert_down", "w_ada_final", "b_ada_final", "g_final"]
_OUTS = [(1, T, D), (B, 1, D), (1, 1, T, H, HD), (1, 1, T, H, HD), (1, 1, T, H), (1, 1, 2, HW),
         (1, B, 1, H, HD), (1, B, 1, H, HD), (1, B, 1, H), (1, B, 2, HW)]


def kernel(**inputs):
    import numpy as _np
    import concourse.bacc as _bacc
    from concourse import mybir as _mybir
    from concourse.bass_utils import run_bass_kernel_spmd as _run

    nc = _bacc.Bacc("TRN2", target_bir_lowering=False, num_devices=1)
    arrays, args = {}, []
    for name in _INS:
        a = _np.ascontiguousarray(inputs[name])
        arrays[f"in_{name}_dram"] = a
        args.append(nc.dram_tensor(f"in_{name}_dram", a.shape, _mybir.dt.from_np(a.dtype), kind="ExternalInput").ap())
    for i, shape in enumerate(_OUTS):
        args.append(nc.dram_tensor(f"out_{i}_dram", shape, F32, kind="ExternalOutput").ap())
    build(nc, *args)
    r = _run(nc, [arrays], core_ids=[0])
    return tuple(r.results[0][f"out_{i}_dram"] for i in range(len(_OUTS)))
```

```python
from contextlib import ExitStack

import concourse.bass as bass
from concourse import mybir

F32 = mybir.dt.float32
I32 = mybir.dt.int32
ALU = mybir.AluOpType
ACT = mybir.ActivationFunctionType
AX = mybir.AxisListType
RED = bass.bass_isa.ReduceOp

P = 128
D = 1024
KD = D // P
T = 512
NT = T // P
B = 8
H, HD = 8, 64
HW = H * HD
C4 = HW // P
NPG, PG = 32, 128
PPP = PG * NPG // P
CH = 4
NCH = PPP // CH
NKV = B * NCH
RING = 4
SCALE = HD ** -0.5
EPS = 1e-6
NEG = -1.0e30
NG, EPG = 4, 8
NE = NG * EPG
DE = 256
SLOTS = 64
PASSES = -(-(T + B) // SLOTS)
FAR = 4096.0
HP = T + B + 24
SECS = 512


def build(nc, x_prompt, x_sample, c_prompt, c_sample, cache_k, cache_v, cache_logf, state_conv,
          page_table, w_ada, b_ada, g_norm1, w_in, b_forget, conv_w, g_attn_out, g_conv_out,
          w_out, g_norm2, w_router_group, b_router_group, w_router_expert, b_router_expert,
          w_expert_gate, w_expert_up, w_expert_down, w_ada_final, b_ada_final, g_final,
          y_prompt, y_sample, k_prompt, v_prompt, logf_prompt, conv_prompt, k_sample, v_sample,
          logf_sample, conv_sample, cap=SLOTS):
    ctx = ExitStack()
    with ctx:
        def sb(name, shape, dt=F32):
            return ctx.enter_context(nc.sbuf_tensor(name, shape, dt))

        def sem(name):
            return ctx.enter_context(nc.semaphore(name))

        q_rows_dram = nc.dram_tensor("q_rows_scratch", [B, HW], F32, kind="Internal").ap()
        h2_dram = nc.dram_tensor("h2_scratch", [2 * (T + B), D // 2], F32, kind="Internal").ap()
        y_dram = nc.dram_tensor("expert_rows_scratch", [4 * (T + B), D // 2], F32, kind="Internal").ap()

        k_rows = cache_k.rearrange("l n (g r) h d -> (l n g) (r h d)", r=CH)
        v_rows = cache_v.rearrange("l n (g r) h d -> (l n g) (r h d)", r=CH)
        f_rows = cache_logf.rearrange("l n (g r) h -> (l n g) (r h)", r=PPP)
        w_ada_v = w_ada.rearrange("l (k p) n -> (l p) k n", p=P)
        w_fin_v = w_ada_final.rearrange("(k p) n -> p k n", p=P)
        w_in_v = w_in.rearrange("l (k p) n -> (l p) k n", p=P)
        w_out_v = w_out.rearrange("l (k p) n -> (l p) k n", p=P)
        f_col = 3 * HW
        sec_col = [0, HW, 2 * HW, f_col + H, f_col + H + 2 * HW, f_col + H + HW]

        R_x = sb("R_x", [P, 5120])
        R_part = sb("R_part", [P, 6144])
        R_h = sb("R_h", [P, KD * HP])
        R_cm = sb("R_cm", [P, 8264])
        R_kv = sb("R_kv", [P, RING * CH * HW])
        R_w = sb("R_w", [P, 6144])
        R_q = sb("R_q", [P, 8192])
        R_t = sb("R_t", [P, 3584])

        def view(region, lo, dims, parts=P):
            n = 1
            for d in dims:
                n *= d
            v = region[0:parts, lo:lo + n]
            if len(dims) == 1:
                return v
            names = "abcd"[:len(dims)]
            return v.rearrange(f"p ({' '.join(names)}) -> p {' '.join(names)}",
                               **{c: d for c, d in zip(names[1:], dims[1:])})

        ident = sb("ident", [P, P])
        block64 = sb("block64", [P, P])
        later = sb("later", [P, P])
        earlier = sb("earlier", [P, P])
        ones = sb("ones", [P, P])
        causal = sb("causal", [P, P])
        sel = sb("sel", [P, B + 1, P])
        head_mask = sb("head_mask", [P, HW])
        vecs = sb("vecs", [P, 20])
        kv_index = sb("kv_index", [P, NKV], I32)
        f_index = sb("f_index", [P, B], I32)
        v_new = sb("v_new", [B, HW])
        eps = sb("eps", [P, 1])
        ssq = sb("ssq", [P, 5])
        rstd = sb("rstd", [P, 5])
        b_f = sb("b_f", [H, 1])
        neg_max = sb("neg_max", [P, 2])
        row_sum = sb("row_sum", [P, 2 * H])
        head_ssq = sb("head_ssq", [P, H])
        quarter = sb("quarter", [P, 10])
        max_count = sb("max_count", [1, 1], I32)
        small_one = sb("small_one", [P, 1])
        e_cols = sb("e_cols", [P, 2], I32)

        sh1_p, sc1_p, sh1_s, sc1_s, g1_b = (view(R_q, i * 1024, [1024]) for i in range(5))
        part_a = view(R_q, 5120, [4, 512])
        x_a = view(R_x, 0, [5, D])
        c_row = view(R_part, 0, [D], B + 1)
        c_t = view(R_q, 7680, [KD, 32])
        b_row_a = view(R_part, 1280, [2048], 1)
        vec_rows = view(R_part, 3328, [P], 20)
        pt_int = view(R_part, 3456, [NPG], B).bitcast(I32)
        pt_exp = view(R_part, 3488, [NPG, 4], B)
        lane = view(R_part, 3616, [1]).bitcast(I32)
        h_row = [view(R_t, i * 1024, [D]) for i in range(2)]
        junk = view(R_t, 2048, [D])
        h_t = view(R_h, 0, [KD, HP])
        q_t, k_t, v_r = (view(R_q, i * 2048, [C4, T]) for i in range(3))
        s_part = view(R_q, 6144, [3, HW])
        qk_new = view(R_part, 4096, [2, HW], B)
        u_part = view(R_part, 5120, [HW])
        qk_prod = view(R_part, 5632, [HW], B)
        conv_in = view(R_cm, 0, [C4, T + B + 2])
        mix_c = view(R_cm, 2088, [C4, T + B])
        scores = view(R_cm, 4168, [B, PPP, H])
        decay = view(R_cm, 6216, [B, PPP, H])
        prod = view(R_x, 0, [CH, HW])
        q_b = view(R_x, 2048, [2, HW])
        f_t = view(R_x, 3072, [T + B], H)
        f_a = view(R_x, 3592, [T + B], H)
        cum = view(R_x, 4112, [T], H)
        neg_cum = f_a
        w_f = view(R_x, 4624, [KD, H])
        k_row = [view(R_t, i * 512, [HW]) for i in range(NT)]
        c_rows = view(R_t, 1024, [HW], 2 + B)
        sq_c = view(R_part, 4096, [T])
        rt_c = view(R_part, 4608, [T])
        probs = [view(R_t, i * 512, [T]) for i in range(2)]
        probs_t = [view(R_t, 1024 + i * 512, [NT, P]) for i in range(2)]
        o_row = view(R_t, 2048, [H, HD])
        o_sq = view(R_t, 2560, [H, HD])
        news = view(R_t, 3072, [B, H])
        top = view(R_t, 3136, [B, H])
        top_all = view(R_t, 3200, [B, H])
        p_new = view(R_t, 3264, [B, H])
        p_sum = view(R_t, 3328, [B, H])
        lf_rows = view(R_t, 3392, [5, H])
        lf_diag = view(R_t, 3432, [B, H], B)
        tail = view(R_t, 3496, [B, H])
        state_t = view(R_part, 3620, [C4, B, 2])
        state_rows = view(R_part, 1280, [HW], 2 * B)
        y_tmp = view(R_part, 3684, [C4, B])
        kv_ring = view(R_kv, 0, [RING, CH, HW])
        kv_flat = view(R_kv, 0, [RING, CH * HW])
        w_unit = view(R_w, 0, [3, 4, SECS])
        part = view(R_part, 0, [12, SECS])
        mix_a = view(R_h, 0, [C4, T + B])
        o_m = [view(R_h, 2080 + i * 512, [HW]) for i in range(2)]
        o_t = view(R_h, 3104, [C4, B])
        o_q = view(R_h, 3136, [C4, B])
        o_r = view(R_h, 3168, [C4, B])
        x_r = view(R_x, 0, [5, D])
        wo = view(R_q, 0, [KD, D])
        ga1_p, sh2_p, sc2_p, ga1_s, sh2_s, sc2_s = (view(R_w, i * 1024, [D]) for i in range(6))
        g_b = view(R_cm, 0, [D])
        prod_o = view(R_t, 2048, [D])
        junk2 = view(R_part, 0, [D])
        h2_t = view(R_cm, 1024, [KD, P])
        w_r = view(R_h, 3200, [KD, NG + NE])
        b_r = view(R_h, 3488, [NG + NE])
        lg = view(R_h, 3524, [5, NG + NE])
        slot_is = view(R_t, 2048, [2, 5, P])
        vals = view(R_cm, 6216, [2, 5, 3 * NE])
        oh = view(R_cm, 7176, [2, 5, NE])
        both = view(R_cm, 7496, [5, NE])
        both_sum = view(R_t, 3392, [5, NE])
        rank_e = view(R_cm, 7656, [5, NE])
        els = view(R_cm, 7816, [5, NG, EPG])
        el = view(R_cm, 7976, [5, EPG])
        e_c = view(R_cm, 8016, [2, 5, EPG])
        e_t = view(R_cm, 8096, [5, EPG])
        ge = view(R_cm, 8136, [5, NG])
        g_oh = view(R_cm, 8156, [5, NG])
        st = view(R_cm, 8176, [12, 5])
        rank = view(R_cm, 8236, [2, 5])
        tok2 = view(R_cm, 8246, [5])
        desc = view(R_cm, 8251, [EPG])
        half_no = view(R_cm, 8259, [1])
        far_half = view(R_cm, 8260, [1])
        cnt_max = view(R_cm, 8261, [1])
        slot_no = view(R_part, 2176, [P])
        spare = view(R_part, 2304, [NE])
        tabs = view(R_part, 2048, [NE])
        g_idx = view(R_part, 2080, [NE]).bitcast(I32)
        mark = view(R_part, 2144, [1])
        s_idx = view(R_part, 2112, [NE]).bitcast(I32)
        exp_w = [view(r, 0, [6144]) for r in (R_kv, R_q, R_cm, R_w)]
        x_e = [view(R_t, i * 512, [512]) for i in range(4)]
        xe_t = [view(R_h, 1024 + i * 512, [4, 2, SLOTS]) for i in range(2)]
        sig = [view(R_h, 2048 + i * 256, [DE], SLOTS) for i in range(2)]
        hid = [view(R_h, 2560 + i * 256, [DE], SLOTS) for i in range(2)]
        hid_t = [view(R_h, 3072 + i * 128, [2, SLOTS]) for i in range(2)]
        y_e = [view(R_h, lo, [512]) for lo in (0, 512, 3328, 3840)]
        y_g = [view(R_w, i * 2048, [2, D]) for i in range(3)] + [view(R_kv, i * 2048, [2, D]) for i in range(2)]
        ga2_p, ga2_s = (view(R_kv, 6144 + i * 1024, [D]) for i in range(2))
        shf_p, shf_s = (view(R_q, 6144 + i * 1024, [D]) for i in range(2))
        scf_p, scf_s = (view(R_part, 3072 + i * 1024, [D]) for i in range(2))
        gf_b = view(R_part, 1024, [D])

        bank = [ctx.enter_context(nc.psum_tensor(f"bank{i}", [P, 512], F32)) for i in range(8)]

        def value_bank(b):
            return bank[7] if b == 0 else bank[b % 2]

        names = """mod_spread mod_scaled side_turned k_products krow_out wo_part_done ov_held unit_used ada_done consts_ready setup_ready setup_psum
            c_silu vec_loaded ba_loaded part_ready sh_ready expand_done h_row_ready ht_ready h_psum
            samp_evac samp_done row_evac row_done samp_u samp_g samp_t acc_act acc_dve acc_done
            krow_evac krow_done wf_loaded f_done lf_ready lf_evac crow_evac
            st_evac sq_ready cn_done cn_sqrt decay_sum select_done tail_done p_ready s_done pt_ready
            pt_done o_taken pv_done o_ready mix_ready ot_done tail_evac wo_attn_loaded
            wo_conv_loaded mix_ready_c wo_taken samp_norm_dve wo_done h2_ready h2t_ready h2_psum
            wr_loaded lg_done exp_ready zeroed pnew_ready om_ready v_used pvs_done ot2_done
            softmax_in samp_norm_psum samp_norm_act route_in rank_done vals_ready tabs_done xe_done
            xet_ready gu_done hid_ready hidt_done hidt_ready y_ready y_done tabs_ready 
            act_step c_loaded x_loaded rstd_sq q_stored outs f_taken ln_ready max_ready o_sq_ready
            o_ssq o_sqrt x1_ready norm_sqrt route_exp sig_ready dve_step pt_loaded g_loaded k_used
            select_in top_ready lg_taken count_ready ov_slots fin_ready pool_step
            f_loaded y_all""".split()
        S = {n: sem(n) for n in names}
        unit_loaded = [sem(f"unit_loaded{i}") for i in range(3)]
        b_loaded = [sem(f"bias_loaded{i}") for i in range(2)]
        kv_loaded = [sem(f"kv_loaded{i}") for i in range(RING)]
        qb_loaded = [sem(f"qb_loaded{i}") for i in range(2)]
        h2_out = [sem(f"h2_out{i}") for i in range(2)]
        gate_loaded = [sem(f"gate_loaded{i}") for i in range(4)]
        down_loaded = [sem(f"down_loaded{i}") for i in range(4)]
        xe_loaded = [sem(f"xe_loaded{i}") for i in range(4)]
        y_stored = [sem(f"y_stored{i}") for i in range(4)]
        yg_loaded = [sem(f"yg_loaded{i}") for i in range(5)]
        y_out = [sem(f"y_out{i}") for i in range(2)]

        block = ctx.enter_context(nc.Block())
        sel8 = sel[:, 0:B, 0]
        chunk_sec = [(w_ada_v, n * SECS) for n in range(12)] + [(w_fin_v, n * SECS) for n in range(4)]
        STORED = 16 * (NE // 4)
        NEW_AT, DIAG_AT = 16, 32

        ADA_AT = {w: n for n, w in enumerate((0, 1, 3, 4, 6, 8, 10, 12, 14, 16, 19, 22))}
        SPREAD_AT = {24: 0, 25: 1}
        SPREAD_BESIDE_V = {8: 2, 10: 3, 11: 4, 13: 5}
        TILE_STEPS = 13
        TURN_AT = 5
        CONSTS_AT = 28
        V_EARLY = 3
        SOFTMAX_AT = 25

        @block.tensor
        def _(pe):
            def use_unit(u):
                pe.wait_ge(unit_loaded[u % 3], 16 * (u // 3 + 1))
                return w_unit[:, u % 3]

            def ada_chunk(n, psum, brow=None):
                for half in range(2):
                    u = (2 * n if n < 4 else 12 + 2 * n) + half
                    w = use_unit(u)
                    for j in range(4):
                        last = nc.tensor.matmul(psum[32 * j:32 * j + 32, :], c_t[:, 4 * half + j, :], w[:, j, :],
                                                start=(half == 0), stop=(half == 1 and (j > 0 or brow is None)))
                    if half == 0 or brow is not None:
                        last.then_inc(S["unit_used"], 1)
                if brow is None:
                    last.then_inc(S["ada_done"], 1)
                else:
                    nc.tensor.matmul(psum[0:B + 1, :], ones[0:1, 0:B + 1], brow, start=False, stop=True)\
                        .then_inc(S["ada_done"], 1)

            pe.wait_ge(S["consts_ready"], 3)
            pe.wait_ge(S["setup_ready"], 1)
            nc.tensor.matmul(bank[6][:, 32:32 + B], pt_exp[:, :, :].rearrange("p a b -> p (a b)"), ident[0:B, 0:B], start=True, stop=True)\
                .then_inc(S["setup_psum"], 1)
            pe.wait_ge(S["c_silu"], 1)
            for k in range(KD):
                last = nc.tensor.transpose(bank[7][:, 9 * k:9 * k + 9], c_row[:, k * P:(k + 1) * P],
                                           ident[0:B + 1, 0:B + 1])
            last.then_inc(S["setup_psum"], 1)
            pe.wait_ge(S["setup_ready"], 4)
            pe.wait_ge(S["ba_loaded"], 16)

            def expand_first(n):
                pe.wait_ge(S["part_ready"], n + 1)
                if n >= 2:
                    pe.wait_ge(S["sh_ready"], n - 1)
                nc.tensor.matmul(bank[2 + n % 2][0:B, :], sel8, part_a[:, n, :], start=True, stop=True)
                nc.tensor.matmul(bank[4 + n % 2][:, :], sel[:, B, :], part_a[:, n, :], start=True, stop=True)\
                    .then_inc(S["expand_done"], 1)

            for n in range(4):
                if n >= 2:
                    pe.wait_ge(S["part_ready"], n - 1)
                ada_chunk(n, bank[n % 2], b_row_a[:, n * SECS:(n + 1) * SECS])
                if n == 1:
                    pe.wait_ge(S["consts_ready"], 4)
                if n:
                    expand_first(n - 1)
            expand_first(3)

            def transpose_h(i):
                pe.wait_ge(S["h_row_ready"], i + 1)
                if i == 0:
                    for k in range(KD):
                        last = nc.tensor.transpose(bank[6][:, 64 + 8 * k:72 + 8 * k],
                                                   h_row[0][0:B, k * P:(k + 1) * P], ident[0:B, 0:B])
                else:
                    if i >= 3:
                        pe.wait_ge(S["ht_ready"], i - 1)
                    for k in range(KD):
                        last = nc.tensor.transpose(bank[(2 if i % 2 else 4) + k // 4][:, (k % 4) * P:(k % 4 + 1) * P],
                                                   h_row[i % 2][:, k * P:(k + 1) * P], ident[:])
                last.then_inc(S["h_psum"], 1)

            def sample_section(s):
                pe.wait_ge(S["ht_ready"], 1)
                pe.wait_ge(S["consts_ready"], 2)
                if s:
                    pe.wait_ge(S["samp_evac"], s)
                for half in range(2):
                    w = use_unit(8 + 2 * s + half)
                    for j in range(4):
                        last = nc.tensor.matmul(bank[7][32 * j:32 * j + 32, :],
                                                h_t[:, 4 * half + j, T:T + 32], w[:, j, :],
                                                start=(half == 0), stop=(half == 1))
                last.then_inc(S["samp_done"], 1)

            def sample_rows(s):
                pe.wait_ge(S["samp_evac"], s + 1)
                if s:
                    pe.wait_ge(S["row_evac"], s)
                nc.tensor.matmul(bank[6][0:B, :], sel8, s_part[:, s, :], start=True, stop=True)\
                    .then_inc(S["row_done"], 1)

            def sample_columns(s):
                pe.wait_ge(S["samp_evac"], s + 1)
                pe.wait_ge(*{3: (S["setup_ready"], 5), 4: (S["samp_u"], 1), 5: (S["samp_g"], 1)}[s])
                for c in range(C4):
                    last = nc.tensor.matmul(bank[6][:, c * B:(c + 1) * B], u_part[:, c * P:(c + 1) * P], sel8,
                                            start=True, stop=True)
                last.then_inc(S["samp_t"], 1)

            def prompt_section(s):
                for half in range(2):
                    w = use_unit(8 + 2 * s + half)
                    for m in range(4):
                        if half == 0:
                            if 1 <= s <= 4:
                                pe.wait_ge(S["acc_act"], 4 * (s - 1) + m + 1)
                            if s == 5:
                                pe.wait_ge(S["acc_dve"], m + 1)
                        for j in range(4):
                            k = 4 * half + j
                            if s == 2:
                                l, r = h_t[:, k, m * P:(m + 1) * P], w[:, j, :]
                            else:
                                l, r = w[:, j, m * P:(m + 1) * P], h_t[:, k, 0:T]
                            last = nc.tensor.matmul(bank[m][:, :], l, r, start=(k == 0), stop=(k == KD - 1))
                        if half:
                            last.then_inc(S["acc_done"], 1)
                    if half == 0:
                        last.then_inc(S["unit_used"], 1)

            transpose_h(0)
            sample_section(0)
            sample_rows(0)
            for i in range(1, 5):
                transpose_h(i)
            pe.wait_ge(S["ht_ready"], 5)
            prompt_section(0)
            for s in (1, 2):
                sample_section(s)
                prompt_section(s)
                sample_rows(s)
            pe.wait_ge(S["vec_loaded"], 64)
            pe.wait_ge(S["row_evac"], 3)
            nc.tensor.transpose(bank[6][:, 0:20], vec_rows[:, :], ident[0:20, 0:20]).then_inc(S["setup_psum"], 1)
            pe.wait_ge(S["acc_act"], 8)
            for t in range(NT):
                if t >= 2:
                    pe.wait_ge(S["krow_evac"], t - 1)
                for c in range(C4):
                    last = nc.tensor.transpose(bank[4 + t % 2][:, c * P:(c + 1) * P],
                                               k_t[:, c, t * P:(t + 1) * P], ident[:])
                last.then_inc(S["krow_done"], 1)
            pe.wait_ge(S["krow_evac"], 4)
            pe.wait_ge(S["wf_loaded"], 32)
            for k in range(KD):
                nc.tensor.matmul(bank[4][0:H, :], w_f[:, k, :], h_t[:, k, 0:T], start=(k == 0), stop=(k == KD - 1))
            for k in range(KD):
                last = nc.tensor.matmul(bank[5][0:H, 0:B], w_f[:, k, :], h_t[:, k, T:T + B],
                                        start=(k == 0), stop=(k == KD - 1))
            last.then_inc(S["f_done"], 1)
            sample_section(3)
            prompt_section(3)
            sample_columns(3)
            pe.wait_ge(S["lf_ready"], 1)
            for t in range(NT):
                nc.tensor.transpose(bank[4][:, t * H:(t + 1) * H], f_t[:, t * P:(t + 1) * P], ident[0:H, 0:H])
            nc.tensor.transpose(bank[4][0:B, 32:32 + H], f_t[:, T:T + B], ident[0:H, 0:H]).then_inc(S["side_turned"], 1)
            for c in range(C4):
                last = nc.tensor.transpose(bank[5][:, c * 16:(c + 1) * 16], state_rows[:, c * P:(c + 1) * P],
                                           ident[0:16, 0:16])
            last.then_inc(S["side_turned"], 1)
            sample_section(4)
            prompt_section(4)
            sample_columns(4)
            sample_section(5)
            prompt_section(5)
            sample_columns(5)
            pe.wait_ge(S["acc_dve"], 4)
            pe.wait_ge(S["samp_g"], 1)
            pe.wait_ge(S["lf_evac"], 2)
            for c in range(C4):
                last = nc.tensor.transpose(bank[4][0:2 + B, c * P:(c + 1) * P], conv_in[:, c, T:T + 2 + B], ident[:])
            last.then_inc(S["side_turned"], 1)
            def score(w):
                t, h = divmod(w, H)
                n, c, o = (t + 1) * P, h // 2, (h % 2) * HD
                if w >= 3:
                    pe.wait_ge(S["p_ready"], w - 2)
                out = bank[w % 3][:, 0:n]
                nc.tensor.matmul(out, q_t[o:o + HD, c, t * P:(t + 1) * P], k_t[o:o + HD, c, 0:n], start=True, stop=False)
                nc.tensor.matmul(out, sel[0:H, h, :], neg_cum[:, 0:n], start=False, stop=True).then_inc(S["s_done"], 1)

            def turn(w):
                t = w // H
                pe.wait_ge(S["p_ready"], w + 1)
                if w >= 2:
                    pe.wait_ge(S["pt_ready"], w - 1)
                for b in range(t + 1):
                    last = nc.tensor.transpose(bank[3 + w % 2][:, b * P:(b + 1) * P],
                                               probs[w % 2][:, b * P:(b + 1) * P], ident[:])
                last.then_inc(S["pt_done"], 1)

            def weigh(w):
                t, h = divmod(w, H)
                pe.wait_ge(S["pt_ready"], w + 1)
                if h == 0 and t:
                    pe.wait_ge(S["o_taken"], t)
                for b in range(t + 1):
                    last = nc.tensor.matmul(bank[5][:, h * HD:(h + 1) * HD], probs_t[w % 2][:, b, :],
                                            v_r[:, b, h * HD:(h + 1) * HD], start=(b == 0), stop=(b == t))
                last.then_inc(S["pv_done"], 1)

            def turn_output(t):
                pe.wait_ge(S["o_ready"], t + 1)
                if t == 2:
                    pe.wait_ge(S["mod_spread"], 2)
                if t:
                    pe.wait_ge(S["mix_ready"], t)
                for c in range(C4):
                    last = nc.tensor.transpose(bank[6][:, c * P:(c + 1) * P],
                                               o_row[:, :, :].rearrange("p a b -> p (a b)")[:, c * P:(c + 1) * P],
                                               ident[:])
                last.then_inc(S["ot_done"], 1)

            def conv_sums(i):
                pe.wait_ge(S["sq_ready"], i + 1)
                n = C4 * B if i == 0 else T
                nc.tensor.matmul(bank[6][:, 0:n], block64[:], sq_c[:, 0:n], start=True, stop=True)\
                    .then_inc(S["cn_done"], 1)

            def tail_sums():
                pe.wait_ge(S["cn_sqrt"], 1 + C4)
                pe.wait_ge(S["decay_sum"], 5)
                pe.wait_ge(S["select_done"], 2)
                nc.tensor.matmul(bank[6][:, 0:B * H], later[:], decay[:, :, 0, :], start=True, stop=False)
                nc.tensor.matmul(bank[6][:, 0:B * H], ones[0:B, :], lf_diag[:, :, :].rearrange("p a b -> p (a b)"),
                                 start=False, stop=True).then_inc(S["tail_done"], 1)

            def spread_chunk(j):
                if j == 0:
                    pe.wait_ge(S["part_ready"], 16)
                    pe.wait_ge(b_loaded[0], 16)
                    pe.wait_ge(S["mix_ready"], 2)
                elif j < 5:
                    pe.wait_ge(S["mod_spread"], j)
                if j == 2:
                    pe.wait_ge(S["mix_ready"], NT)
                    pe.wait_ge(S["om_ready"], 1)
                if j == 5:
                    pe.wait_ge(S["mod_scaled"], 1)
                nc.tensor.matmul(bank[6][0:B, :], sel8, part[:, j, :], start=True, stop=True)
                nc.tensor.matmul(bank[7][:, :], sel[:, B, :], part[:, j, :], start=True, stop=True)\
                    .then_inc(S["expand_done"], 1)

            def value_chunk(g):
                b, c = divmod(g, NCH)
                if c == 0:
                    pe.wait_ge(S["exp_ready"], b + 1)
                    if b < 2:
                        pe.wait_ge(S["zeroed"], b + 1)
                    if b >= 2:
                        pe.wait_ge(S["om_ready"], b - 1)
                n = NKV + g
                pe.wait_ge(kv_loaded[n % RING], 16 * (n // RING + 1))
                out = value_bank(b)
                for j in range(CH):
                    last = nc.tensor.matmul(out[32 * j:32 * j + H, :], scores[:, b, c * CH + j, :],
                                            kv_ring[:, n % RING, j, :], start=(c == 0),
                                            stop=(c == NCH - 1 and j > 0))
                last.then_inc(S["v_used"], 1)
                if c == NCH - 1:
                    pe.wait_ge(S["pnew_ready"], 1)
                    nc.tensor.matmul(out[0:H, :], p_new[0:B, b, :], v_new[:], start=False, stop=True)\
                        .then_inc(S["pvs_done"], 1)

            pe.wait_ge(S["acc_dve"], 8)
            pe.wait_ge(S["samp_evac"], 6)
            pe.wait_ge(S["samp_g"], 2)
            pe.wait_ge(S["crow_evac"], 1)
            pe.wait_ge(S["st_evac"], 1)
            score(0)
            score(1)
            for w in range(NT * H):
                turn(w)
                if w + 2 < NT * H:
                    score(w + 2)
                if w >= NT * H - V_EARLY:
                    value_chunk(w - (NT * H - V_EARLY))
                weigh(w)
                if w < 1 + C4:
                    conv_sums(w)
                if w == 1 + C4:
                    tail_sums()
                if w in SPREAD_AT:
                    spread_chunk(SPREAD_AT[w])
                if w in ADA_AT:
                    n = ADA_AT[w]
                    if n:
                        pe.wait_ge(S["part_ready"], 4 + n)
                    ada_chunk(4 + n, bank[7])
                if w % H == 3 and w > H:
                    if w // H == 1:
                        pe.wait_ge(S["tail_evac"], 1)
                    turn_output(w // H - 1)

            def out_part(t, half, k0):
                if t == 0 and half == 0:
                    pe.wait_ge(*((S["wo_attn_loaded"], 16) if k0 < C4 else (S["wo_conv_loaded"], 32)))
                    pe.wait_ge(S["mix_ready"], NT)
                    pe.wait_ge(S["mix_ready_c"], 1 + C4)
                if t and k0 == 0:
                    pe.wait_ge(S["wo_taken"], 2 * t)
                for k in (k0, k0 + 1):
                    m = (mix_a[:, k, t * P:(t + 1) * P] if k < C4 else mix_c[:, k - C4, t * P:(t + 1) * P])
                    last = nc.tensor.matmul(bank[4 + half][:, :], m, wo[:, k, half * 512:(half + 1) * 512],
                                            start=(k == 0), stop=(k == KD - 1))
                if k0 == KD - 2:
                    last.then_inc(S["wo_done"], 1)

            def out_samples_conv():
                pe.wait_ge(S["om_ready"], B)
                for half in range(2):
                    for k in range(C4):
                        nc.tensor.matmul(bank[half][32 * k:32 * k + B, :], mix_c[:, k, T:T + B],
                                         wo[:, C4 + k, half * 512:(half + 1) * 512], start=True, stop=False)

            def out_samples():
                pe.wait_ge(S["samp_norm_dve"], 2)
                for half in range(2):
                    for k in range(C4):
                        last = nc.tensor.matmul(bank[half][32 * k:32 * k + B, :], mix_a[:, k, T:T + B],
                                                wo[:, k, half * 512:(half + 1) * 512], start=False, stop=True)
                    last.then_inc(S["wo_part_done"], 1)
                pe.wait_ge(S["wo_taken"], 2 * NT)
                for half in range(2):
                    pe.wait_ge(S["samp_norm_act"], 3 + half)
                    nc.tensor.matmul(bank[4 + half][0:B, :], sel8, o_m[half][:, :], start=True, stop=True)\
                        .then_inc(S["wo_done"], 1)

            def turn_rows(t):
                n = P if t < NT else B
                pe.wait_ge(S["h2_ready"], t + 1)
                if t == 0:
                    pe.wait_ge(S["mod_scaled"], 2)
                if t:
                    pe.wait_ge(S["h2t_ready"], t)
                h = h_row[t % 2][0:n, :].rearrange("p (a k) -> p k a", k=KD)
                for k in range(KD):
                    last = nc.tensor.transpose(bank[6 + k // 4][:, (k % 4) * P:(k % 4) * P + n], h[:, k, :], ident[0:n, 0:n])
                last.then_inc(S["h2_psum"], 1)

            def route(t):
                n = P if t < NT else B
                pe.wait_ge(S["h2t_ready"], t + 1)
                if t == 0:
                    pe.wait_ge(S["wr_loaded"], 64)
                for k in range(KD):
                    last = nc.tensor.matmul(bank[3][0:n, t * 36:(t + 1) * 36], h2_t[:, k, 0:n], w_r[:, k, :],
                                            start=(k == 0), stop=(k == KD - 1))
                last.then_inc(S["lg_done"], 1)

            def gather_values(b):
                pe.wait_ge(S["om_ready"], b + 1)
                for c in range(C4):
                    last = nc.tensor.matmul(bank[2][:, c * B + b:c * B + b + 1], o_m[b % 2][:, c * P:(c + 1) * P],
                                            ones[:, 0:1], start=True, stop=True)
                last.then_inc(S["ot2_done"], 1)

            def ranks(a, b):
                n = P if b <= NT else B
                out = bank[3][0:n, 192 + a * NE:192 + b * NE]
                nc.tensor.matmul(out, earlier[0:n, 0:n], both[0:n, a:b, :].rearrange("p t e -> p (t e)"),
                                 start=True, stop=False)
                nc.tensor.matmul(out, ones[:, 0:n], both_sum[:, a:b, :].rearrange("p t e -> p (t e)"),
                                 start=False, stop=True).then_inc(S["rank_done"], 1)

            def tables(a, b):
                for t in range(a, b):
                    for c in range(2):
                        m = P if t < NT else B
                        last = nc.tensor.matmul(bank[2][:, 0:3 * NE], slot_is[0:m, c, t, :], vals[0:m, c, t, :],
                                                start=(c == 0 and t == 0), stop=(c == 1 and t == NT))
                return last

            for g in range(V_EARLY, NKV):
                value_chunk(g)
                if g == TURN_AT:
                    turn_output(NT - 1)
                if g in SPREAD_BESIDE_V:
                    spread_chunk(SPREAD_BESIDE_V[g])
                t, j = divmod(g - TURN_AT - 1, TILE_STEPS)
                if 0 <= t < NT and j < KD:
                    out_part(t, j // 4, 2 * (j % 4))
                if 0 <= t < NT and j == TILE_STEPS - 2:
                    turn_rows(t)
                if 0 <= t < NT and j == TILE_STEPS - 1:
                    route(t)
                if g % NCH == 5 and g >= NCH:
                    gather_values(g // NCH - 1)
                if g == NKV // 2:
                    pe.wait_ge(S["softmax_in"], 4)
                    for c in range(C4):
                        for hh in range(2):
                            last = nc.tensor.matmul(bank[2][hh * HD:(hh + 1) * HD, 64 + c * B:64 + (c + 1) * B],
                                                    ones[:, 0:HD], p_sum[:, :, 2 * c + hh], start=True, stop=True)
                    last.then_inc(S["samp_norm_psum"], 1)
                if g == NKV - 2:
                    pe.wait_ge(S["route_in"], 3)
                    ranks(0, NT)
            gather_values(B - 1)
            pe.wait_ge(S["samp_norm_act"], 1)
            nc.tensor.matmul(bank[2][:, 128:128 + C4 * B], block64[:], o_q[:, :, :].rearrange("p a b -> p (a b)"),
                             start=True, stop=True).then_inc(S["samp_norm_psum"], 1)
            out_samples_conv()
            out_samples()
            turn_rows(NT)
            route(NT)

            pe.wait_ge(S["vals_ready"], 1)
            tables(0, NT)
            pe.wait_ge(S["route_in"], 6)
            ranks(NT, NT + 1)
            nc.tensor.matmul(bank[1][:, 0:NE], ones[:, :], both_sum[:, NT, :], start=True, stop=False)
            nc.tensor.matmul(bank[1][:, 0:NE], ones[0:B, :], both[0:B, NT, :], start=False, stop=True)\
                .then_inc(S["rank_done"], 1)
            pe.wait_ge(S["vals_ready"], 2)
            tables(NT, NT + 1).then_inc(S["tabs_done"], 1)

            def gate_up(s, xs):
                gw = exp_w[s][:, 0:2048].rearrange("p (a c f) -> p a c f", a=2, c=4)
                uw = exp_w[s][:, 2048:4096].rearrange("p (a c f) -> p a c f", a=2, c=4)
                for a in range(2):
                    for c in range(4):
                        k = 4 * a + c
                        nc.tensor.matmul(bank[2 + xs][0:SLOTS, 0:DE], xe_t[xs][:, c, a, :], gw[:, a, c, :],
                                         start=(k == 0), stop=(k == 7))
                        last = nc.tensor.matmul(bank[2 + xs][SLOTS:2 * SLOTS, 0:DE], xe_t[xs][:, c, a, :],
                                                uw[:, a, c, :], start=(k == 0), stop=(k == 7))
                return last

            def transpose_x(s, xs):
                x4 = x_e[s][:, :].rearrange("p (a c) -> p c a", c=4)
                for c in range(4):
                    last = nc.tensor.transpose(bank[xs][:, c * P:(c + 1) * P], x4[:, c, :], ident[:])
                return last

            def transpose_hidden(xs):
                h2 = hid[xs][:, :].rearrange("p (a k) -> p k a", k=2)
                for k in range(2):
                    last = nc.tensor.matmul(bank[2 + xs][:, 256 + k * SLOTS:256 + (k + 1) * SLOTS], h2[:, k, :],
                                            ident[0:SLOTS, 0:SLOTS], start=True, stop=True)
                return last

            def down(s, xs):
                dw = exp_w[s][:, 4096:6144].rearrange("p (k n) -> p k n", k=2)
                for k in range(2):
                    for half in range(2):
                        last = nc.tensor.matmul(bank[4 + xs][half * SLOTS:(half + 1) * SLOTS, :], hid_t[xs][:, k, :],
                                                dw[:, k, half * 512:(half + 1) * 512], start=(k == 0), stop=(k == 1))
                return last

            def last_spread(j):
                if j == 0:
                    pe.wait_ge(b_loaded[1], 16)
                elif j < 5:
                    pe.wait_ge(S["mod_spread"], j + 4)
                else:
                    pe.wait_ge(S["mod_scaled"], 3)
                nc.tensor.matmul(bank[6][0:B, :], sel8, part[:, 6 + j, :], start=True, stop=True)
                nc.tensor.matmul(bank[7][:, :], sel[:, B, :], part[:, 6 + j, :], start=True, stop=True)\
                    .then_inc(S["expand_done"], 1)

            def front_of(g, s):
                xs, e1 = s % 2, 4 * g + s + 1
                pe.wait_ge(xe_loaded[s], (g + 1) * 16)
                transpose_x(s, xs).then_inc(S["xe_done"], 1)
                pe.wait_ge(S["xet_ready"], e1)
                pe.wait_ge(gate_loaded[s], (g + 1) * 32)
                gate_up(s, xs).then_inc(S["gu_done"], 1)

            def back_of(g, s):
                xs, e1 = s % 2, 4 * g + s + 1
                pe.wait_ge(S["hid_ready"], e1)
                transpose_hidden(xs).then_inc(S["hidt_done"], 1)
                pe.wait_ge(S["hidt_ready"], e1)
                pe.wait_ge(down_loaded[s], (g + 1) * 16)
                pe.wait_ge(S["y_ready"], e1)
                down(s, xs).then_inc(S["y_done"], 1)

            pe.wait_ge(S["tabs_ready"], 1)
            front_of(0, 0)
            for s in range(1, 4):
                front_of(0, s)
                back_of(0, s - 1)
            last_turn = NE // 4 - 1
            with pe.Fori(1, last_turn) as g:
                for s in range(4):
                    front_of(g, s)
                    if s == 0:
                        back_of(g - 1, 3)
                    else:
                        back_of(g, s - 1)
            last_spread(0)
            front_of(last_turn, 0)
            last_spread(1)
            back_of(last_turn - 1, 3)
            last_spread(2)
            front_of(last_turn, 1)
            last_spread(3)
            back_of(last_turn, 0)
            last_spread(4)
            front_of(last_turn, 2)
            back_of(last_turn, 1)
            last_spread(5)
            front_of(last_turn, 3)
            back_of(last_turn, 2)
            back_of(last_turn, 3)

            count = pe.value_load(max_count[0:1, 0:1], min_val=0, max_val=2 * (T + B))
            with pe.If(count > cap):
                with pe.Fori(1, PASSES) as p:
                    pe.wait_ge(S["vals_ready"], p + 2)
                    tables(0, NT + 1).then_inc(S["tabs_done"], 1)
                    with pe.Fori(0, NE) as e:
                        n = p * NE + e
                        pe.wait_ge(xe_loaded[0], (n - NE) * 16 + NE * 4 + 16)
                        transpose_x(0, 0).then_inc(S["xe_done"], 1)
                        pe.wait_ge(S["xet_ready"], n + 1)
                        pe.wait_ge(gate_loaded[0], (n - NE) * 32 + NE * 8 + 32)
                        gate_up(0, 0).then_inc(S["gu_done"], 1)
                        pe.wait_ge(S["hid_ready"], n + 1)
                        transpose_hidden(0).then_inc(S["hidt_done"], 1)
                        pe.wait_ge(S["hidt_ready"], n + 1)
                        pe.wait_ge(down_loaded[0], (n - NE) * 16 + NE * 4 + 16)
                        pe.wait_ge(S["y_ready"], n + 1)
                        down(0, 0).then_inc(S["y_done"], 1)

        @block.scalar
        def _(act):
            steps = [0]

            def step(ins):
                steps[0] += 1
                ins.then_inc(S["act_step"], 1)
                act.wait_ge(S["act_step"], steps[0])

            def copy(out, in_, scale=1.0):
                return nc.scalar.activation(out, in_, ACT.Copy, scale=scale)

            act.wait_ge(S["c_loaded"], 32)
            nc.scalar.activation(c_row[:, :], c_row[:, :], ACT.Silu).then_inc(S["c_silu"], 1)
            for n in range(4):
                act.wait_ge(S["ada_done"], n + 1)
                copy(part_a[:, n, :], bank[n % 2][:, :]).then_inc(S["part_ready"], 1)
                if n in (1, 2):
                    m = n - 1
                    act.wait_ge(S["expand_done"], m + 1)
                    copy(sh1_s[0:B, m * SECS:(m + 1) * SECS], bank[2 + m][0:B, :])
                    copy(sh1_p[:, m * SECS:(m + 1) * SECS], bank[4 + m][:, :]).then_inc(S["sh_ready"], 1)
                if n == 2:
                    act.wait_ge(S["x_loaded"], 32)
                    act.wait_ge(S["consts_ready"], 2)
                    for t in (NT, 0, 1, 2, 3):
                        rows = P if t < NT else B
                        step(nc.scalar.activation(junk[0:rows, :], x_a[0:rows, t, :], ACT.Square,
                                                  accum_out=ssq[0:rows, t:t + 1]))
                    nc.scalar.activation(ssq[:, :], ssq[:, :], ACT.Sqrt, bias=eps[:, 0:1], scale=1.0 / D)\
                        .then_inc(S["rstd_sq"], 1)
            for i in range(5):
                act.wait_ge(S["h_psum"], i + 1)
                if i == 0:
                    copy(h_t[:, :, T:T + B], bank[6][:, 64:128].rearrange("p (k n) -> p k n", k=KD))\
                        .then_inc(S["ht_ready"], 1)
                    act.wait_ge(S["samp_done"], 1)
                    copy(s_part[:, 0, :], bank[7][:, :]).then_inc(S["samp_evac"], 1)
                    act.wait_ge(S["row_done"], 1)
                    copy(qk_new[:, 0, :], bank[6][0:B, :]).then_inc(S["row_evac"], 1)
                    act.wait_ge(S["row_evac"], 1)
                    act.dma_start(q_rows_dram[:, :], qk_new[:, 0, :]).then_inc(S["q_stored"], 16)
                    continue
                lo = (i - 1) * P
                for q in range(2):
                    last = copy(h_t[:, 4 * q:4 * q + 4, lo:lo + P],
                                bank[(2 if i % 2 else 4) + q][:, :].rearrange("p (k n) -> p k n", k=4))
                last.then_inc(S["ht_ready"], 1)

            def acc(s, m):
                act.wait_ge(S["acc_done"], 4 * s + m + 1)

            for m in range(4):
                acc(0, m)
                copy(q_t[:, m, :], bank[m][:, :], SCALE).then_inc(S["acc_act"], 1)
            for s in (1, 2):
                act.wait_ge(S["samp_done"], s + 1)
                copy(s_part[:, s, :], bank[7][:, :]).then_inc(S["samp_evac"], 1)
                for m in range(4):
                    acc(s, m)
                    copy((k_t if s == 1 else v_r)[:, m, :], bank[m][:, :]).then_inc(S["acc_act"], 1)
                act.wait_ge(S["row_done"], s + 1)
                new = qk_new[:, 1, :] if s == 1 else v_new[:, :]
                copy(new, bank[6][0:B, :]).then_inc(S["row_evac"], 1)
                act.wait_ge(S["row_evac"], s + 1)
                dst = (k_sample if s == 1 else v_sample).rearrange("l b t h d -> (l b t) (h d)")
                act.dma_start(dst, new).then_inc(S["outs"], 16)
            act.wait_ge(S["acc_act"], 12)
            act.dma_start(v_prompt.rearrange("l b (t p) h d -> (l b p) t (h d)", p=P), v_r[:, :, :])\
                .then_inc(S["outs"], 16)
            kp = k_prompt.rearrange("l b (t p) h d -> (l b t) p (h d)", p=P)
            for t in range(NT):
                act.wait_ge(S["krow_done"], t + 1)
                copy(k_row[t][:, :], bank[4 + t % 2][:, :]).then_inc(S["krow_evac"], 1)
                act.wait_ge(S["krow_evac"], t + 1)
                act.dma_start(kp[t, :, :], k_row[t][:, :]).then_inc(S["krow_out"], 16)
            act.wait_ge(S["f_taken"], 1)
            step(nc.scalar.activation(f_a[:, :], f_a[:, :], ACT.Exp, scale=-1.0))
            nc.scalar.activation(f_a[:, :], f_a[:, :], ACT.Ln, bias=ones[0:H, 0:1]).then_inc(S["ln_ready"], 1)
            act.wait_ge(S["samp_done"], 4)
            act.wait_ge(S["consts_ready"], 4)
            copy(u_part[:, :], bank[7][:, :]).then_inc(S["samp_evac"], 1)
            for m in range(4):
                acc(3, m)
                copy(conv_in[:, m, 2:2 + T], bank[m][:, :]).then_inc(S["acc_act"], 1)
            act.wait_ge(S["samp_t"], 1)
            copy(conv_in[:, :, T + 2:T + 2 + B], bank[6][:, 0:C4 * B].rearrange("p (c b) -> p c b", c=C4))\
                .then_inc(S["samp_u"], 1)
            act.wait_ge(S["side_turned"], 1)
            copy(lf_rows[:, 0:NT, :], bank[4][:, 0:NT * H].rearrange("p (t h) -> p t h", t=NT))\
                .then_inc(S["lf_evac"], 1)
            copy(lf_rows[0:B, NT, :], bank[4][0:B, 32:32 + H]).then_inc(S["lf_evac"], 1)
            act.wait_ge(S["lf_evac"], 2)
            act.dma_start(logf_prompt.rearrange("l b (t p) h -> (l b p) t h", p=P), lf_rows[:, 0:NT, :])\
                .then_inc(S["outs"], 16)
            act.dma_start(logf_sample.rearrange("l b t h -> (l b t) h"), lf_rows[0:B, NT, :])\
                .then_inc(S["outs"], 16)
            act.wait_ge(S["side_turned"], 2)
            copy(state_t[:, :, :, :], bank[5][:, 0:C4 * 16].rearrange("p (c b j) -> p c b j", c=C4, b=B))\
                .then_inc(S["st_evac"], 1)
            for s in (4, 5):
                act.wait_ge(S["samp_done"], s + 1)
                act.wait_ge(S["samp_t"], s - 3)
                copy(u_part[:, :], bank[7][:, :]).then_inc(S["samp_evac"], 1)
            act.wait_ge(S["side_turned"], 3)
            act.wait_ge(S["krow_out"], 64)
            copy(c_rows[:, :], bank[4][0:2 + B, :]).then_inc(S["crow_evac"], 1)
            act.wait_ge(S["crow_evac"], 1)
            act.dma_start(conv_prompt.rearrange("l b j c -> (l b j) c"), c_rows[0:2, :]).then_inc(S["outs"], 16)
            act.dma_start(conv_sample[0, :, 1, :], c_rows[2:2 + B, :]).then_inc(S["outs"], 16)
            act.wait_ge(S["outs"], 16 * 8)
            act.wait_ge(S["krow_out"], 64)

            def conv_square(i):
                act.wait_ge(S["acc_dve"], 4 + C4)
                act.wait_ge(S["samp_g"], 2)
                if i:
                    act.wait_ge(S["cn_done"], i)
                src = mix_c[:, :, T:T + B] if i == 0 else mix_c[:, i - 1, 0:T]
                dst = sq_c[:, 0:C4 * B].rearrange("p (c b) -> p c b", c=C4) if i == 0 else sq_c[:, 0:T]
                nc.scalar.activation(dst, src, ACT.Square).then_inc(S["sq_ready"], 1)

            def conv_sqrt(i):
                act.wait_ge(S["cn_done"], i + 1)
                if i:
                    act.wait_ge(S["mix_ready_c"], i)
                n = C4 * B if i == 0 else T
                nc.scalar.activation(rt_c[:, 0:n], bank[6][:, 0:n], ACT.Sqrt, bias=eps[:, 0:1], scale=1.0 / HD)\
                    .then_inc(S["cn_sqrt"], 1)

            def ada_evac(n):
                act.wait_ge(S["ada_done"], 4 + n + 1)
                copy(part[:, n, :], bank[7][:, :]).then_inc(S["part_ready"], 1)

            def spread_evac(j):
                act.wait_ge(S["expand_done"], 4 + j + 1)
                half = slice((j % 2) * SECS, (j % 2 + 1) * SECS)
                copy((ga1_s if j < 2 else sh2_s)[0:B, half], bank[6][0:B, :])
                copy((ga1_p if j < 2 else sh2_p)[:, half], bank[7][:, :]).then_inc(S["mod_spread"], 1)

            def soft(w):
                t = w // H
                n = (t + 1) * P
                act.wait_ge(S["max_ready"], w + 1)
                if w >= 2:
                    act.wait_ge(S["pt_done"], w - 1)
                i = (t % 2) * H + w % H
                nc.scalar.activation(probs[w % 2][:, 0:n], bank[w % 3][:, 0:n], ACT.Exp,
                                     bias=neg_max[:, w % 2:w % 2 + 1], accum_out=row_sum[:, i:i + 1])\
                    .then_inc(S["p_ready"], 1)

            def square_output(t):
                act.wait_ge(S["o_taken"], t + 1)
                nc.scalar.activation(o_sq[:, :, :], o_row[:, :, :], ACT.Square).then_inc(S["o_sq_ready"], 1)

            def norm_output(t):
                act.wait_ge(S["o_ssq"], t + 1)
                nc.scalar.activation(head_ssq[:, :], head_ssq[:, :], ACT.Sqrt, bias=eps[:, 0:1], scale=1.0 / HD)\
                    .then_inc(S["o_sqrt"], 1)

            def output_out(t):
                act.wait_ge(S["ot_done"], t + 1)
                for c in range(C4):
                    last = copy(mix_a[:, c, t * P:(t + 1) * P], bank[6][:, c * P:(c + 1) * P], vecs[:, c:c + 1])
                last.then_inc(S["mix_ready"], 1)

            conv_square(0)
            for w in range(NT * H):
                soft(w)
                t = w // H
                act.wait_ge(S["pt_done"], w + 1)
                if w >= 2:
                    act.wait_ge(S["pv_done"], w - 1)
                copy(probs_t[w % 2][:, 0:t + 1, :],
                     bank[3 + w % 2][:, 0:(t + 1) * P].rearrange("p (b n) -> p b n", n=P)).then_inc(S["pt_ready"], 1)
                if w < 1 + C4:
                    conv_sqrt(w)
                if w < C4:
                    conv_square(w + 1)
                if w == 1 + C4:
                    act.wait_ge(S["tail_done"], 1)
                    copy(tail[:, :, :], bank[6][:, 0:B * H].rearrange("p (b h) -> p b h", b=B))\
                        .then_inc(S["tail_evac"], 1)
                if w - 1 in ADA_AT:
                    ada_evac(ADA_AT[w - 1])
                if w - 1 in SPREAD_AT:
                    spread_evac(SPREAD_AT[w - 1])
                if w % H == 0 and w:
                    square_output(t - 1)
                if w % H == 1 and w > H:
                    norm_output(t - 1)
                if w % H == 3 and w > H:
                    output_out(t - 1)
                if w in (NT * H - 4, NT * H - 3):
                    if w == NT * H - 4:
                        act.wait_ge(S["softmax_in"], 3)
                        nc.scalar.activation(p_new[:, :, :], p_new[:, :, :], ACT.Exp).then_inc(S["pnew_ready"], 1)
                    for b in range(4 * (w % 2), 4 * (w % 2) + 4):
                        nc.scalar.activation(scores[:, b, :, :], scores[:, b, :, :], ACT.Exp)\
                            .then_inc(S["exp_ready"], 1)
            square_output(NT - 1)
            norm_output(NT - 1)
            output_out(NT - 1)
            spread_evac(2)
            spread_evac(3)

            def second_norm(t):
                n = P if t < NT else B
                act.wait_ge(S["x1_ready"], t + 1)
                step(nc.scalar.activation(junk2[0:n, :], x_r[0:n, t, :], ACT.Square, accum_out=ssq[0:n, t:t + 1]))
                nc.scalar.activation(ssq[0:n, t:t + 1], ssq[0:n, t:t + 1], ACT.Sqrt, bias=eps[0:n, 0:1], scale=1.0 / D)\
                    .then_inc(S["norm_sqrt"], 1)
                act.wait_ge(S["h2_ready"], t + 1)
                act.dma_start(h2_dram[t * 2 * P:t * 2 * P + 2 * n, :].rearrange("(p a) d -> p (a d)", a=2),
                              h_row[t % 2][0:n, :]).then_inc(h2_out[t % 2], 16)
                act.wait_ge(S["h2_psum"], t + 1)
                if t:
                    act.wait_ge(S["lg_done"], t)
                for q in range(2):
                    last = copy(h2_t[:, 4 * q:4 * q + 4, 0:n],
                                bank[6 + q][:, :].rearrange("p (k n) -> p k n", k=4)[:, :, 0:n])
                last.then_inc(S["h2t_ready"], 1)

            def choice_exp(i, values):
                act.wait_ge(S["route_in"], i)
                nc.scalar.activation(values, values, ACT.Exp).then_inc(S["route_exp"], 1)

            for t in range(NT):
                second_norm(t)
            choice_exp(1, ge[:, 0:NT, :])
            choice_exp(2, el[:, 0:NT, :])
            act.wait_ge(S["samp_norm_dve"], 1)
            nc.scalar.activation(o_q[:, :, :], o_t[:, :, :], ACT.Square).then_inc(S["samp_norm_act"], 1)
            act.wait_ge(S["samp_norm_psum"], 2)
            nc.scalar.activation(o_r[:, :, :], bank[2][:, 128:128 + C4 * B].rearrange("p (c b) -> p c b", c=C4),
                                 ACT.Sqrt, bias=eps[:, 0:1], scale=1.0 / HD).then_inc(S["samp_norm_act"], 1)
            act.wait_ge(S["ot2_done"], B)
            for half in range(2):
                act.wait_ge(S["wo_part_done"], half + 1)
                copy(o_m[half][:, :], bank[half][:, :]).then_inc(S["samp_norm_act"], 1)
            second_norm(NT)

            choice_exp(4, ge[:, NT:NT + 1, :])
            choice_exp(5, el[:, NT:NT + 1, :])

            def x_out(xs):
                return copy(xe_t[xs][:, :, :, :],
                            bank[xs][:, :].rearrange("p (c a n) -> p c a n", c=4, a=2))

            def gate_silu(xs):
                return nc.scalar.activation(sig[xs][:, :], bank[2 + xs][0:SLOTS, 0:DE], ACT.Silu)

            def last_spread(j):
                act.wait_ge(S["expand_done"], j + 11)
                half = slice((j % 2) * SECS, (j % 2 + 1) * SECS)
                copy((ga2_s if j < 2 else shf_s)[0:B, half], bank[6][0:B, :])
                copy((ga2_p if j < 2 else shf_p)[:, half], bank[7][:, :]).then_inc(S["mod_spread"], 1)

            def one_expert(g, s):
                xs, e1 = s % 2, 4 * g + s + 1
                act.wait_ge(S["xe_done"], e1)
                if s >= 2:
                    act.wait_ge(S["gu_done"], e1 - 2)
                x_out(xs).then_inc(S["xet_ready"], 1)
                act.wait_ge(S["gu_done"], e1)
                gate_silu(xs).then_inc(S["sig_ready"], 1)

            with act.Fori(0, NE // 4 - 1) as g:
                for s in range(4):
                    one_expert(g, s)
            last_spread(0)
            one_expert(NE // 4 - 1, 0)
            last_spread(1)
            last_spread(2)
            one_expert(NE // 4 - 1, 1)
            last_spread(3)
            one_expert(NE // 4 - 1, 2)
            one_expert(NE // 4 - 1, 3)
            count = act.value_load(max_count[0:1, 0:1], min_val=0, max_val=2 * (T + B))
            with act.If(count > cap):
                with act.Fori(NE, PASSES * NE) as n:
                    act.wait_ge(S["xe_done"], n + 1)
                    x_out(0).then_inc(S["xet_ready"], 1)
                    act.wait_ge(S["gu_done"], n + 1)
                    gate_silu(0).then_inc(S["sig_ready"], 1)

            for i, t in enumerate((0, 1, 2, 3, NT)):
                n = P if t < NT else B
                act.wait_ge(S["x1_ready"], i + 6)
                step(nc.scalar.activation(junk2[0:n, :], x_r[0:n, t, :], ACT.Square, accum_out=ssq[0:n, t:t + 1]))
                nc.scalar.activation(ssq[0:n, t:t + 1], ssq[0:n, t:t + 1], ACT.Sqrt, bias=eps[0:n, 0:1], scale=1.0 / D)\
                    .then_inc(S["norm_sqrt"], 1)
            act.wait_ge(S["outs"], 16 * 8)

        @block.vector
        def _(dve):
            V = nc.vector
            steps = [0]

            def step(ins):
                steps[0] += 1
                ins.then_inc(S["dve_step"], 1)
                dve.wait_ge(S["dve_step"], steps[0])

            def spread(ap, shape):
                return ap.to_broadcast(shape)

            step(V.memset(c_t[:, :, :], 0.0))
            dve.wait_ge(S["pt_loaded"], 16)
            V.tensor_copy(pt_exp[:, :, :], spread(pt_int[:, :].rearrange("b (j o) -> b j o", o=1), [B, NPG, 4]))\
                .then_inc(S["setup_ready"], 1)
            dve.wait_ge(S["consts_ready"], 1)
            step(V.tensor_single_scalar(lane[:, :], lane[:, :], 3, ALU.bitwise_and))
            step(V.tensor_copy(quarter[:, 8:9], lane[:, :]))
            for s in range(NCH):
                last = V.tensor_scalar(quarter[:, s:s + 1], quarter[:, 8:9], float(NCH), float(s), ALU.mult, ALU.add)
            step(last)
            dve.wait_ge(S["setup_psum"], 1)
            ids = bank[6][:, 32:32 + B]
            V.tensor_scalar(f_index[:, :], ids, 4.0, quarter[:, 8:9], ALU.mult, ALU.add).then_inc(S["setup_ready"], 1)
            for s in range(NCH):
                last = V.tensor_scalar(kv_index[:, :].rearrange("p (b s) -> p s b", s=NCH)[:, s, :], ids,
                                       4.0 * NCH, quarter[:, s:s + 1], ALU.mult, ALU.add)
            last.then_inc(S["setup_ready"], 1)
            dve.wait_ge(S["setup_psum"], 2)
            V.tensor_copy(c_t[:, :, 0:B + 1], bank[7][:, 0:KD * 9].rearrange("p (k n) -> p k n", k=KD))\
                .then_inc(S["setup_ready"], 1)
            dve.wait_ge(S["rstd_sq"], 1)
            step(V.reciprocal(rstd[:, :], ssq[:, :]))
            dve.wait_ge(S["g_loaded"], 16)
            for m in range(2):
                dve.wait_ge(S["expand_done"], m + 3)
                lo = slice(m * SECS, (m + 1) * SECS)
                V.scalar_tensor_tensor(sc1_s[0:B, lo], bank[2 + m][0:B, :], 1.0, g1_b[0:B, lo], ALU.add, ALU.mult)
                step(V.scalar_tensor_tensor(sc1_p[:, lo], bank[4 + m][:, :], 1.0, g1_b[:, lo], ALU.add, ALU.mult))
            dve.wait_ge(S["sh_ready"], 2)
            for i in range(5):
                t, n = (NT, B) if i == 0 else (i - 1, P)
                sc, sh = (sc1_s, sh1_s) if i == 0 else (sc1_p, sh1_p)
                if i >= 2:
                    dve.wait_ge(S["h_psum"], i - 1)
                r = h_row[i % 2]
                step(V.scalar_tensor_tensor(r[0:n, :], x_a[0:n, t, :], rstd[0:n, t:t + 1], sc[0:n, :], ALU.mult, ALU.mult))
                V.tensor_tensor(r[0:n, :], r[0:n, :], sh[0:n, :], ALU.add).then_inc(S["h_row_ready"], 1)


            def k_chunk(n):
                b, s = divmod(n, NCH)
                dve.wait_ge(kv_loaded[n % RING], 16 * (n // RING + 1))
                if s == 0:
                    dve.wait_ge(qb_loaded[b % 2], 16 * (b // 2 + 1))
                q = q_b[:, b % 2, :].rearrange("p (o c) -> p o c", o=1)
                for i in range(2):
                    if n:
                        dve.wait_ge(S["k_used"], 2 * n - 1 + i)
                    r = slice(i * CH // 2, (i + 1) * CH // 2)
                    V.tensor_tensor(prod[:, r, :], kv_ring[:, n % RING, r, :], spread(q, [P, CH // 2, HW]), ALU.mult)\
                        .then_inc(S["k_products"], 1)
                for i in range(2):
                    dve.wait_ge(S["k_products"], 2 * n + i + 1)
                    r = slice(i * CH // 2, (i + 1) * CH // 2)
                    lo = s * CH + i * CH // 2
                    V.reduce_sum(scores[:, b, lo:lo + CH // 2, :],
                                 prod[:, r, :].rearrange("p r (h d) -> p r h d", h=H), AX.X).then_inc(S["k_used"], 1)
            next_k = [0]

            def k_chunks(m):
                for _ in range(m):
                    if next_k[0] < NKV:
                        k_chunk(next_k[0])
                        next_k[0] += 1

            k_chunks(NEW_AT)
            dve.wait_ge(S["row_evac"], 2)
            step(V.tensor_tensor(qk_prod[:, :], qk_new[:, 0, :], qk_new[:, 1, :], ALU.mult))
            step(V.memset(news[:, :, :], NEG))
            step(V.reduce_sum(top[0:B, 0, :], qk_prod[:, :].rearrange("p (h d) -> p h d", h=H), AX.X))
            V.tensor_scalar(news[0:B, :, :], spread(top[0:B, 0:1, :], [B, B, H]), SCALE, None, ALU.mult)\
                .then_inc(S["select_in"], 1)
            k_chunks(6)
            dve.wait_ge(S["setup_psum"], 3)
            V.tensor_copy(vecs[:, :], bank[6][:, 0:20]).then_inc(S["setup_ready"], 1)
            dve.wait_ge(S["f_done"], 1)
            dve.wait_ge(S["vec_loaded"], 64)
            V.tensor_scalar(f_t[:, 0:T], bank[4][0:H, :], b_f[:, 0:1], None, ALU.add)
            step(V.tensor_scalar(f_t[:, T:T + B], bank[5][0:H, 0:B], b_f[:, 0:1], None, ALU.add))
            step(V.tensor_scalar(f_a[:, :], f_t[:, :], -1.0, None, ALU.mult))
            V.tensor_tensor(f_a[:, :], f_a[:, :], f_t[:, :], ALU.max).then_inc(S["f_taken"], 1)
            k_chunks(1)
            dve.wait_ge(S["ln_ready"], 1)
            step(V.scalar_tensor_tensor(f_t[:, :], f_t[:, :], 0.0, f_a[:, :], ALU.min, ALU.subtract))
            step(V.tensor_tensor_scan(cum[:, :], f_t[:, 0:T], f_t[:, 0:T], 0.0, ALU.add, ALU.bypass))
            V.tensor_scalar(neg_cum[:, 0:T], cum[:, :], -1.0, None, ALU.mult).then_inc(S["lf_ready"], 1)
            k_chunks(DIAG_AT - NEW_AT - 7)
            dve.wait_ge(S["lf_evac"], 2)
            V.tensor_copy(lf_diag[:, :, :], spread(lf_rows[0:B, NT:NT + 1, :], [B, B, H])).then_inc(S["select_in"], 1)
            for m in range(4):
                dve.wait_ge(S["acc_done"], 16 + m + 1)
                dve.wait_ge(S["acc_act"], 12 + m + 1)
                V.tensor_tensor(conv_in[:, m, 2:2 + T], bank[m][:, :], conv_in[:, m, 2:2 + T], ALU.mult)\
                    .then_inc(S["acc_dve"], 1)
                k_chunks(1)
            dve.wait_ge(S["samp_t"], 2)
            dve.wait_ge(S["samp_u"], 1)
            new_in = conv_in[:, :, T + 2:T + 2 + B]
            V.tensor_tensor(new_in, bank[6][:, 0:C4 * B].rearrange("p (c b) -> p c b", c=C4), new_in, ALU.mult)\
                .then_inc(S["samp_g"], 1)
            dve.wait_ge(S["samp_g"], 1)
            dve.wait_ge(S["acc_dve"], 4)
            dve.wait_ge(S["st_evac"], 1)
            for j in range(3):
                src = state_t[:, :, :, j] if j < 2 else new_in
                w = spread(vecs[:, 8 + 4 * j:12 + 4 * j].rearrange("p (c o) -> p c o", o=1), [P, C4, B])
                out = mix_c[:, :, T:T + B] if j == 0 else y_tmp[:, :, :]
                step(V.tensor_tensor(out, src, w, ALU.mult))
                if j:
                    step(V.tensor_tensor(mix_c[:, :, T:T + B], mix_c[:, :, T:T + B], y_tmp[:, :, :], ALU.add))
            for m in range(4):
                out = mix_c[:, m, 0:T]
                step(V.tensor_scalar(out, conv_in[:, m, 0:T], vecs[:, 8 + m:9 + m], None, ALU.mult))
                for j in (1, 2):
                    step(V.scalar_tensor_tensor(out, conv_in[:, m, j:j + T], vecs[:, 8 + 4 * j + m:9 + 4 * j + m], out,
                                                ALU.mult, ALU.add))
            for m in range(4):
                dve.wait_ge(S["acc_done"], 20 + m + 1)
                V.tensor_tensor(mix_c[:, m, 0:T], bank[m][:, :], mix_c[:, m, 0:T], ALU.mult).then_inc(S["acc_dve"], 1)
                k_chunks(1)
            dve.wait_ge(S["samp_t"], 3)
            V.tensor_tensor(mix_c[:, :, T:T + B], bank[6][:, 0:C4 * B].rearrange("p (c b) -> p c b", c=C4),
                            mix_c[:, :, T:T + B], ALU.mult).then_inc(S["samp_g"], 1)

            def conv_norm(i):
                dve.wait_ge(S["cn_sqrt"], i + 1)
                n = C4 * B if i == 0 else T
                step(V.reciprocal(rt_c[:, 0:n], rt_c[:, 0:n]))
                if i == 0:
                    m = mix_c[:, :, T:T + B]
                    step(V.tensor_tensor(m, m, rt_c[:, 0:n].rearrange("p (c b) -> p c b", c=C4), ALU.mult))
                    V.tensor_tensor(m, m, spread(vecs[:, 4:8].rearrange("p (c o) -> p c o", o=1), [P, C4, B]), ALU.mult)\
                        .then_inc(S["mix_ready_c"], 1)
                else:
                    m = mix_c[:, i - 1, 0:T]
                    V.scalar_tensor_tensor(m, m, vecs[:, 3 + i:4 + i], rt_c[:, 0:n], ALU.mult, ALU.mult)\
                        .then_inc(S["mix_ready_c"], 1)

            def row_max(w):
                t = w // H
                n = (t + 1) * P
                dve.wait_ge(S["s_done"], w + 1)
                step(V.tensor_tensor(bank[w % 3][:, t * P:n], bank[w % 3][:, t * P:n], causal[:, :], ALU.add))
                if w >= 2:
                    dve.wait_ge(S["p_ready"], w - 1)
                V.reduce_max(neg_max[:, w % 2:w % 2 + 1], bank[w % 3][:, 0:n], AX.X, negate=True)\
                    .then_inc(S["max_ready"], 1)

            def attention_output(t):
                dve.wait_ge(S["pv_done"], H * (t + 1))
                sums = row_sum[:, (t % 2) * H:(t % 2 + 1) * H]
                step(V.reciprocal(sums, sums))
                if t:
                    dve.wait_ge(S["ot_done"], t)
                V.tensor_tensor(o_row[:, :, :], bank[5][:, :].rearrange("p (h d) -> p h d", h=H),
                                spread(sums.rearrange("p (h o) -> p h o", o=1), [P, H, HD]), ALU.mult)\
                    .then_inc(S["o_taken"], 1)

            def attention_squares(t):
                dve.wait_ge(S["o_sq_ready"], t + 1)
                V.reduce_sum(head_ssq[:, :], o_sq[:, :, :], AX.X).then_inc(S["o_ssq"], 1)

            def attention_norm(t):
                dve.wait_ge(S["o_sqrt"], t + 1)
                step(V.reciprocal(head_ssq[:, :], head_ssq[:, :]))
                V.tensor_tensor(o_row[:, :, :], o_row[:, :, :],
                                spread(head_ssq[:, :].rearrange("p (h o) -> p h o", o=1), [P, H, HD]), ALU.mult)\
                    .then_inc(S["o_ready"], 1)

            def spread_scale(j):
                if j == 4:
                    dve.wait_ge(S["g_loaded"], 32)
                dve.wait_ge(S["expand_done"], j + 5)
                lo = slice((j % 2) * SECS, (j % 2 + 1) * SECS)
                V.scalar_tensor_tensor(sc2_s[0:B, lo], bank[6][0:B, :], 1.0, g_b[0:B, lo], ALU.add, ALU.mult)
                V.scalar_tensor_tensor(sc2_p[:, lo], bank[7][:, :], 1.0, g_b[:, lo], ALU.add, ALU.mult)\
                    .then_inc(S["mod_scaled"], 1)

            def sample_softmax(i):
                flat = scores[:, :, :, :].rearrange("p b i h -> p (b i h)")
                if i == 0:
                    dve.wait_ge(S["k_used"], 2 * NKV)
                    dve.wait_ge(S["select_done"], 3)
                    step(V.scalar_tensor_tensor(flat, flat, SCALE, decay[:, :, :, :].rearrange("p b i h -> p (b i h)"),
                                                ALU.mult, ALU.add))
                if i == 1:
                    step(V.reduce_max(top[:, :, :], scores[:, :, :, :].rearrange("p b i h -> p b h i"), AX.X))
                    V.tensor_tensor(top[:, :, :], top[:, :, :], news[:, :, :], ALU.max).then_inc(S["softmax_in"], 1)
                if i == 2:
                    dve.wait_ge(S["top_ready"], 1)
                    V.tensor_tensor(p_new[:, :, :], news[:, :, :], top_all[:, :, :], ALU.subtract)\
                        .then_inc(S["softmax_in"], 1)
                    V.tensor_tensor(scores[:, :, :, :], scores[:, :, :, :],
                                    spread(top_all[:, :, :].rearrange("p b (o h) -> p b o h", o=1), [P, B, PPP, H]),
                                    ALU.subtract).then_inc(S["softmax_in"], 1)

            for w in range(NT * H):
                row_max(w)
                if w % H == 0 and w:
                    attention_output(w // H - 1)
                if w % H == 1 and w > H:
                    attention_squares(w // H - 1)
                if w % H == 2 and w > H:
                    attention_norm(w // H - 1)
                k_chunks(1)
                if w < 1 + C4:
                    conv_norm(w)
                if w >= SOFTMAX_AT:
                    sample_softmax(w - SOFTMAX_AT)
                if w == NT * H - 4:
                    dve.wait_ge(S["mod_spread"], 2)
                    V.memset(bank[7][:, :], 0.0).then_inc(S["zeroed"], 1)
            dve.wait_ge(S["p_ready"], NT * H)
            V.memset(bank[0][:, :], 0.0)
            V.memset(bank[1][:, :], 0.0).then_inc(S["zeroed"], 1)
            attention_output(NT - 1)
            attention_squares(NT - 1)
            attention_norm(NT - 1)


            def residual(t):
                n = P if t < NT else B
                ga, sc, sh, gated = (ga1_p, sc2_p, sh2_p, prod_o) if t < NT else (ga1_s, sc2_s, sh2_s, junk2)
                for half in range(2):
                    lo = slice(half * 512, (half + 1) * 512)
                    dve.wait_ge(S["wo_done"], 2 * t + half + 1)
                    V.tensor_tensor(gated[0:n, lo], bank[4 + half][0:n, :], ga[0:n, lo], ALU.mult)\
                        .then_inc(S["wo_taken"], 1)
                dve.wait_ge(S["wo_taken"], 2 * t + 2)
                if t == 0:
                    dve.wait_ge(S["x_loaded"], 80)
                V.tensor_tensor(x_r[0:n, t, :], x_r[0:n, t, :], gated[0:n, :], ALU.add).then_inc(S["x1_ready"], 1)
                dve.wait_ge(S["norm_sqrt"], t + 1)
                step(V.reciprocal(rstd[0:n, t:t + 1], ssq[0:n, t:t + 1]))
                if t >= 2:
                    dve.wait_ge(h2_out[t % 2], 16 * (t // 2))
                    dve.wait_ge(S["h2_psum"], t - 1)
                r = h_row[t % 2]
                step(V.scalar_tensor_tensor(r[0:n, :], x_r[0:n, t, :], rstd[0:n, t:t + 1], sc[0:n, :], ALU.mult, ALU.mult))
                V.tensor_tensor(r[0:n, :], r[0:n, :], sh[0:n, :], ALU.add).then_inc(S["h2_ready"], 1)

            def own_heads(b):
                dve.wait_ge(S["pvs_done"], b + 1)
                if b >= 2:
                    dve.wait_ge(S["ot2_done"], b - 1)
                V.tensor_tensor(o_m[b % 2][:, :], value_bank(b)[:, :], head_mask[:, :], ALU.mult).then_inc(S["om_ready"], 1)

            def logits(t):
                n = P if t < NT else B
                dve.wait_ge(S["lg_done"], t + 1)
                V.tensor_tensor(lg[0:n, t, :], bank[3][0:n, t * 36:(t + 1) * 36], b_r[0:n, :], ALU.add)\
                    .then_inc(S["lg_taken"], 1)

            def one(i, a, b):
                return st[:, i, a:b]

            def wide(i, a, b, n):
                return spread(one(i, a, b).rearrange("p (t o) -> p t o", o=1), [P, b - a, n])

            def first_of(out, values, top_value, n, a, b):
                step(V.reduce_max(one(top_value, a, b), values, AX.X))
                step(V.tensor_tensor(out, values, wide(top_value, a, b, n), ALU.is_equal))
                d = spread(desc[:, 8 - n:8].rearrange("p (o n) -> p o n", o=1), [P, b - a, n])
                step(V.tensor_tensor(out, out, d, ALU.mult))
                step(V.reduce_max(one(11, a, b), out, AX.X))
                step(V.tensor_tensor(out, out, wide(11, a, b, n), ALU.is_equal))

            def choose(a, b, i):
                r = b - a
                gl, gx, go, ex, es = lg[:, a:b, 0:NG], ge[:, a:b, :], g_oh[:, a:b, :], el[:, a:b, :], els[:, a:b, :, :]
                dve.wait_ge(S["lg_taken"], b)
                step(V.reduce_max(one(0, a, b), gl, AX.X))
                V.tensor_tensor(gx, gl, wide(0, a, b, NG), ALU.subtract).then_inc(S["route_in"], 1)
                if i == 0:
                    dve.wait_ge(S["consts_ready"], 5)
                first_of(go, gl, 1, NG, a, b)
                wide_g = spread(go.rearrange("p t (g o) -> p t g o", o=1), [P, r, NG, EPG])
                step(V.tensor_tensor(es, lg[:, a:b, NG:NG + NE].rearrange("p t (g e) -> p t g e", g=NG), wide_g, ALU.mult))
                step(V.reduce_sum(ex, es.rearrange("p t g e -> p t e g"), AX.X))
                step(V.reduce_max(one(2, a, b), ex, AX.X))
                V.tensor_tensor(ex, ex, wide(2, a, b, EPG), ALU.subtract).then_inc(S["route_in"], 1)
                dve.wait_ge(S["route_exp"], 2 * i + 1)
                step(V.reduce_sum(one(3, a, b), gx, AX.X))
                step(V.reciprocal(one(3, a, b), one(3, a, b)))
                dve.wait_ge(S["route_exp"], 2 * i + 2)
                first, second = e_c[:, 0, a:b, :], e_c[:, 1, a:b, :]
                first_of(first, ex, 4, EPG, a, b)
                step(V.tensor_tensor(e_t[:, a:b, :], ex, first, ALU.mult))
                step(V.tensor_tensor(ex, ex, e_t[:, a:b, :], ALU.subtract))
                step(V.tensor_tensor(ex, ex, first, ALU.subtract))
                first_of(second, ex, 5, EPG, a, b)
                for c, chosen in enumerate((first, second)):
                    step(V.tensor_tensor(oh[:, c, a:b, :].rearrange("p t (g e) -> p t g e", g=NG), wide_g,
                                         spread(chosen.rearrange("p t (o e) -> p t o e", o=1), [P, r, NG, EPG]), ALU.mult))
                last = V.tensor_tensor(both[:, a:b, :], oh[:, 0, a:b, :], oh[:, 1, a:b, :], ALU.add)
                if i == 0:
                    V.memset(both_sum[:, 0, :], 0.0)
                    step(last)
                    for t in range(NT):
                        last = (V.tensor_copy(both_sum[:, 1, :], both[:, 0, :]) if t == 0 else
                                V.tensor_tensor(both_sum[:, t + 1, :], both_sum[:, t, :], both[:, t, :], ALU.add))
                        if t < NT - 1:
                            step(last)
                last.then_inc(S["route_in"], 1)
                step(V.tensor_tensor(one(6, a, b), one(4, a, b), one(5, a, b), ALU.add))
                step(V.reciprocal(one(6, a, b), one(6, a, b)))
                step(V.tensor_tensor(one(6, a, b), one(6, a, b), one(3, a, b), ALU.mult))
                for c in range(2):
                    step(V.tensor_tensor(one(7 + c, a, b), one(4 + c, a, b), one(6, a, b), ALU.mult))
                    step(V.tensor_scalar(one(9, a, b), tok2[:, a:b], 2.0, 2.0 * c - FAR, ALU.mult, ALU.add))
                    for k, v in ((1, 9), (2, 7 + c)):
                        V.tensor_tensor(vals[:, c, a:b, k * NE:(k + 1) * NE], oh[:, c, a:b, :], wide(v, a, b, NE), ALU.mult)
                    step(V.tensor_tensor(vals[:, c, a:b, 0:NE], oh[:, c, a:b, :],
                                         spread(tok2[:, a:b].rearrange("p (t o) -> p t o", o=1), [P, r, NE]), ALU.mult))

            def ranks(a, b, done):
                dve.wait_ge(S["rank_done"], done)
                n = P if b <= NT else B
                step(V.tensor_copy(rank_e[0:n, a:b, :],
                                   bank[3][0:n, 192 + a * NE:192 + b * NE].rearrange("p (t e) -> p t e", e=NE)))
                flat = els[0:n, a:b, :, :].rearrange("p t g e -> p t (g e)")
                for c in range(2):
                    step(V.tensor_tensor(flat, rank_e[0:n, a:b, :], oh[0:n, c, a:b, :], ALU.mult))
                    step(V.reduce_sum(rank[0:n, c, a:b], flat, AX.X))

            def slots(a, b):
                n = P if a < NT else B
                for c in range(2):
                    last = V.tensor_tensor(slot_is[0:n, c, a:b, :],
                                           spread(slot_no[0:n, :].rearrange("p (o n) -> p o n", o=1), [n, b - a, P]),
                                           spread(rank[0:n, c, a:b].rearrange("p (t o) -> p t o", o=1), [n, b - a, P]),
                                           ALU.is_equal)
                return last

            def read_tables():
                V.tensor_scalar(g_idx[:, :], bank[2][:, 0:NE], half_no[:, 0:1], None, ALU.add)
                V.tensor_scalar(s_idx[:, :], bank[2][:, NE:2 * NE], far_half[:, 0:1], None, ALU.add)
                return V.tensor_copy(tabs[:, :], bank[2][:, 2 * NE:3 * NE])

            dve.wait_ge(S["wr_loaded"], 64)
            step(V.memset(lg[:, :, :], 0.0))
            own_heads(0)
            spread_scale(4)
            spread_scale(5)
            for t in range(NT):
                if t:
                    own_heads((2, 4, 5)[t - 1])
                residual(t)
                if t == 0:
                    dve.wait_ge(S["exp_ready"], B)
                    step(V.reduce_sum(p_sum[:, :, :], scores[:, :, :, :].rearrange("p b i h -> p b h i"), AX.X))
                    V.tensor_tensor(p_sum[:, :, :], p_sum[:, :, :], p_new[:, :, :], ALU.add).then_inc(S["softmax_in"], 1)
                if t != 2:
                    own_heads((1, 3, None, 6)[t])
                logits(t)
            choose(0, NT, 0)
            own_heads(7)
            dve.wait_ge(S["samp_norm_psum"], 1)
            dve.wait_ge(S["ot2_done"], B)
            c3 = lambda lo: bank[2][:, lo:lo + C4 * B].rearrange("p (c b) -> p c b", c=C4)
            step(V.reciprocal(o_r[:, :, :], c3(64)))
            V.tensor_tensor(o_t[:, :, :], c3(0), o_r[:, :, :], ALU.mult).then_inc(S["samp_norm_dve"], 1)
            dve.wait_ge(S["samp_norm_act"], 2)
            step(V.reciprocal(o_r[:, :, :], o_r[:, :, :]))
            step(V.tensor_tensor(o_t[:, :, :], o_t[:, :, :], o_r[:, :, :], ALU.mult))
            V.tensor_tensor(mix_a[:, :, T:T + B], o_t[:, :, :],
                            spread(vecs[:, 0:C4].rearrange("p (c o) -> p c o", o=1), [P, C4, B]), ALU.mult)\
                .then_inc(S["samp_norm_dve"], 1)
            ranks(0, NT, 1)
            slots(0, NT).then_inc(S["vals_ready"], 1)
            residual(NT)
            logits(NT)
            choose(NT, NT + 1, 1)
            ranks(NT, NT + 1, 2)
            slots(NT, NT + 1).then_inc(S["vals_ready"], 1)
            dve.wait_ge(S["rank_done"], 3)
            step(V.reduce_max(cnt_max[:, 0:1], bank[1][:, 0:NE], AX.X))
            V.tensor_copy(max_count[0:1, 0:1], cnt_max[0:1, 0:1]).then_inc(S["count_ready"], 1)
            dve.wait_ge(S["tabs_done"], 1)
            read_tables().then_inc(S["tabs_ready"], 1)
            V.memset(spare[:, :], 0.0).then_inc(S["y_ready"], 2)

            def hidden(xs):
                return V.tensor_tensor(hid[xs][:, :], sig[xs][:, :], bank[2 + xs][SLOTS:2 * SLOTS, 0:DE], ALU.mult)

            def hidden_out(xs):
                return V.tensor_copy(hid_t[xs][:, :, :], bank[2 + xs][:, 256:256 + 2 * SLOTS].rearrange("p (k n) -> p k n", k=2))

            def weighted(s, xs, e):
                return V.tensor_scalar(y_e[s][:, :], bank[4 + xs][:, :], tabs[:, bass.ds(e, 1)], None, ALU.mult)

            def last_scale(j):
                dve.wait_ge(S["g_loaded"], 48)
                dve.wait_ge(S["expand_done"], j + 11)
                lo = slice((j % 2) * SECS, (j % 2 + 1) * SECS)
                V.scalar_tensor_tensor(scf_s[0:B, lo], bank[6][0:B, :], 1.0, gf_b[0:B, lo], ALU.add, ALU.mult)
                V.scalar_tensor_tensor(scf_p[:, lo], bank[7][:, :], 1.0, gf_b[:, lo], ALU.add, ALU.mult)\
                    .then_inc(S["mod_scaled"], 1)

            def four_experts(g):
                for s in range(4):
                    xs, e = s % 2, 4 * g + s
                    dve.wait_ge(S["sig_ready"], e + 1)
                    hidden(xs).then_inc(S["hid_ready"], 1)
                    dve.wait_ge(S["hidt_done"], e + 1)
                    hidden_out(xs).then_inc(S["hidt_ready"], 1)
                    dve.wait_ge(S["y_done"], e + 1)
                    if not (isinstance(g, int) and g == 0):
                        dve.wait_ge(y_stored[s], g * 16)
                    weighted(s, xs, e).then_inc(S["y_ready"], 1)
                    if isinstance(g, int) and g > 0 and s < 2:
                        last_scale(s + 4)

            four_experts(0)
            with dve.Fori(1, NE // 4 - 1) as g:
                four_experts(g)
            four_experts(NE // 4 - 1)
            count = dve.value_load(max_count[0:1, 0:1], min_val=0, max_val=2 * (T + B))
            with dve.If(count > cap):
                with dve.Fori(1, PASSES) as p:
                    dve.wait_ge(y_stored[0], (p - 1) * NE * 16 + STORED)
                    for i in (1, 2, 3):
                        dve.wait_ge(y_stored[i], STORED)
                    V.tensor_scalar(slot_no[:, :], slot_no[:, :], float(SLOTS), None, ALU.add).then_inc(S["ov_slots"], 1)
                    dve.wait_ge(S["ov_slots"], p)
                    slots(0, NT)
                    slots(NT, NT + 1).then_inc(S["vals_ready"], 1)
                    dve.wait_ge(S["tabs_done"], p + 1)
                    read_tables().then_inc(S["tabs_ready"], 1)
                    dve.wait_ge(S["tabs_done"], 2)
                    dve.wait_ge(S["tabs_ready"], p + 1)
                    with dve.Fori(0, NE) as e:
                        n = p * NE + e
                        dve.wait_ge(S["sig_ready"], n + 1)
                        hidden(0).then_inc(S["hid_ready"], 1)
                        dve.wait_ge(S["hidt_done"], n + 1)
                        hidden_out(0).then_inc(S["hidt_ready"], 1)
                        dve.wait_ge(S["y_done"], n + 1)
                        dve.wait_ge(y_stored[0], (n - NE) * 16 + STORED)
                        weighted(0, 0, e).then_inc(S["y_ready"], 1)

            dve.wait_ge(S["mod_spread"], 8)
            dve.wait_ge(S["mod_scaled"], 4)
            last_tiles = (0, 1, 2, 3, NT)

            def last_residual(i):
                t = last_tiles[i]
                n = P if t < NT else B
                ga = ga2_p if t < NT else ga2_s
                y = y_g[i][0:n, 0, :]
                dve.wait_ge(yg_loaded[i], 16)
                step(V.tensor_tensor(y, y, y_g[i][0:n, 1, :], ALU.add))
                step(V.tensor_tensor(y, y, ga[0:n, :], ALU.mult))
                V.tensor_tensor(x_r[0:n, t, :], x_r[0:n, t, :], y, ALU.add).then_inc(S["x1_ready"], 1)

            def last_norm(i):
                t = last_tiles[i]
                n = P if t < NT else B
                sc = scf_p if t < NT else scf_s
                dve.wait_ge(S["norm_sqrt"], i + 6)
                step(V.reciprocal(rstd[0:n, t:t + 1], ssq[0:n, t:t + 1]))
                V.scalar_tensor_tensor(y_g[i][0:n, 1, :], x_r[0:n, t, :], rstd[0:n, t:t + 1], sc[0:n, :], ALU.mult, ALU.mult)\
                    .then_inc(S["h_row_ready"], 1)

            last_residual(0)
            for i in range(1, 5):
                last_residual(i)
                last_norm(i - 1)
            last_norm(4)
            dve.wait_ge(S["h_row_ready"], 10)
            V.tensor_tensor(y_g[4][0:B, 1, :], y_g[4][0:B, 1, :], shf_s[0:B, :], ALU.add).then_inc(S["h_row_ready"], 1)

        @block.gpsimd
        def _(pool):
            G = nc.gpsimd
            steps = [0]

            def step(ins):
                steps[0] += 1
                ins.then_inc(S["pool_step"], 1)
                pool.wait_ge(S["pool_step"], steps[0])

            G.iota(lane[:, :], [[0, 1]], base=0, channel_multiplier=1).then_inc(S["consts_ready"], 1)
            G.memset(ones[:, :], 1.0)
            G.memset(eps[:, :], EPS)
            G.memset(ssq[:, :], 1.0)
            G.memset(h_t[:, :, T + B:HP], 0.0).then_inc(S["consts_ready"], 1)
            step(G.memset(ident[:, :], 0.0))
            G.affine_select(out=ident[:, :], in_=ident[:, :], compare_op=ALU.not_equal, fill=1.0, base=0,
                            pattern=[[-1, P]], channel_multiplier=1).then_inc(S["consts_ready"], 1)
            G.memset(block64[:, :], 0.0)
            G.memset(sel[:, :, :], 0.0)
            G.memset(head_mask[:, :], 0.0)
            step(G.memset(causal[:, :], 0.0))
            G.memset(block64[0:64, 0:64], 1.0)
            step(G.memset(block64[64:128, 64:128], 1.0))
            G.affine_select(out=causal[:, :], in_=causal[:, :], compare_op=ALU.is_ge, fill=NEG, base=0,
                            pattern=[[-1, P]], channel_multiplier=1)
            G.affine_select(out=later[:, :], in_=ones[:, :], compare_op=ALU.is_gt, fill=0.0, base=0,
                            pattern=[[-1, P]], channel_multiplier=1)
            G.affine_select(out=earlier[:, :], in_=ones[:, :], compare_op=ALU.is_gt, fill=0.0, base=0,
                            pattern=[[1, P]], channel_multiplier=-1)
            for j in range(4):
                G.affine_select(out=sel[:, :, :], in_=sel[:, :, :], compare_op=ALU.not_equal, fill=1.0, base=-32 * j,
                                pattern=[[-1, B + 1], [0, P]], channel_multiplier=1)
                hm = head_mask[:, :].rearrange("p (h d) -> p h d", h=H)
                step(G.affine_select(out=hm, in_=hm, compare_op=ALU.not_equal, fill=1.0, base=-32 * j,
                                     pattern=[[-1, H], [0, HD]], channel_multiplier=1))
            G.affine_select(out=sel[:, :, :], in_=sel[:, :, :], compare_op=ALU.not_equal, fill=1.0, base=-31,
                            pattern=[[0, B + 1], [0, P]], channel_multiplier=1)
            step(G.memset(conv_in[:, :, 0:2], 0.0))
            pool.wait_ge(S["consts_ready"], 3)
            G.memset(small_one[:, :], 1.0).then_inc(S["consts_ready"], 1)

            pool.wait_ge(S["setup_ready"], 3)
            def cache_chunk(g):
                n = g % NKV
                if g >= RING:
                    pool.wait_ge(*((S["k_used"], 2 * (g - RING + 1)) if g - RING < NKV else (S["v_used"], g - RING - NKV + 1)))
                pool.indirect_dma_start(kv_flat[:, g % RING, :], None, k_rows if g < NKV else v_rows,
                                        bass.IndirectOffsetOnAxis(kv_index[:, n:n + 1], 0))\
                    .then_inc(kv_loaded[g % RING], 16)

            pool.wait_ge(S["unit_used"], 8)
            for n in range(RING):
                cache_chunk(n)
            f_view = decay[:, :, :, :].rearrange("p b i h -> p b (i h)")
            for b in range(B):
                pool.indirect_dma_start(f_view[:, b, :], None, f_rows, bass.IndirectOffsetOnAxis(f_index[:, b:b + 1], 0))\
                    .then_inc(S["f_loaded"], 16)

            def query(b):
                pool.dma_start(q_b[:, b % 2, :], q_rows_dram[b:b + 1, :].to_broadcast([P, HW]))\
                    .then_inc(qb_loaded[b % 2], 16)

            pool.wait_ge(S["h_row_ready"], 5)
            pool.wait_ge(S["q_stored"], 16)
            query(0)
            for n in range(RING, NKV):
                if n % NCH == 0:
                    if n >= 2 * NCH:
                        pool.wait_ge(S["k_used"], 2 * (n - NCH))
                    query(n // NCH)
                cache_chunk(n)
                if 8 <= n < 13:
                    if n == 8:
                        pool.wait_ge(S["f_loaded"], 16 * B)
                    d = 1 << (n - 8)
                    if n > 8:
                        pool.wait_ge(S["decay_sum"], n - 8)
                    G.tensor_tensor(decay[:, :, 0:PPP - d, :], decay[:, :, 0:PPP - d, :], decay[:, :, d:PPP, :], ALU.add)\
                        .then_inc(S["decay_sum"], 1)
                if n == NEW_AT + RING - 1:
                    pool.wait_ge(S["select_in"], 1)
                    G.affine_select(out=news[0:B, :, :], in_=news[0:B, :, :], compare_op=ALU.is_equal, fill=NEG, base=0,
                                    pattern=[[-1, B], [0, H]], channel_multiplier=1).then_inc(S["select_done"], 1)
                if n == DIAG_AT + RING - 1:
                    pool.wait_ge(S["select_in"], 2)
                    G.affine_select(out=lf_diag[:, :, :], in_=lf_diag[:, :, :], compare_op=ALU.is_equal, fill=0.0, base=0,
                                    pattern=[[-1, B], [0, H]], channel_multiplier=1).then_inc(S["select_done"], 1)
            pool.wait_ge(S["tail_evac"], 1)
            wide_tail = tail[:, :, :].rearrange("p b (o h) -> p b o h", o=1)
            step(G.tensor_tensor(decay[:, :, 0:PPP - 1, :], decay[:, :, 1:PPP, :],
                                 wide_tail.to_broadcast([P, B, PPP - 1, H]), ALU.add))
            G.tensor_copy(decay[:, :, PPP - 1, :], tail[:, :, :]).then_inc(S["select_done"], 1)
            for g in range(NKV, NKV + RING):
                cache_chunk(g)
            pool.wait_ge(S["softmax_in"], 1)
            G.partition_all_reduce(top_all[:, :, :].rearrange("p b h -> p (b h)"), top[:, :, :].rearrange("p b h -> p (b h)"),
                                   P, RED.max).then_inc(S["top_ready"], 1)
            for g in range(NKV + RING, NKV + CONSTS_AT):
                cache_chunk(g)
            pool.wait_ge(S["expand_done"], 10)
            G.iota(slot_no[:, :], [[0, 2], [1, SLOTS]], base=0, channel_multiplier=0, allow_small_or_imprecise_dtypes=True)
            G.iota(tok2[:, :], [[2 * P, 5]], base=0, channel_multiplier=2, allow_small_or_imprecise_dtypes=True)
            G.iota(desc[:, :], [[-1, EPG]], base=EPG, channel_multiplier=0, allow_small_or_imprecise_dtypes=True)
            step(G.memset(mark[:, :], 0.0))
            G.memset(half_no[0:SLOTS, :], 0.0)
            step(G.memset(half_no[SLOTS:P, :], 1.0))
            G.memset(far_half[0:SLOTS, :], FAR)
            G.memset(far_half[SLOTS:P, :], FAR + 1.0).then_inc(S["consts_ready"], 1)
            for g in range(NKV + CONSTS_AT, 2 * NKV):
                cache_chunk(g)
            pool.wait_ge(S["consts_ready"], 5)

            def gather(s, col):
                return pool.indirect_dma_start(x_e[s][:, :], None, h2_dram, bass.IndirectOffsetOnAxis(col, 0))

            def scatter(s, col):
                return pool.indirect_dma_start(y_dram, bass.IndirectOffsetOnAxis(col, 0), y_e[s][:, :], None,
                                               bounds_check=4 * (T + B) - 1, oob_is_err=False)

            def columns(e):
                G.tensor_copy(e_cols[:, 0:1], g_idx[:, bass.ds(e, 1)])
                return G.tensor_copy(e_cols[:, 1:2], s_idx[:, bass.ds(e, 1)])

            def hold(steps_done):
                pool.wait_ge(S["ov_held"], steps_done)
                G.tensor_tensor(mark[:, :], mark[:, :], mark[:, :], ALU.add).then_inc(S["ov_held"], 1)

            pool.wait_ge(S["tabs_ready"], 1)
            pool.wait_ge(h2_out[0], 48)
            pool.wait_ge(h2_out[1], 32)
            for e in range(NE + 4):
                if e < NE:
                    if e >= 4:
                        pool.wait_ge(S["xe_done"], e - 3)
                    gather(e % 4, g_idx[:, e:e + 1]).then_inc(xe_loaded[e % 4], 16)
                if e >= 4:
                    pool.wait_ge(S["y_ready"], e - 4 + 3)
                    scatter(e % 4, s_idx[:, e - 4:e - 3]).then_inc(y_stored[e % 4], 16)
            count = pool.value_load(max_count[0:1, 0:1], min_val=0, max_val=2 * (T + B))
            with pool.If(count > cap):
                pool.sem_inc(S["ov_held"], 1)
                with pool.Fori(1, PASSES) as p:
                    with pool.Fori(0, NE) as e:
                        n = p * NE + e
                        pool.wait_ge(S["tabs_ready"], p + 1)
                        pool.wait_ge(y_stored[0], (n - NE) * 16 + STORED)
                        columns(e).then_inc(S["ov_held"], 1)
                        hold(3 * (n - NE) + 2)
                        gather(0, e_cols[:, 0:1]).then_inc(xe_loaded[0], 16)
                        pool.wait_ge(S["y_ready"], n + 3)
                        hold(3 * (n - NE) + 3)
                        scatter(0, e_cols[:, 1:2]).then_inc(y_stored[0], 16)
                pool.wait_ge(y_stored[0], (PASSES - 1) * NE * 16 + STORED)
            for i in range(4):
                pool.wait_ge(y_stored[i], STORED)
            pool.sem_inc(S["y_all"], 1)

            for t in range(NT):
                pool.wait_ge(S["h_row_ready"], t + 6)
                G.tensor_tensor(y_g[t][:, 1, :], y_g[t][:, 1, :], shf_p[:, :], ALU.add).then_inc(S["fin_ready"], 1)

        @block.sync
        def _(sp):
            def unit(u):
                if u >= 3:
                    f = u - 3
                    if f < 8:
                        sp.wait_ge(S["unit_used"], f + 1)
                    elif f < 20:
                        s, half = divmod(f - 8, 2)
                        if half == 0:
                            sp.wait_ge(S["unit_used"], 8 + s + 1)
                        else:
                            sp.wait_ge(S["acc_done"], 4 * (s + 1))
                    else:
                        c, half = divmod(f - 20, 2)
                        if half == 0:
                            sp.wait_ge(S["unit_used"], 14 + c + 1)
                        else:
                            sp.wait_ge(S["ada_done"], 4 + c + 1)
                half = u % 2
                if u < 8:
                    v, lo = chunk_sec[u // 2]
                elif u < 20:
                    v, lo = w_in_v, sec_col[(u - 8) // 2]
                else:
                    v, lo = chunk_sec[4 + (u - 20) // 2]
                sp.dma_start(w_unit[:, u % 3], v[:, 4 * half:4 * half + 4, lo:lo + SECS]).then_inc(unit_loaded[u % 3], 16)

            row = lambda a: a.rearrange("(o n) -> o n", o=1)
            sp.dma_start(c_row[0:B, :], c_sample).then_inc(S["c_loaded"], 16)
            sp.dma_start(c_row[B:B + 1, :], c_prompt).then_inc(S["c_loaded"], 16)
            sp.dma_start(pt_int[:, :], page_table).then_inc(S["pt_loaded"], 16)
            sp.dma_start(b_row_a[:, :], b_ada[0:1, 0:4 * SECS]).then_inc(S["ba_loaded"], 16)
            unit(0)
            unit(1)
            unit(2)
            unit(3)
            unit(4)
            unit(5)
            sp.dma_start(x_a[0:B, NT, :], x_sample.rearrange("b t d -> (b t) d")).then_inc(S["x_loaded"], 16)
            sp.dma_start(x_a[:, 0:NT, :], x_prompt.rearrange("b (t p) d -> (b p) t d", p=P)).then_inc(S["x_loaded"], 16)
            sp.dma_start(g1_b[:, :], g_norm1.to_broadcast([P, D])).then_inc(S["g_loaded"], 16)
            sp.dma_start(vec_rows[0:4, :], g_attn_out.rearrange("l (c a) d -> (l c) (a d)", a=2)).then_inc(S["vec_loaded"], 16)
            sp.dma_start(vec_rows[4:8, :], g_conv_out.rearrange("l (c a) d -> (l c) (a d)", a=2)).then_inc(S["vec_loaded"], 16)
            sp.dma_start(vec_rows[8:20, :], conv_w.rearrange("l j (c p) -> (l j c) p", p=P)).then_inc(S["vec_loaded"], 16)
            sp.dma_start(b_f[:, :], b_forget.rearrange("l h -> h l")).then_inc(S["vec_loaded"], 16)
            sp.dma_start(conv_sample[0, :, 0, :], state_conv[0, :, 1, :]).then_inc(S["outs"], 16)
            for u in range(6, 8):
                unit(u)
            for u in range(8, 20):
                unit(u)
                if u == 11:
                    sp.wait_ge(S["h_row_ready"], 5)
                    sp.dma_start(w_f[:, :, :], w_in_v[:, :, f_col:f_col + H]).then_inc(S["wf_loaded"], 16)
                    sp.dma_start(state_rows[:, :], state_conv.rearrange("l b j c -> (l b j) c")).then_inc(S["wf_loaded"], 16)
            for u in range(20, 44):
                unit(u)
            sp.wait_ge(S["part_ready"], 12)
            sp.dma_start(part[31:32, 0:8, :], b_ada[0:1, 4 * SECS:].rearrange("o (n c) -> o n c", c=SECS))\
                .then_inc(b_loaded[0], 16)
            sp.wait_ge(S["part_ready"], 16)
            sp.dma_start(part[31:32, 8:12, :], row(b_ada_final).rearrange("o (n c) -> o n c", c=SECS))\
                .then_inc(b_loaded[1], 16)
            sp.wait_ge(S["side_turned"], 3)
            sp.wait_ge(S["acc_dve"], 8)
            sp.wait_ge(S["samp_g"], 2)
            sp.dma_start(g_b[:, :], g_norm2.to_broadcast([P, D])).then_inc(S["g_loaded"], 16)
            sp.wait_ge(S["ada_done"], 16)
            for lo, n, src in ((0, NG, w_router_group), (NG, NE, w_router_expert)):
                sp.dma_start(w_r[:, :, lo:lo + n], src.rearrange("l (p k) n -> (l p) k n", k=KD)).then_inc(S["wr_loaded"], 16)
            for lo, n, src in ((0, NG, b_router_group), (NG, NE, b_router_expert)):
                sp.dma_start(b_r[:, lo:lo + n], src.to_broadcast([P, n])).then_inc(S["wr_loaded"], 16)
            sp.wait_ge(S["k_used"], 2 * NKV)
            sp.dma_start(x_r[:, 0:3, :], x_prompt.rearrange("b (t p) d -> (b p) t d", p=P)[:, 0:3, :]).then_inc(S["x_loaded"], 16)
            sp.dma_start(wo[:, 6:KD, :], w_out_v[:, 6:KD, :]).then_inc(S["wo_conv_loaded"], 16)
            sp.wait_ge(S["s_done"], NT * H)
            sp.dma_start(wo[:, 0:C4, :], w_out_v[:, 0:C4, :]).then_inc(S["wo_attn_loaded"], 16)
            sp.wait_ge(S["pv_done"], NT * H)
            sp.dma_start(wo[:, C4:6, :], w_out_v[:, C4:6, :]).then_inc(S["wo_conv_loaded"], 16)
            sp.dma_start(x_r[0:B, NT, :], x_sample.rearrange("b t d -> (b t) d")).then_inc(S["x_loaded"], 16)
            sp.dma_start(x_r[:, 3, :], x_prompt.rearrange("b (t p) d -> (b p) t d", p=P)[:, 3, :]).then_inc(S["x_loaded"], 16)

            sp.wait_ge(S["expand_done"], 10)
            sp.dma_start(gf_b[:, :], row(g_final).to_broadcast([P, D])).then_inc(S["g_loaded"], 16)

            wg = w_expert_gate.rearrange("l e (a p c) f -> (l e) p a (c f)", a=2, c=4)
            wu = w_expert_up.rearrange("l e (a p c) f -> (l e) p a (c f)", a=2, c=4)
            wd = w_expert_down.rearrange("l e (p k) n -> (l e) p (k n)", k=2)

            def gate_up(e, s):
                for o, src in ((0, wg), (2048, wu)):
                    sp.dma_start(exp_w[s][:, o:o + 2048].rearrange("p (a n) -> p a n", a=2), pick(src, e))\
                        .then_inc(gate_loaded[s], 16)

            def down(e, s):
                sp.dma_start(exp_w[s][:, 4096:6144], pick(wd, e)).then_inc(down_loaded[s], 16)

            def pick(src, e):
                if isinstance(e, int):
                    return src[e]
                v = src[bass.ds(e, 1)]
                return v.rearrange("o p a n -> (o p) a n") if len(v.shape) == 4 else v.rearrange("o p n -> (o p) n")

            free = ((S["v_used"], NKV), (S["wo_part_done"], 2), (S["lg_done"], 5), (S["h2_ready"], 5))
            for s in range(4):
                sp.wait_ge(*free[s])
                if s == 3:
                    sp.wait_ge(xe_loaded[0], 16)
                gate_up(s, s)
                down(s, s)
            with sp.Fori(1, NE // 4) as g:
                for s in range(4):
                    e = 4 * g + s
                    sp.wait_ge(S["gu_done"], e - 3)
                    gate_up(e, s)
                    sp.wait_ge(S["y_done"], e - 3)
                    down(e, s)
            sp.wait_ge(S["count_ready"], 1)
            count = sp.value_load(max_count[0:1, 0:1], min_val=0, max_val=2 * (T + B))
            with sp.If(count > cap):
                with sp.Fori(1, PASSES) as p:
                    with sp.Fori(0, NE) as e:
                        sp.wait_ge(S["y_done"], p * NE + e)
                        gate_up(e, 0)
                        down(e, 0)

            sp.wait_ge(S["y_all"], 1)
            sp.wait_ge(S["y_done"], NE)
            tok_rows = lambda lo, n: y_dram[4 * lo:4 * (lo + n), :].rearrange("(p a) d -> p (a d)", a=4)
            for i, t in enumerate((0, 1, 2, 3, NT)):
                n = P if t < NT else B
                sp.dma_start(y_g[i][0:n, :, :].rearrange("p a d -> p (a d)"), tok_rows(t * P, n)).then_inc(yg_loaded[i], 16)
            for i, t in enumerate((0, 1, 2, 3, NT)):
                n = P if t < NT else B
                dst = y_prompt[0, t * P:(t + 1) * P, :] if t < NT else y_sample.rearrange("b t d -> (b t) d")
                if t < NT:
                    sp.wait_ge(S["fin_ready"], i + 1)
                else:
                    sp.wait_ge(S["h_row_ready"], 11)
                sp.dma_start(dst, y_g[i][0:n, 1, :]).then_inc(y_out[i % 2], 16)
            sp.wait_ge(y_out[0], 48)
            sp.wait_ge(y_out[1], 32)
            sp.wait_ge(S["outs"], 16 * 8)
            sp.wait_ge(S["krow_out"], 64)


_INS = ["x_prompt", "x_sample", "c_prompt", "c_sample", "cache_k", "cache_v", "cache_logf", "state_conv",
        "page_table", "w_ada", "b_ada", "g_norm1", "w_in", "b_forget", "conv_w", "g_attn_out", "g_conv_out",
        "w_out", "g_norm2", "w_router_group", "b_router_group", "w_router_expert", "b_router_expert",
        "w_expert_gate", "w_expert_up", "w_expert_down", "w_ada_final", "b_ada_final", "g_final"]
_OUTS = [(1, T, D), (B, 1, D), (1, 1, T, H, HD), (1, 1, T, H, HD), (1, 1, T, H), (1, 1, 2, HW),
         (1, B, 1, H, HD), (1, B, 1, H, HD), (1, B, 1, H), (1, B, 2, HW)]


def kernel(**inputs):
    import numpy as _np
    import concourse.bacc as _bacc
    from concourse import mybir as _mybir
    from concourse.bass_utils import run_bass_kernel_spmd as _run

    nc = _bacc.Bacc("TRN2", target_bir_lowering=False, num_devices=1)
    arrays, args = {}, []
    for name in _INS:
        a = _np.ascontiguousarray(inputs[name])
        arrays[f"in_{name}_dram"] = a
        args.append(nc.dram_tensor(f"in_{name}_dram", a.shape, _mybir.dt.from_np(a.dtype), kind="ExternalInput").ap())
    for i, shape in enumerate(_OUTS):
        args.append(nc.dram_tensor(f"out_{i}_dram", shape, F32, kind="ExternalOutput").ap())
    build(nc, *args)
    r = _run(nc, [arrays], core_ids=[0])
    return tuple(r.results[0][f"out_{i}_dram"] for i in range(len(_OUTS)))
```
